# Optimizing a Trainium2 kernel written in Bass

```python
import jax, jax.numpy as jnp
from jax import lax
import numpy as np

D_MODEL = 1024
BATCH = 1
SEQ = 512
DEPTH = 2
DEC_BATCH = 8
DEC_SEQ = 4
PAST_LEN = 256
PAGE_SIZE = 128

HEAD_DIM = 64
ROPE_THETA = 10000.0
A_HEADS = 8
A_KV_HEADS = 2
IDX_HEADS = 4
IDX_DIM = 64
A_TOPK_MAX = 256
A_WIDTH = A_HEADS * HEAD_DIM
B_WIDTH = D_MODEL // 2
CONV_W = 3
C_HEADS = 16
C_KV_HEADS = 4
C_WIDTH = C_HEADS * HEAD_DIM
CMP_BLOCK = 32
CMP_STRIDE = 16
SLC_BLOCK = 64
SLC_TOPN = 16
WINDOW = 512
D_FF = ((8 * D_MODEL + 3 * 256 - 1) // (3 * 256)) * 256
LN_EPS = 1e-5
ALPHA = (2 * DEPTH) ** 0.25
BETA = (8 * DEPTH) ** -0.25
Q_BLOCK = 128
N_AB = (DEPTH + 1) // 2
N_C = DEPTH // 2

AB_SIZES = (A_WIDTH, A_KV_HEADS * HEAD_DIM, A_KV_HEADS * HEAD_DIM, IDX_HEADS * IDX_DIM, IDX_DIM, IDX_HEADS,
            B_WIDTH, B_WIDTH, B_WIDTH)
AB_IN = sum(AB_SIZES)
AB_SPLITS = tuple(int(s) for s in np.cumsum(AB_SIZES)[:-1])
C_SIZES = (C_WIDTH,) + (C_KV_HEADS * HEAD_DIM,) * 6 + (3 * C_HEADS,)
C_IN = sum(C_SIZES)
C_SPLITS = tuple(int(s) for s in np.cumsum(C_SIZES)[:-1])

kernel_name = "hybrid_dsa_conv_nsa_deepnorm_step"

F32 = jnp.float32

def rope(x, pos):
    half = x.shape[-1] // 2
    inv = ROPE_THETA ** (-jnp.arange(half, dtype=F32) / half)
    ang = pos.astype(F32)[:, None] * inv[None, :]
    cos = jnp.cos(ang)[None, :, None, :]
    sin = jnp.sin(ang)[None, :, None, :]
    xf = x.astype(F32)
    x1, x2 = xf[..., :half], xf[..., half:]
    return jnp.concatenate([x1 * cos - x2 * sin, x2 * cos + x1 * sin], -1).astype(x.dtype)

def layernorm(x, g, b):
    xf = x.astype(F32)
    mu = jnp.mean(xf, -1, keepdims=True)
    var = jnp.mean(jnp.square(xf - mu), -1, keepdims=True)
    return ((xf - mu) * lax.rsqrt(var + LN_EPS) * g + b).astype(x.dtype)

def masked_softmax(s, mask):
    s = jnp.where(mask, s.astype(F32), -jnp.inf)
    m = jnp.max(s, -1, keepdims=True)
    m = jnp.where(jnp.isfinite(m), m, 0.0)
    p = jnp.exp(s - m)
    den = jnp.sum(p, -1, keepdims=True)
    return p / jnp.where(den > 0, den, 1.0)

def to_blocks(a, blk):
    return a.reshape(a.shape[0], a.shape[1] // blk, blk, *a.shape[2:])

def map_blocks(fn, args):
    nb = args[0].shape[1]
    if nb == 1:
        return fn(*[a[:, 0] for a in args])
    out = lax.map(lambda xs: fn(*xs), tuple(jnp.moveaxis(a, 1, 0) for a in args))
    out = jnp.moveaxis(out, 0, 1)
    return out.reshape(out.shape[0], -1, *out.shape[3:])

def gather_pages(pool, layer, page_table):
    g = pool[layer, page_table]
    return g.reshape(g.shape[0], g.shape[1] * g.shape[2], *g.shape[3:])

def dsa_block(q, iq, iw, pos, k_all, v_all, ik_all, topk):
    bsz, tb = q.shape[:2]
    L = k_all.shape[1]
    causal = jnp.arange(L)[None, None, :] <= pos[:, :, None]
    logits = jnp.einsum('bthd,bsd->bths', iq.astype(F32), ik_all.astype(F32)) * IDX_DIM ** -0.5
    score = jnp.einsum('bths,bth->bts', jax.nn.relu(logits), iw.astype(F32))
    score = jnp.where(causal, score, -jnp.inf)
    top_val, top_idx = lax.top_k(score, topk)
    take = jax.vmap(lambda kk, ii: kk[ii])
    k_sel = take(k_all, top_idx).astype(F32)
    v_sel = take(v_all, top_idx).astype(F32)
    qg = q.reshape(bsz, tb, A_KV_HEADS, A_HEADS // A_KV_HEADS, HEAD_DIM).astype(F32)
    s = jnp.einsum('btghd,btkgd->btghk', qg, k_sel) * HEAD_DIM ** -0.5
    p = masked_softmax(s, (top_val > -jnp.inf)[:, :, None, None, :])
    o = jnp.einsum('btghk,btkgd->btghd', p, v_sel)
    return o.reshape(bsz, tb, A_WIDTH).astype(q.dtype)

def ab_mixer(x, start, past, w_in, conv_w, w_out):
    bsz, T, _ = x.shape
    pos = start + jnp.arange(T)
    q, k, v, iq, ik, iw, gate_b, gate_c, h = jnp.split(x @ w_in, AB_SPLITS, axis=-1)
    q = rope(q.reshape(bsz, T, A_HEADS, HEAD_DIM), pos)
    k = rope(k.reshape(bsz, T, A_KV_HEADS, HEAD_DIM), pos)
    v = v.reshape(bsz, T, A_KV_HEADS, HEAD_DIM)
    iq = rope(iq.reshape(bsz, T, IDX_HEADS, IDX_DIM), pos)
    ik = rope(ik.reshape(bsz, T, 1, IDX_DIM), pos)[:, :, 0]
    iw = iw * IDX_HEADS ** -0.5
    u = gate_c * h
    if past is None:
        k_all, v_all, ik_all = k, v, ik
        prev = jnp.zeros((bsz, CONV_W - 1, B_WIDTH), u.dtype)
    else:
        k_past, v_past, ik_past, prev = past
        k_all = jnp.concatenate([k_past, k], 1)
        v_all = jnp.concatenate([v_past, v], 1)
        ik_all = jnp.concatenate([ik_past, ik], 1)
    topk = min(A_TOPK_MAX, k_all.shape[1] // 4)
    blk = min(Q_BLOCK, T)
    a_out = map_blocks(lambda qb, iqb, iwb, pb: dsa_block(qb, iqb, iwb, pb, k_all, v_all, ik_all, topk),
                       (to_blocks(q, blk), to_blocks(iq, blk), to_blocks(iw, blk), to_blocks(pos[None], blk)))
    full = jnp.concatenate([prev, u], 1)
    conv = full[:, 0:T] * conv_w[0]
    for j in range(1, CONV_W):
        conv = conv + full[:, j:j + T] * conv_w[j]
    b_out = gate_b * conv
    y = jnp.concatenate([a_out, b_out], -1) @ w_out
    return y, (k, v, ik, full[:, T:])

def compress(k_all, pe, w1, w2):
    L = k_all.shape[1]
    n_cmp = (L - CMP_BLOCK) // CMP_STRIDE + 1
    idx = jnp.arange(n_cmp)[:, None] * CMP_STRIDE + jnp.arange(CMP_BLOCK)[None, :]
    blocks = k_all[:, idx] + pe[None, None, :, None, :]
    hid = jax.nn.gelu(jnp.einsum('bnjgd,jde->bnge', blocks, w1))
    return jnp.einsum('bnge,ef->bngf', hid, w2)

def nsa_block(q, pos, gates, kw_span, vw_span, kw_pos, k_cmp, v_cmp, ks_blk, vs_blk, cmp_end, cmp_to_slc):
    bsz, tb = q.shape[:2]
    scale = HEAD_DIM ** -0.5
    qf = q.astype(F32)
    t = pos[:, :, None]
    s_c = jnp.einsum('btghd,bngd->btghn', qf, k_cmp.astype(F32)) * scale
    p_c = masked_softmax(s_c, (cmp_end[None, None, :] <= t)[:, :, None, None, :])
    o_c = jnp.einsum('btghn,bngd->btghd', p_c, v_cmp.astype(F32))
    imp = jnp.einsum('btghn,nm->btgm', p_c, cmp_to_slc)
    n_sblk = cmp_to_slc.shape[1]
    blk_id = jnp.arange(n_sblk)[None, None, :]
    cur = t // SLC_BLOCK
    forced = (blk_id == 0) | (blk_id == cur) | (blk_id == cur - 1)
    imp = jnp.where(forced[:, :, None, :], jnp.inf, imp)
    imp = jnp.where((blk_id * SLC_BLOCK <= t)[:, :, None, :], imp, -jnp.inf)
    n_sel = min(SLC_TOPN, n_sblk)
    sel_val, sel_idx = lax.top_k(imp, n_sel)
    take = jax.vmap(jax.vmap(lambda kk, ii: kk[ii]))
    idx_bg = jnp.moveaxis(sel_idx, 2, 1)
    k_s = take(ks_blk, idx_bg).reshape(bsz, C_KV_HEADS, tb, n_sel * SLC_BLOCK, HEAD_DIM).astype(F32)
    v_s = take(vs_blk, idx_bg).reshape(bsz, C_KV_HEADS, tb, n_sel * SLC_BLOCK, HEAD_DIM).astype(F32)
    key_pos = sel_idx[..., None] * SLC_BLOCK + jnp.arange(SLC_BLOCK)
    ok = (key_pos <= pos[:, :, None, None, None]) & (sel_val > -jnp.inf)[..., None]
    ok = ok.reshape(bsz, tb, C_KV_HEADS, n_sel * SLC_BLOCK)
    s_s = jnp.einsum('btghd,bgtkd->btghk', qf, k_s) * scale
    p_s = masked_softmax(s_s, ok[:, :, :, None, :])
    o_s = jnp.einsum('btghk,bgtkd->btghd', p_s, v_s)
    kp = kw_pos[:, None, :]
    ok_w = (kp >= 0) & (kp <= t) & (t - kp < WINDOW)
    s_w = jnp.einsum('btghd,bsgd->btghs', qf, kw_span.astype(F32)) * scale
    p_w = masked_softmax(s_w, ok_w[:, :, None, None, :])
    o_w = jnp.einsum('btghs,bsgd->btghd', p_w, vw_span.astype(F32))
    g = gates.reshape(bsz, tb, C_KV_HEADS, C_HEADS // C_KV_HEADS, 3)
    o = g[..., 0:1] * o_c + g[..., 1:2] * o_s + g[..., 2:3] * o_w
    return o.reshape(bsz, tb, C_WIDTH).astype(q.dtype)

def nsa_mixer(x, start, past, w_in, pe_k, w1_k, w2_k, pe_v, w1_v, w2_v, w_out):
    bsz, T, _ = x.shape
    pos = start + jnp.arange(T)
    q, kc, vc, ks, vs, kw, vw, g = jnp.split(x @ w_in, C_SPLITS, axis=-1)
    kvr = lambda a: a.reshape(bsz, T, C_KV_HEADS, HEAD_DIM)
    q = rope(q.reshape(bsz, T, C_HEADS, HEAD_DIM), pos)
    kc, ks, kw = rope(kvr(kc), pos), rope(kvr(ks), pos), rope(kvr(kw), pos)
    vc, vs, vw = kvr(vc), kvr(vs), kvr(vw)
    gates = jax.nn.sigmoid(g.astype(F32)).reshape(bsz, T, C_HEADS, 3)
    if past is None:
        kc_all, vc_all, ks_all, vs_all = kc, vc, ks, vs
        zpad = jnp.zeros((bsz, WINDOW, C_KV_HEADS, HEAD_DIM), kw.dtype)
        pre_k, pre_v = zpad, zpad
        keep = min(WINDOW, T)
        win_k, win_v = kw[:, T - keep:], vw[:, T - keep:]
    else:
        pkc, pvc, pks, pvs, buf_k, buf_v = past
        kc_all = jnp.concatenate([pkc, kc], 1)
        vc_all = jnp.concatenate([pvc, vc], 1)
        ks_all = jnp.concatenate([pks, ks], 1)
        vs_all = jnp.concatenate([pvs, vs], 1)
        nbuf = buf_k.shape[1]
        zpad = jnp.zeros((bsz, WINDOW - nbuf, C_KV_HEADS, HEAD_DIM), kw.dtype)
        pre_k = jnp.concatenate([zpad, buf_k], 1)
        pre_v = jnp.concatenate([zpad, buf_v], 1)
        win_k = jnp.concatenate([buf_k, kw], 1)[:, T:]
        win_v = jnp.concatenate([buf_v, vw], 1)[:, T:]
    L = kc_all.shape[1]
    k_cmp = compress(kc_all, pe_k, w1_k, w2_k)
    v_cmp = compress(vc_all, pe_v, w1_v, w2_v)
    n_cmp = k_cmp.shape[1]
    cmp_start = jnp.arange(n_cmp) * CMP_STRIDE
    cmp_end = cmp_start + CMP_BLOCK - 1
    n_sblk = -(-L // SLC_BLOCK)
    padn = n_sblk * SLC_BLOCK - L
    def sel_blocks(a):
        a = jnp.pad(a, ((0, 0), (0, padn), (0, 0), (0, 0)))
        return a.reshape(bsz, n_sblk, SLC_BLOCK, C_KV_HEADS, HEAD_DIM).transpose(0, 3, 1, 2, 4)
    ks_blk, vs_blk = sel_blocks(ks_all), sel_blocks(vs_all)
    lo = jnp.arange(n_sblk) * SLC_BLOCK
    cmp_to_slc = ((cmp_start[:, None] < lo[None, :] + SLC_BLOCK)
                  & (cmp_start[:, None] + CMP_BLOCK > lo[None, :])).astype(F32)
    blk = min(Q_BLOCK, T)
    nb = T // blk
    ext_k = jnp.concatenate([pre_k, kw], 1)
    ext_v = jnp.concatenate([pre_v, vw], 1)
    span_idx = jnp.arange(nb)[:, None] * blk + jnp.arange(WINDOW + blk)[None, :]
    kw_span, vw_span = ext_k[:, span_idx], ext_v[:, span_idx]
    span_pos = (start - WINDOW + span_idx)[None]
    qg = q.reshape(bsz, T, C_KV_HEADS, C_HEADS // C_KV_HEADS, HEAD_DIM)
    out = map_blocks(
        lambda qb, pb, gb, kwb, vwb, kpb: nsa_block(qb, pb, gb, kwb, vwb, kpb, k_cmp, v_cmp, ks_blk, vs_blk,
                                                   cmp_end, cmp_to_slc),
        (to_blocks(qg, blk), to_blocks(pos[None], blk), to_blocks(gates, blk), kw_span, vw_span, span_pos))
    y = out @ w_out
    return y, (kc, vc, ks, vs, win_k, win_v)

def swiglu(x, wg, wu, wd):
    return (jax.nn.silu(x @ wg) * (x @ wu)) @ wd

def setup_inputs(seed: int = 0) -> dict:
    key = jax.random.key(seed)
    ks = jax.random.split(key, 40)
    nrm = lambda k, shape, s=1.0: jax.random.normal(k, shape, F32) * s
    n_pages = PAST_LEN // PAGE_SIZE
    n_used = DEC_BATCH * n_pages
    n_pool = n_used + max(1, n_used // 4)
    win_buf = min(WINDOW, PAST_LEN)
    page_table = jax.random.permutation(ks[0], n_pool)[:n_used].reshape(DEC_BATCH, n_pages).astype(jnp.int32)
    a_kv = (N_AB, n_pool, PAGE_SIZE, A_KV_HEADS, HEAD_DIM)
    c_kv = (N_C, n_pool, PAGE_SIZE, C_KV_HEADS, HEAD_DIM)
    c_win = (N_C, DEC_BATCH, win_buf, C_KV_HEADS, HEAD_DIM)
    return {
        "x_prompt": nrm(ks[1], (BATCH, SEQ, D_MODEL)),
        "x_sample": nrm(ks[2], (DEC_BATCH, DEC_SEQ, D_MODEL)),
        "cache_a_k": nrm(ks[3], a_kv),
        "cache_a_v": nrm(ks[4], a_kv),
        "cache_a_ik": nrm(ks[5], (N_AB, n_pool, PAGE_SIZE, IDX_DIM)),
        "state_b_conv": nrm(ks[6], (N_AB, DEC_BATCH, CONV_W - 1, B_WIDTH)),
        "cache_c_cmp_k": nrm(ks[7], c_kv),
        "cache_c_cmp_v": nrm(ks[8], c_kv),
        "cache_c_slc_k": nrm(ks[9], c_kv),
        "cache_c_slc_v": nrm(ks[10], c_kv),
        "state_c_win_k": nrm(ks[11], c_win),
        "state_c_win_v": nrm(ks[12], c_win),
        "page_table": page_table,
        "ab_w_in": nrm(ks[13], (N_AB, D_MODEL, AB_IN), D_MODEL ** -0.5),
        "ab_conv_w": nrm(ks[14], (N_AB, CONV_W, B_WIDTH), CONV_W ** -0.5),
        "ab_w_out": nrm(ks[15], (N_AB, A_WIDTH + B_WIDTH, D_MODEL), BETA * (A_WIDTH + B_WIDTH) ** -0.5),
        "c_w_in": nrm(ks[16], (N_C, D_MODEL, C_IN), D_MODEL ** -0.5),
        "c_cmp_pe_k": nrm(ks[17], (N_C, CMP_BLOCK, HEAD_DIM), 0.02),
        "c_cmp_w1_k": nrm(ks[18], (N_C, CMP_BLOCK, HEAD_DIM, HEAD_DIM), (CMP_BLOCK * HEAD_DIM) ** -0.5),
        "c_cmp_w2_k": nrm(ks[19], (N_C, HEAD_DIM, HEAD_DIM), HEAD_DIM ** -0.5),
        "c_cmp_pe_v": nrm(ks[20], (N_C, CMP_BLOCK, HEAD_DIM), 0.02),
        "c_cmp_w1_v": nrm(ks[21], (N_C, CMP_BLOCK, HEAD_DIM, HEAD_DIM), (CMP_BLOCK * HEAD_DIM) ** -0.5),
        "c_cmp_w2_v": nrm(ks[22], (N_C, HEAD_DIM, HEAD_DIM), HEAD_DIM ** -0.5),
        "c_w_out": nrm(ks[23], (N_C, C_WIDTH, D_MODEL), BETA * C_WIDTH ** -0.5),
        "ffn_w_gate": nrm(ks[24], (DEPTH, D_MODEL, D_FF), D_MODEL ** -0.5),
        "ffn_w_up": nrm(ks[25], (DEPTH, D_MODEL, D_FF), BETA * D_MODEL ** -0.5),
        "ffn_w_down": nrm(ks[26], (DEPTH, D_FF, D_MODEL), BETA * D_FF ** -0.5),
        "ln1_g": 1.0 + nrm(ks[27], (DEPTH, D_MODEL), 0.01),
        "ln1_b": nrm(ks[28], (DEPTH, D_MODEL), 0.01),
        "ln2_g": 1.0 + nrm(ks[29], (DEPTH, D_MODEL), 0.01),
        "ln2_b": nrm(ks[30], (DEPTH, D_MODEL), 0.01),
    }

def reference(x_prompt, x_sample, cache_a_k, cache_a_v, cache_a_ik, state_b_conv, cache_c_cmp_k, cache_c_cmp_v,
              cache_c_slc_k, cache_c_slc_v, state_c_win_k, state_c_win_v, page_table, ab_w_in, ab_conv_w,
              ab_w_out, c_w_in, c_cmp_pe_k, c_cmp_w1_k, c_cmp_w2_k, c_cmp_pe_v, c_cmp_w1_v, c_cmp_w2_v, c_w_out,
              ffn_w_gate, ffn_w_up, ffn_w_down, ln1_g, ln1_b, ln2_g, ln2_b):
    xp, xs = x_prompt, x_sample
    ab_p, ab_s, c_p, c_s = [], [], [], []
    for layer in range(DEPTH):
        i = layer // 2
        if layer % 2 == 0:
            mp, st_p = ab_mixer(xp, 0, None, ab_w_in[i], ab_conv_w[i], ab_w_out[i])
            past = (gather_pages(cache_a_k, i, page_table), gather_pages(cache_a_v, i, page_table),
                    gather_pages(cache_a_ik, i, page_table), state_b_conv[i])
            ms, st_s = ab_mixer(xs, PAST_LEN, past, ab_w_in[i], ab_conv_w[i], ab_w_out[i])
            ab_p.append(st_p)
            ab_s.append(st_s)
        else:
            wts = (c_w_in[i], c_cmp_pe_k[i], c_cmp_w1_k[i], c_cmp_w2_k[i], c_cmp_pe_v[i], c_cmp_w1_v[i],
                   c_cmp_w2_v[i], c_w_out[i])
            mp, st_p = nsa_mixer(xp, 0, None, *wts)
            past = (gather_pages(cache_c_cmp_k, i, page_table), gather_pages(cache_c_cmp_v, i, page_table),
                    gather_pages(cache_c_slc_k, i, page_table), gather_pages(cache_c_slc_v, i, page_table),
                    state_c_win_k[i], state_c_win_v[i])
            ms, st_s = nsa_mixer(xs, PAST_LEN, past, *wts)
            c_p.append(st_p)
            c_s.append(st_s)
        xp = layernorm(ALPHA * xp + mp, ln1_g[layer], ln1_b[layer])
        xs = layernorm(ALPHA * xs + ms, ln1_g[layer], ln1_b[layer])
        xp = layernorm(ALPHA * xp + swiglu(xp, ffn_w_gate[layer], ffn_w_up[layer], ffn_w_down[layer]),
                       ln2_g[layer], ln2_b[layer])
        xs = layernorm(ALPHA * xs + swiglu(xs, ffn_w_gate[layer], ffn_w_up[layer], ffn_w_down[layer]),
                       ln2_g[layer], ln2_b[layer])
    stk = lambda lst, j: jnp.stack([e[j] for e in lst], 0)
    return (xp, xs,
            stk(ab_p, 0), stk(ab_p, 1), stk(ab_p, 2), stk(ab_p, 3),
            stk(c_p, 0), stk(c_p, 1), stk(c_p, 2), stk(c_p, 3), stk(c_p, 4), stk(c_p, 5),
            stk(ab_s, 0), stk(ab_s, 1), stk(ab_s, 2), stk(ab_s, 3),
            stk(c_s, 0), stk(c_s, 1), stk(c_s, 2), stk(c_s, 3), stk(c_s, 4), stk(c_s, 5))


_drawn_inputs = setup_inputs


def setup_inputs(seed=0):
    import zlib

    import numpy as np

    out = dict(_drawn_inputs(seed))
    spreads = {}
    factors = {'cache_c_cmp_k': 3.402,
     'cache_c_slc_k': 3.69,
     'cache_c_slc_v': 2.951,
     'c_cmp_pe_k': 22.572,
     'c_cmp_w1_k': 3.247,
     'c_cmp_w2_k': 3.172,
     'c_cmp_pe_v': 64.0,
     'ln1_g': 3.948,
     'ln1_b': 3.76,
     'ln2_g': 3.852,
     'ln2_b': 3.72}
    for name, (base, spread) in spreads.items():
        noise = np.random.default_rng([zlib.crc32(name.encode()), seed]).standard_normal(out[name].shape)
        drawn = base * np.exp(spread * noise) if base else spread * noise
        out[name] = __import__('jax').numpy.asarray(drawn.astype(out[name].dtype))
    for name, factor in factors.items():
        out[name] = (out[name] * factor).astype(out[name].dtype)
    return out
```

```python
from contextlib import ExitStack

import numpy as np

import concourse.bass as bass
from concourse import mybir

ALU = mybir.AluOpType
ACT = mybir.ActivationFunctionType
AX_X = mybir.AxisListType.X
F32 = mybir.dt.float32
F32R = mybir.dt.float32r
BF16 = mybir.dt.bfloat16
I32 = mybir.dt.int32

P = 128
D = 1024
KT = D // P
SEQ = 512
NB = SEQ // P
DEC_B = 8
DEC_T = 4
PAST = 256
PAGE = 128
NPAGE = PAST // PAGE
TS = DEC_B * DEC_T
T = SEQ + TS
HALF = T // 2
HD = 64
FF = 2816
FT = FF // P
KCH = FT // 2
TOPK_P = 128
TOPK_S = 65
CMP_W = 32
CMP_S = 16
NCMP_P = (SEQ - CMP_W) // CMP_S + 1
NCMP_S = (PAST + DEC_T - CMP_W) // CMP_S + 1
ALPHA = 4 ** 0.25
EPS = 1e-5
SCALE = HD ** -0.5
BIG = 1e30
TAKEN = -2.0 ** 127
NEW = PAST + TS

A_Q, A_K, A_V, A_IQ, A_IK, A_IW, A_GB, A_GC, A_H = 0, 512, 640, 768, 1024, 1088, 1092, 1604, 2116
C_Q, C_KC, C_VC, C_KS, C_VS, C_KW, C_VW, C_G = 0, 1024, 1280, 1536, 1792, 2048, 2304, 2560


def constants():
    pos = np.concatenate([np.arange(SEQ), PAST + np.tile(np.arange(DEC_T), DEC_B)]).astype(np.float32)
    inv = np.float32(10000.0) ** (-np.arange(HD // 2, dtype=np.float32) / np.float32(HD // 2))
    ang = inv[:, None].astype(np.float32) * pos[None, :]
    cos, sin = np.cos(ang), np.sin(ang)
    parts = {}
    parts["cos"] = np.tile(cos, (4, 1))
    parts["sin"] = np.concatenate([-sin, sin, -sin, sin], 0)
    parts["ident"] = np.eye(P)
    parts["mean"] = np.full((P, P), 1.0 / D)
    q, k = np.arange(P)[:, None], np.arange(P)[None, :]
    parts["causal"] = -1.0 * (k > q)
    row = np.arange(P)
    u, side, head, t = row // 32, row // 16 % 2, row // 4 % 4, row % 4
    new = np.zeros((P, 6, TS))
    pick = np.zeros((P, 6, P))
    for j in range(6):
        b = 4 * j + u if j < 2 else 2 * (j - 2) + u // 2
        tok = np.arange(TS)[None, :]
        new[:, j] = -1.0 * ~((tok // 4 == b[:, None]) & (tok % 4 <= t[:, None]))
        pick[b * 4 + t, j, row] = 1.0
    parts["new"] = new.reshape(P, -1)
    parts["pick"] = pick.reshape(P, -1)
    r = row % 32
    iside, itile = r // 8, r // 4 % 2
    parts["ihead"] = (r < 16)[:, None] * (np.arange(4)[None, :] == (2 * itile + iside)[:, None])
    parts["imix"] = ((r < 16)[:, None] & (u[:, None] == u[None, :]) & (t[:, None] == t[None, :]))
    parts["chead"] = np.arange(16)[None, :] == ((2 * (u % 2) + side) * 4 + head)[:, None]
    cend = np.arange(32)[None, None, :] * CMP_S + CMP_W - 1
    tt = (np.arange(NB)[None, :] * P + row[:, None])[:, :, None]
    parts["cmp"] = (-1.0 * (cend > tt)).reshape(P, -1)
    at, n = {}, 0
    for name, a in parts.items():
        at[name] = (n, n + a.shape[1])
        n += a.shape[1]
    return np.concatenate([a.astype(np.float32) for a in parts.values()], 1), at


CONST, AT = constants()


class Core:
    pass


def setup_memory(nc, ctx, dram):
    c = Core()
    c.nc, c.dram = nc, dram
    c.n_stage = 0
    sb = lambda n, s, d=F32: ctx.enter_context(nc.sbuf_tensor(n, s, d))
    c.sems = []
    c.const = sb("tables", [P, CONST.shape[1]])
    c.causal_bf = sb("causal_bf", [P, P], BF16)
    c.cmp_bf = sb("cmp_bf", [P, NB * 32], BF16)
    c.new_bf = sb("new_bf", [P, 6 * TS], BF16)
    c.ident_big = sb("ident_big", [P, P], BF16)
    c.xT = sb("xT", [P, KT, T])
    c.x_hi = sb("x_hi", [P, KT, T], F32R)
    c.x_lo = sb("x_lo", [P, KT, T], F32R)
    c.ln_gb = sb("ln_gb", [P, 4, 2, KT])
    c.w_raw = sb("w_raw", [P, 2, KCH, P])
    c.w_hi = sb("w_hi", [P, 2, KCH, P], F32R)
    c.w_lo = sb("w_lo", [P, 2, KCH, P], F32R)
    c.ps = ctx.enter_context(nc.psum_tensor("ps", [P, 8, 512], F32))
    c.k = lambda name: c.const[:, AT[name][0]:AT[name][1]]
    return c


def stage(c, name):
    c.n_stage += 1
    tag = f"{name}{c.n_stage}"


    def sem(signal):
        c.sems.append(c.nc.alloc_semaphore(name=f"{tag}_{signal}"))
        return c.sems[-1]
    return c.nc.Block(tag), sem


def reuse_semaphores(c):
    c.nc.clear_and_free_semaphores(c.sems)
    c.sems = []
    c.nc.all_engine_barrier()


def halves(ap):
    return ap.rearrange("p (h n) -> p h n", h=2)



def load_unit(c, sp, slot, pieces, raw_in):
    for place, src in pieces:
        sp.dma_start(place(c.w_raw[:, slot]), src).then_inc(raw_in, 16)


class Ahead:

    def __init__(self, c, sem, units):
        self.c, self.units = c, units
        self.raw_in = [sem("ahead_raw0"), sem("ahead_raw1")]
        self.hi_made = sem("ahead_hi")

    def load(self, sp):
        for slot, (pieces, _) in enumerate(self.units):
            load_unit(self.c, sp, slot, pieces, self.raw_in[slot])

    def split_hi(self, act, slot):
        pieces, kt = self.units[slot]
        act.wait_ge(self.raw_in[slot], 16 * len(pieces))
        split_hi(self.c, act, slot, kt).then_inc(self.hi_made, 1)

    def split_lo(self, dve, slot):
        dve.wait_ge(self.hi_made, slot + 1)
        split_lo(self.c, dve, slot, self.units[slot][1])


def pe_unit(c, pe, slot, kt, k0, x_hi, x_lo, bank, start, stop):
    for h in range(2):
        cols = slice(h * HALF, (h + 1) * HALF)
        out = c.ps[:, bank + h, 0:HALF]
        for k in range(kt):
            first, end = start and k == 0, stop and k == kt - 1
            pe.matmul(out, c.w_hi[:, slot, k, :], x_hi[:, k0 + k, cols], start=first, stop=False)
            pe.matmul(out, c.w_hi[:, slot, k, :], x_lo[:, k0 + k, cols], start=False, stop=False)
            last = pe.matmul(out, c.w_lo[:, slot, k, :], x_hi[:, k0 + k, cols], start=False, stop=end)
    return last


def split_hi(c, act, slot, kt):
    return act.activation(c.w_hi[:, slot, 0:kt, :], c.w_raw[:, slot, 0:kt, :], ACT.Copy)


def split_lo(c, dve, slot, kt):
    return dve.tensor_tensor(c.w_lo[:, slot, 0:kt, :], c.w_raw[:, slot, 0:kt, :],
                             c.w_hi[:, slot, 0:kt, :].bitcast(F32), ALU.subtract)


def w_rows(w, cols, k0=0, kt=KT):
    return w[k0 * P:(k0 + kt) * P, cols].rearrange("(k p) n -> p k n", p=P)


def slab_pieces(w, slab):
    return [(lambda r, d0=d0, n=n: r[:, 0:KT, d0:d0 + n], w_rows(w, slice(col, col + n))) for d0, col, n in slab]


def up_pieces(w, cols):
    return [(lambda r: r[:, 0:KT, :], w_rows(w, cols))]


def down_pieces(w, s, cols):
    return [(lambda r: r[:, :, :], w_rows(w, cols, s * KCH, KCH))]



def stage_load(c, ahead_units):
    nc = c.nc
    block, sem = stage(c, "load")
    with ExitStack() as tmp:
        x_nat = tmp.enter_context(nc.sbuf_tensor("x_nat", [P, NB + 1, D], F32))
        ln_nat = tmp.enter_context(nc.sbuf_tensor("ln_nat", [64, P], F32))
        const_in, x_in, ln_in = sem("const_in"), sem("x_in"), sem("ln_in")
        ahead = Ahead(c, sem, ahead_units)
        turned, evac, hi, masks, ln_t, ln_e = (sem(s) for s in
                                               ("turned", "evac", "hi", "masks", "ln_t", "ln_e"))
        with block as blk:
            @blk.sync
            def _(sp):
                sp.dma_start(c.const[:, :], c.dram["const"]).then_inc(const_in, 16)
                sp.dma_start(x_nat[:, 0:NB, :], c.dram["x_prompt"][0].rearrange("(b p) d -> p b d", p=P)).then_inc(x_in, 16)
                sp.dma_start(x_nat[0:TS, NB, :], c.dram["x_sample"].rearrange("b t d -> (b t) d")).then_inc(x_in, 16)
                for i, name in enumerate(("ln1_g", "ln1_b", "ln2_g", "ln2_b")):
                    sp.dma_start(ln_nat[16 * i:16 * i + 16, :],
                                 c.dram[name].rearrange("l (k p) -> (l k) p", p=P)).then_inc(ln_in, 16)
                ahead.load(sp)

            @blk.tensor
            def _(pe):
                pe.wait_ge(const_in, 16)
                pe.wait_ge(ln_in, 64)
                pe.transpose(c.ps[:, 7, 0:64], ln_nat[:, :], c.k("ident")[0:64, 0:64]).then_inc(ln_t, 1)
                pe.wait_ge(x_in, 32)
                for k in range(KT):
                    if k >= 3:
                        pe.wait_ge(evac, k - 2)
                    b0 = 2 * (k % 3)
                    for b in range(NB):
                        pe.transpose(c.ps[:, b0, b * P:(b + 1) * P], x_nat[:, b, k * P:(k + 1) * P], c.k("ident"))
                    pe.transpose(c.ps[:, b0 + 1, 0:TS], x_nat[0:TS, NB, k * P:(k + 1) * P],
                                 c.k("ident")[0:TS, 0:TS]).then_inc(turned, 1)

            @blk.vector
            def _(dve):
                dve.wait_ge(const_in, 16)
                dve.tensor_copy(c.causal_bf[:, :], c.k("causal"))
                dve.tensor_copy(c.cmp_bf[:, :], c.k("cmp"))
                dve.tensor_copy(c.new_bf[:, :], c.k("new"))
                dve.tensor_scalar(c.ident_big[:, :], c.k("ident"), BIG, None, ALU.mult).then_inc(masks, 1)
                dve.wait_ge(ln_t, 1)
                dve.tensor_copy(c.ln_gb[:, :, :, :].rearrange("p (w l) g k -> p w g l k", w=2),
                                c.ps[:, 7, 0:64].rearrange("p (w g l k) -> p w g l k", w=2, g=2, l=2)).then_inc(ln_e, 1)
                for k in range(KT):
                    dve.wait_ge(turned, k + 1)
                    b0 = 2 * (k % 3)
                    dve.tensor_copy(c.xT[:, k, 0:SEQ], c.ps[:, b0, :])
                    dve.tensor_copy(c.xT[:, k, SEQ:T], c.ps[:, b0 + 1, 0:TS]).then_inc(evac, 1)
                    dve.wait_ge(hi, k + 1)
                    dve.tensor_tensor(c.x_lo[:, k, :], c.xT[:, k, :], c.x_hi[:, k, :].bitcast(F32), ALU.subtract)
                    if k >= KT - 2:
                        ahead.split_lo(dve, k - KT + 2)

            @blk.scalar
            def _(act):
                for k in range(KT):
                    act.wait_ge(evac, k + 1)
                    act.activation(c.x_hi[:, k, :], c.xT[:, k, :], ACT.Copy).then_inc(hi, 1)
                    if k >= KT - 3 and k < KT - 1:
                        ahead.split_hi(act, k - KT + 3)


def stage_in_proj(c, name, w, rope_slabs, plain_slabs, projT):
    nc = c.nc
    block, sem = stage(c, name)
    slabs = rope_slabs + plain_slabs
    n_rope = len(rope_slabs)
    raw_loaded = [sem("raw0"), sem("raw1")]
    hi_made, lo_made, unit_used = sem("hi_made"), sem("lo_made"), sem("unit_used")
    swapped, cosed, sined, summed = sem("swapped"), sem("cosed"), sem("sined"), sem("summed")
    with ExitStack() as tmp:
        swap = tmp.enter_context(nc.sbuf_tensor(f"{name}_swap", [P, 2, T], F32))
        n_dma = [0, 0]
        loads = []
        for n, slab in enumerate(slabs):
            n_dma[n % 2] += len(slab) if n >= 2 else 0
            loads.append(16 * n_dma[n % 2])
        with block as blk:
            @blk.sync
            def _(sp):
                for n, slab in enumerate(slabs):
                    if n >= 2:
                        sp.wait_ge(hi_made, n - 1)
                        sp.wait_ge(lo_made, n - 1)
                        load_unit(c, sp, n % 2, slab_pieces(w, slab), raw_loaded[n % 2])

            def psum_of(n):
                return c.ps[:, 2 * (n % 4):2 * (n % 4) + 2, 0:HALF]

            @blk.scalar
            def _(act):
                def hi(n):
                    act.wait_ge(raw_loaded[n % 2], loads[n])
                    act.wait_ge(unit_used, n - 1)
                    split_hi(c, act, n % 2, KT).then_inc(hi_made, 1)

                act.sem_inc(hi_made, 2)
                for n in range(len(slabs)):
                    if 2 <= n + 1 < len(slabs):
                        hi(n + 1)
                    act.wait_ge(unit_used, n + 1)
                    if n < n_rope:
                        if n >= 2:
                            act.wait_ge(summed, n - 1)
                        for qd in range(4):
                            o = 32 * (qd ^ 1)
                            last = act.activation(halves(swap[32 * qd:32 * qd + 32, n % 2, :]),
                                                  psum_of(n)[o:o + 32], ACT.Copy)
                        last.then_inc(swapped, 1)
                    else:
                        act.activation(halves(projT[:, n, :]), psum_of(n), ACT.Copy).then_inc(swapped, 1)

            @blk.vector
            def _(dve):
                def lo(n):
                    dve.wait_ge(hi_made, n + 1)
                    split_lo(c, dve, n % 2, KT).then_inc(lo_made, 1)

                dve.sem_inc(lo_made, 2)
                for n in range(len(slabs)):
                    if 2 <= n + 1 < len(slabs):
                        lo(n + 1)
                    if n < n_rope:
                        dve.wait_ge(swapped, n + 1)
                        dve.tensor_tensor(halves(projT[:, n, :]), psum_of(n), halves(c.k("cos")), ALU.mult).then_inc(cosed, 1)
                        dve.tensor_tensor(swap[:, n % 2, :], swap[:, n % 2, :], c.k("sin"), ALU.mult).then_inc(sined, 1)
                        dve.wait_ge(cosed, n + 1)
                        dve.wait_ge(sined, n + 1)
                        dve.tensor_tensor(projT[:, n, :], projT[:, n, :], swap[:, n % 2, :], ALU.add).then_inc(summed, 1)

            @blk.tensor
            def _(pe):
                for n in range(len(slabs)):
                    pe.wait_ge(lo_made, n + 1)
                    if n >= 4:
                        pe.wait_ge(swapped, n - 3)
                        pe.wait_ge(cosed, min(n - 3, n_rope))
                    pe_unit(c, pe, n % 2, KT, 0, c.x_hi, c.x_lo, 2 * (n % 4), True, True).then_inc(unit_used, 1)


def stage_out_proj(c, name, w, row_of):
    block, sem = stage(c, name)
    raw_loaded = [sem("raw0"), sem("raw1")]
    hi_made, lo_made, unit_used, added = sem("hi_made"), sem("lo_made"), sem("unit_used"), sem("added")
    with block as blk:
        @blk.sync
        def _(sp):
            for n in range(2, KT):
                sp.wait_ge(hi_made, n - 1)
                sp.wait_ge(lo_made, n - 1)
                load_unit(c, sp, n % 2, row_of(w, slice(n * P, (n + 1) * P)), raw_loaded[n % 2])
        n_piece = len(row_of(w, slice(0, P)))

        @blk.scalar
        def _(act):
            act.sem_inc(hi_made, 2)
            for n in range(2, KT):
                act.wait_ge(raw_loaded[n % 2], 16 * n_piece * (n // 2))
                act.wait_ge(unit_used, n - 1)
                split_hi(c, act, n % 2, KT).then_inc(hi_made, 1)

        @blk.vector
        def _(dve):
            def lo(n):
                dve.wait_ge(hi_made, n + 1)
                split_lo(c, dve, n % 2, KT).then_inc(lo_made, 1)

            dve.sem_inc(lo_made, 2)
            for n in range(KT):
                if 2 <= n + 1 < KT:
                    lo(n + 1)
                dve.wait_ge(unit_used, n + 1)
                dve.scalar_tensor_tensor(halves(c.xT[:, n, :]), halves(c.xT[:, n, :]), ALPHA,
                                         c.ps[:, 2 * (n % 4):2 * (n % 4) + 2, 0:HALF], ALU.mult, ALU.add).then_inc(added, 1)

        @blk.tensor
        def _(pe):
            for n in range(KT):
                pe.wait_ge(lo_made, n + 1)
                if n >= 4:
                    pe.wait_ge(added, n - 3)
                pe_unit(c, pe, n % 2, KT, 0, c.x_hi, c.x_lo, 2 * (n % 4), True, True).then_inc(unit_used, 1)


def stage_norm(c, name, which, ahead_units=None):
    nc = c.nc
    block, sem = stage(c, name)
    mean_done, centred, squared, var_done, rooted, inverted = (sem(s) for s in
        ("mean_done", "centred", "squared", "var_done", "rooted", "inverted"))
    scaled, shifted, hi = sem("scaled"), sem("shifted"), sem("hi")
    ahead = Ahead(c, sem, ahead_units) if ahead_units else None
    with ExitStack() as tmp:
        sq = tmp.enter_context(nc.sbuf_tensor(f"{name}_sq", [P, 4, T], F32))
        std = tmp.enter_context(nc.sbuf_tensor(f"{name}_std", [P, T], F32))
        rstd = tmp.enter_context(nc.sbuf_tensor(f"{name}_rstd", [P, T], F32))
        eps = tmp.enter_context(nc.sbuf_tensor(f"{name}_eps", [P, 1], F32))
        eps_set = sem("eps_set")
        with block as blk:
            @blk.tensor
            def _(pe):
                for h in range(2):
                    for k in range(KT):
                        last_mm = pe.matmul(c.ps[:, h, 0:HALF], c.k("mean"), c.xT[:, k, h * HALF:(h + 1) * HALF],
                                            start=(k == 0), stop=(k == KT - 1))
                last_mm.then_inc(mean_done, 1)
                for k in range(KT):
                    pe.wait_ge(squared, k + 1)
                    for h in range(2):
                        last_mm = pe.matmul(c.ps[:, 2 + h, 0:HALF], c.k("mean"), sq[:, k % 4, h * HALF:(h + 1) * HALF],
                                            start=(k == 0), stop=(k == KT - 1))
                    last_mm.then_inc(var_done, 1)

            if ahead:
                @blk.sync
                def _(sp):
                    ahead.load(sp)

            @blk.vector
            def _(dve):
                dve.memset(eps[:, :], EPS).then_inc(eps_set, 1)
                if ahead:
                    ahead.split_lo(dve, 0)
                    ahead.split_lo(dve, 1)
                dve.wait_ge(mean_done, 1)
                for k in range(KT):
                    dve.tensor_tensor(halves(c.xT[:, k, :]), halves(c.xT[:, k, :]), c.ps[:, 0:2, 0:HALF],
                                      ALU.subtract).then_inc(centred, 1)
                dve.wait_ge(rooted, 1)
                dve.reciprocal(rstd[:, :], std[:, :]).then_inc(inverted, 1)
                dve.wait_ge(inverted, 1)

                def scale(k):
                    dve.wait_ge(squared, k + 1)
                    dve.tensor_tensor(c.xT[:, k, :], c.xT[:, k, :], rstd[:, :], ALU.mult).then_inc(scaled, 1)

                def lo(k):
                    dve.wait_ge(hi, k + 1)
                    dve.tensor_tensor(c.x_lo[:, k, :], c.xT[:, k, :], c.x_hi[:, k, :].bitcast(F32), ALU.subtract)

                dve.wait_ge(centred, KT)
                for k in range(KT):
                    scale(k)
                    if k >= 2:
                        lo(k - 2)
                lo(KT - 2)
                lo(KT - 1)

            @blk.scalar
            def _(act):
                if ahead:
                    ahead.split_hi(act, 0)
                    ahead.split_hi(act, 1)
                for k in range(KT):
                    act.wait_ge(centred, k + 1)
                    if k >= 4:
                        act.wait_ge(var_done, k - 3)
                    act.activation(sq[:, k % 4, :], c.xT[:, k, :], ACT.Square).then_inc(squared, 1)
                act.wait_ge(var_done, KT)
                act.wait_ge(eps_set, 1)
                act.activation(halves(std[:, :]), c.ps[:, 2:4, 0:HALF], ACT.Sqrt, bias=eps[:, :]).then_inc(rooted, 1)
                for k in range(KT):
                    act.wait_ge(scaled, k + 1)
                    act.activation(c.xT[:, k, :], c.xT[:, k, :], ACT.Identity, bias=c.ln_gb[:, which, 1, k:k + 1],
                                   scale=c.ln_gb[:, which, 0, k:k + 1]).then_inc(shifted, 1)
                    act.wait_ge(shifted, k + 1)
                    act.activation(c.x_hi[:, k, :], c.xT[:, k, :], ACT.Copy).then_inc(hi, 1)


def stage_ffn_up(c, layer, h_hi, h_lo):
    nc = c.nc
    wg, wu = c.dram["ffn_w_gate"][layer], c.dram["ffn_w_up"][layer]
    block, sem = stage(c, "up")
    g_raw, u_raw = sem("gate_raw_in"), sem("up_raw_in")
    g_hi, u_hi, g_lo, u_lo = sem("gate_hi"), sem("up_hi"), sem("gate_lo"), sem("up_lo")
    g_used, u_used = sem("gate_used"), sem("up_used")
    ahead = Ahead(c, sem, [(down_pieces(c.dram["ffn_w_down"][layer], s, slice(0, P)), KCH) for s in range(2)])
    silu, prod, h_top, h_rest = sem("silu"), sem("prod"), sem("h_top"), sem("h_rest")
    with ExitStack() as tmp:
        act_g = tmp.enter_context(nc.sbuf_tensor(f"silu{layer}", [P, T], F32))
        h_f = tmp.enter_context(nc.sbuf_tensor(f"h_f{layer}", [P, T], F32))
        with block as blk:
            @blk.sync
            def _(sp):
                with sp.Fori(1, FT) as f:
                    cols = bass.ds(f * P, P)
                    sp.wait_ge(g_lo, f)
                    load_unit(c, sp, 0, up_pieces(wg, cols), g_raw)
                    sp.wait_ge(u_lo, f)
                    load_unit(c, sp, 1, up_pieces(wu, cols), u_raw)
                sp.wait_ge(g_lo, FT)
                sp.wait_ge(u_lo, FT)
                ahead.load(sp)

            @blk.scalar
            def _(act):
                def gate_hi(f):
                    act.wait_ge(g_raw, 16 * f)
                    act.wait_ge(g_used, f)
                    split_hi(c, act, 0, KT).then_inc(g_hi, 1)

                def up_hi(f):
                    act.wait_ge(u_raw, 16 * f)
                    act.wait_ge(u_used, f)
                    split_hi(c, act, 1, KT).then_inc(u_hi, 1)

                def gate_act(f, first=False):
                    act.wait_ge(g_used, f + 1)
                    if not first:
                        act.wait_ge(prod, f)
                    act.activation(halves(act_g[:, :]), c.ps[:, 0:2, 0:HALF], ACT.Silu).then_inc(silu, 1)

                def top(f):
                    act.wait_ge(prod, f + 1)
                    act.activation(h_hi[:, bass.ds(f, 1), :], h_f[:, :].rearrange("p (a n) -> p a n", a=1),
                                   ACT.Copy).then_inc(h_top, 1)

                act.sem_inc(g_hi, 1)
                act.sem_inc(u_hi, 1)
                gate_hi(1)
                gate_act(0, True)
                up_hi(1)
                top(0)
                with act.Fori(1, FT - 1) as f:
                    gate_hi(f + 1)
                    gate_act(f)
                    up_hi(f + 1)
                    top(f)
                gate_act(FT - 1)
                ahead.split_hi(act, 0)
                top(FT - 1)
                ahead.split_hi(act, 1)

            @blk.vector
            def _(dve):
                def gate_lo(f):
                    dve.wait_ge(g_hi, f + 1)
                    split_lo(c, dve, 0, KT).then_inc(g_lo, 1)

                def up_lo(f):
                    dve.wait_ge(u_hi, f + 1)
                    split_lo(c, dve, 1, KT).then_inc(u_lo, 1)

                def mul(f, first=False):
                    if not first:
                        dve.wait_ge(h_rest, f)
                    dve.wait_ge(silu, f + 1)
                    dve.wait_ge(u_used, f + 1)
                    dve.tensor_tensor(halves(h_f[:, :]), halves(act_g[:, :]), c.ps[:, 2:4, 0:HALF], ALU.mult).then_inc(prod, 1)

                def low(f):
                    dve.wait_ge(h_top, f + 1)
                    at = bass.ds(f, 1)
                    dve.tensor_tensor(h_lo[:, at, :], h_f[:, :].rearrange("p (a n) -> p a n", a=1),
                                      h_hi[:, at, :].bitcast(F32), ALU.subtract).then_inc(h_rest, 1)

                dve.sem_inc(g_lo, 1)
                dve.sem_inc(u_lo, 1)

                def tile(f, first=False):
                    gate_lo(f + 1)
                    mul(f, first)
                    up_lo(f + 1)
                    low(f)

                tile(0, True)
                with dve.Fori(1, FT - 1) as f:
                    tile(f)
                ahead.split_lo(dve, 0)
                mul(FT - 1)
                low(FT - 1)
                ahead.split_lo(dve, 1)

            @blk.tensor
            def _(pe):
                def tile(f, first=False):
                    pe.wait_ge(g_lo, f + 1)
                    if not first:
                        pe.wait_ge(silu, f)
                    pe_unit(c, pe, 0, KT, 0, c.x_hi, c.x_lo, 0, True, True).then_inc(g_used, 1)
                    pe.wait_ge(u_lo, f + 1)
                    if not first:
                        pe.wait_ge(prod, f)
                    pe_unit(c, pe, 1, KT, 0, c.x_hi, c.x_lo, 2, True, True).then_inc(u_used, 1)

                tile(0, True)
                with pe.Fori(1, FT) as f:
                    tile(f)


def stage_ffn_down(c, layer, h_hi, h_lo):
    wd = c.dram["ffn_w_down"][layer]
    block, sem = stage(c, "down")
    raw = [sem("raw_a_in"), sem("raw_b_in")]
    hi = [sem("hi_a"), sem("hi_b")]
    lo = [sem("lo_a"), sem("lo_b")]
    used = [sem("used_a"), sem("used_b")]
    added = sem("added")
    with block as blk:
        @blk.sync
        def _(sp):
            with sp.Fori(1, KT) as n:
                for s in range(2):
                    sp.wait_ge(lo[s], n)
                    load_unit(c, sp, s, down_pieces(wd, s, bass.ds(n * P, P)), raw[s])

        @blk.scalar
        def _(act):
            act.sem_inc(hi[0], 1)
            act.sem_inc(hi[1], 1)
            with act.Fori(1, KT) as n:
                for s in range(2):
                    act.wait_ge(raw[s], 16 * n)
                    act.wait_ge(used[s], n)
                    split_hi(c, act, s, KCH).then_inc(hi[s], 1)

        @blk.vector
        def _(dve):
            def split(n, s):
                dve.wait_ge(hi[s], n + 1)
                split_lo(c, dve, s, KCH).then_inc(lo[s], 1)

            def add(n, bank):
                dve.wait_ge(used[1], n + 1)
                at = bass.ds(n, 1)
                x = c.xT[:, at, :].rearrange("p a (h n) -> p (a h) n", h=2)
                dve.scalar_tensor_tensor(x, x, ALPHA, c.ps[:, bank:bank + 2, 0:HALF], ALU.mult, ALU.add).then_inc(added, 1)

            dve.sem_inc(lo[0], 1)
            dve.sem_inc(lo[1], 1)

            def pair(n):
                for j in range(2):
                    split(n + j + 1, 0)
                    split(n + j + 1, 1)
                    add(n + j, 2 * j)

            with dve.Fori(0, KT - 2, 2) as n:
                pair(n)
            split(KT - 1, 0)
            split(KT - 1, 1)
            add(KT - 2, 0)
            add(KT - 1, 2)

        @blk.tensor
        def _(pe):
            def tile(n, bank, first=False):
                pe.wait_ge(lo[0], n + 1)
                if not first:
                    pe.wait_ge(added, n - 1)
                pe_unit(c, pe, 0, KCH, 0, h_hi, h_lo, bank, True, False).then_inc(used[0], 1)
                pe.wait_ge(lo[1], n + 1)
                pe_unit(c, pe, 1, KCH, KCH, h_hi, h_lo, bank, False, True).then_inc(used[1], 1)
            tile(0, 0, True)
            tile(1, 2, True)
            with pe.Fori(2, KT, 2) as n:
                tile(n, 0)
                tile(n + 1, 2)


def stage_store(c):
    nc = c.nc
    block, sem = stage(c, "store")
    turned, evac, out = sem("turned"), sem("evac"), sem("out")
    with ExitStack() as tmp:
        y = tmp.enter_context(nc.sbuf_tensor("y_nat", [P, NB + 1, D], F32))
        with block as blk:
            @blk.tensor
            def _(pe):
                for b in range(NB + 1):
                    n = P if b < NB else TS
                    if b >= 3:
                        pe.wait_ge(evac, b - 2)
                    for k in range(KT):
                        last = pe.transpose(c.ps[0:n, 2 * (b % 3) + k // 4, (k % 4) * P:(k % 4 + 1) * P],
                                            c.xT[:, k, b * P:b * P + n], c.k("ident"))
                    last.then_inc(turned, 1)

            @blk.vector
            def _(dve):
                for b in range(NB + 1):
                    n = P if b < NB else TS
                    dve.wait_ge(turned, b + 1)
                    dve.tensor_copy(y[0:n, b, :].rearrange("p (a m) -> p a m", a=2),
                                    c.ps[0:n, 2 * (b % 3):2 * (b % 3) + 2, :]).then_inc(evac, 1)

            @blk.sync
            def _(sp):
                for b in range(NB):
                    sp.wait_ge(evac, b + 1)
                    sp.dma_start(c.dram["y_prompt"][0, b * P:(b + 1) * P, :], y[:, b, :]).then_inc(out, 16)
                sp.wait_ge(evac, NB + 1)
                sp.dma_start(c.dram["y_sample"].rearrange("b t d -> (b t) d"), y[0:TS, NB, :]).then_inc(out, 16)
                sp.wait_ge(out, 16 * (NB + 1))



def stage_rows(c, name, projT, items):
    nc = c.nc
    block, sem = stage(c, name)
    turned, evac_p, evac_s, out = sem("turned"), sem("evac_p"), sem("evac_s"), [sem("out0"), sem("out1")]
    with ExitStack() as tmp:
        ring = tmp.enter_context(nc.sbuf_tensor(f"{name}_rows", [P, 2, NB + 1, P], F32))
        dst = [ring[:, n % 2] if keep is None else keep for n, (_, keep, _) in enumerate(items)]
        sent, before = [0, 0], []
        for n, (_, _, stores) in enumerate(items):
            before.append(sent[n % 2])
            sent[n % 2] += 32 * len(stores)
        with block as blk:
            @blk.tensor
            def _(pe):
                for n, (slab, _, _) in enumerate(items):
                    if n >= 3:
                        pe.wait_ge(evac_p, n - 2)
                        pe.wait_ge(evac_s, n - 2)
                    bank = 2 * (n % 3)
                    for b in range(NB):
                        pe.transpose(c.ps[:, bank, b * P:(b + 1) * P], projT[:, slab, b * P:(b + 1) * P], c.k("ident"))
                    pe.transpose(c.ps[0:TS, bank + 1, 0:P], projT[:, slab, SEQ:T], c.k("ident")).then_inc(turned, 1)

            @blk.vector
            def _(dve):
                for n in range(len(items)):
                    dve.wait_ge(turned, n + 1)
                    if n >= 2 and before[n]:
                        dve.wait_ge(out[n % 2], before[n])
                    dve.tensor_copy(dst[n][:, 0:NB, :], c.ps[:, 2 * (n % 3), :].rearrange("p (b n) -> p b n", b=NB)).then_inc(evac_p, 1)

            @blk.scalar
            def _(act):
                for n in range(len(items)):
                    act.wait_ge(turned, n + 1)
                    if n >= 2 and before[n]:
                        act.wait_ge(out[n % 2], before[n])
                    act.activation(dst[n][0:TS, NB, :], c.ps[0:TS, 2 * (n % 3) + 1, 0:P], ACT.Copy).then_inc(evac_s, 1)

            @blk.sync
            def _(sp):
                for n, (_, _, stores) in enumerate(items):
                    if stores:
                        sp.wait_ge(evac_p, n + 1)
                        sp.wait_ge(evac_s, n + 1)
                    for col, prompt, sample in stores:
                        w = prompt.shape[-1]
                        sp.dma_start(prompt.rearrange("(b p) n -> p b n", p=P), dst[n][:, 0:NB, col:col + w]).then_inc(out[n % 2], 16)
                        sp.dma_start(sample, dst[n][0:TS, NB, col:col + w]).then_inc(out[n % 2], 16)
                for s in range(2):
                    if sent[s]:
                        sp.wait_ge(out[s], sent[s])


def stage_pages(c, name, seqs, turn, copy):
    nc = c.nc
    block, sem = stage(c, name)
    table_in, rest_in, turned = (sem(s) for s in ("table_in", "rest_in", "turned"))
    evac = [sem("evac_dve"), sem("evac_act")]
    pages = [(b, g) for b in seqs for g in range(NPAGE)]
    n_turn = len(turn)
    steps = [(i, b, g, t) for i, (b, g) in enumerate(pages) for t in range(n_turn)]
    land = [sem(f"land{i}") for i in range(4)]
    with ExitStack() as tmp:
        table = tmp.enter_context(nc.sbuf_tensor(f"{name}_table", [1, DEC_B * NPAGE], I32))
        ring = tmp.enter_context(nc.sbuf_tensor(f"{name}_ring", [P, 4, 2 * P], F32))
        loads, count = [], [0] * 4
        for n, (_, _, _, t) in enumerate(steps):
            count[n % 4] += 16 * len(turn[t][1])
            loads.append(count[n % 4])
        with block as blk:
            @blk.sync
            def _(sp):
                sp.dma_start(table[:, :], c.dram["page_table"].rearrange("(a b) g -> a (b g)", a=1)).then_inc(table_in, 16)
                sp.wait_ge(table_in, 16)
                n = n_rest = 0
                n_pool = c.dram["cache_a_k"].shape[1]
                for i, (b, g) in enumerate(pages):
                    page = sp.value_load(table[0:1, b * NPAGE + g:b * NPAGE + g + 1], min_val=0, max_val=n_pool - 1)
                    for t, (src, places, _) in enumerate(turn):
                        if n >= 4:
                            sp.wait_ge(turned, n - 3)
                        for col, w in places:
                            sp.dma_start(ring[:, n % 4, col:col + w], src(page)).then_inc(land[n % 4], 16)
                        n += 1
                    for src, dst in copy:
                        sp.dma_start(dst(b, g), src(b, g, page)).then_inc(rest_in, 16)
                        n_rest += 1
                sp.wait_ge(rest_in, 16 * n_rest) if n_rest else None

            @blk.tensor
            def _(pe):
                for n, (i, b, g, t) in enumerate(steps):
                    if n >= 4:
                        pe.wait_ge(evac[n % 2], (n - 4) // 2 + 1)
                    pe.wait_ge(land[n % 4], loads[n])
                    wide = sum(w for _, w in turn[t][1])
                    for h in range(wide // P):
                        last = pe.transpose(c.ps[:, n % 4, h * P:(h + 1) * P], ring[:, n % 4, h * P:(h + 1) * P], c.k("ident"))
                    last.then_inc(turned, 1)

            def move(eng, n):
                i, b, g, t = steps[n]
                wide = sum(w for _, w in turn[t][1])
                src = c.ps[:, n % 4, 0:wide].rearrange("p (h n) -> p h n", n=P)
                dst = turn[t][2][:, :, seqs.index(b), g * PAGE:(g + 1) * PAGE]
                eng.wait_ge(turned, n + 1)
                return dst, src

            @blk.vector
            def _(dve):
                for n in range(0, len(steps), 2):
                    dst, src = move(dve, n)
                    dve.tensor_copy(dst, src).then_inc(evac[0], 1)

            @blk.scalar
            def _(act):
                for n in range(1, len(steps), 2):
                    dst, src = move(act, n)
                    act.activation(dst, src, ACT.Copy).then_inc(evac[1], 1)



class Tile:

    def __init__(self, scores, biases, n_keys, values, mover):
        self.scores, self.biases, self.n_keys, self.values, self.mover = scores, biases, n_keys, values, mover
        self.chunks = [(c0, min(P, n_keys - c0)) for c0 in range(0, n_keys, P)]


class Group:

    def __init__(self, tiles, n_seg, n_br, gate, leaves):
        self.tiles, self.n_seg, self.n_br, self.gate, self.leaves = tiles, n_seg, n_br, gate, leaves


TURN = 3
VALUE = 5
S_RING, P_RING, PT_RING = 3, 4, 3


def stage_attend(c, name, groups, ahead_units=None, beside=None):
    nc = c.nc
    block, sem = stage(c, name)
    scored, peaked, scaled, exped, turned, valued = (sem(s) for s in
        ("scored", "peaked", "scaled", "exped", "turned", "valued"))
    moved = {"act": sem("moved_act"), "dve": sem("moved_dve")}
    guarded, inverted, weighed, mixing, mixed, back, top, rest = (sem(s) for s in
        ("guarded", "inverted", "weighed", "mixing", "mixed", "back", "top", "rest"))
    ahead = Ahead(c, sem, ahead_units) if ahead_units else None
    tiles = [t for g in groups for t in g.tiles]
    group_of = [g for g, x in enumerate(groups) for _ in x.tiles]
    last_of = [max(j for j, x in enumerate(group_of) if x == g) for g in range(len(groups))]
    n_t, per = len(tiles), len(groups[0].tiles)
    n_steps = n_t + VALUE + 5
    S = lambda j: c.ps[:, j % S_RING, :]
    TB = lambda j: c.ps[:, 3 + j % 2, :]
    OB = lambda g: c.ps[:, 5 + g % 2, :]
    BACK = c.ps[:, 7, 0:P]

    def wait_moved(eng, j):
        who = tiles[j].mover
        eng.wait_ge(moved[who], sum(t.mover == who for t in tiles[:j + 1]))

    def groups_at(j, lag):
        return [g for g in range(len(groups)) if last_of[g] == j - lag]

    with ExitStack() as tmp:
        sb = lambda n, s: tmp.enter_context(nc.sbuf_tensor(f"{name}_{n}", s, F32))
        prob = sb("prob", [P, P_RING, max(t.n_keys for t in tiles)])
        probT = sb("probT", [P, PT_RING, max(len(t.chunks) for t in tiles), P])
        peak, shift, total, total1, inv, weight = (sb(n, [P, n_t]) for n in
            ("peak", "shift", "total", "total1", "inv", "weight"))
        rows = sb("rows", [P, 2, P])
        with block as blk:
            if ahead:
                @blk.sync
                def _(sp):
                    ahead.load(sp)

            @blk.tensor
            def _(pe):
                def scores(j):
                    t = tiles[j]
                    if j >= S_RING:
                        pe.wait_ge(exped, j - S_RING + 1)
                    mm = t.scores + [(0, P, c0, n, c.ident_big[:, :], rhs) for c0, n, rhs in t.biases]
                    opened = set()
                    for i, (p0, p1, c0, n, lhsT, rhs) in enumerate(mm):
                        last = pe.matmul(S(j)[p0:p1, c0:c0 + n], lhsT, rhs, start=p0 not in opened,
                                         stop=i == len(mm) - 1, skip_group_check=True)
                        opened |= set(range(p0, p1, 32))
                    last.then_inc(scored, 1)

                def turn(j):
                    pe.wait_ge(exped, j + 1)
                    if j >= 2:
                        wait_moved(pe, j - 2)
                    for i, (c0, n) in enumerate(tiles[j].chunks):
                        last = pe.transpose(TB(j)[0:n, i * P:(i + 1) * P], prob[:, j % P_RING, c0:c0 + n], c.k("ident"))
                    last.then_inc(turned, 1)

                def values(j):
                    t, g = tiles[j], group_of[j]
                    wait_moved(pe, j)
                    if g >= 2 and group_of[j - 1] != g:
                        pe.wait_ge(mixed, g - 1)
                    for p0, p1, c0, n, who, chunk, rhs, start, stop in t.values:
                        keys = t.chunks[chunk][1]
                        last = pe.matmul(OB(g)[p0:p1, c0:c0 + n], probT[0:keys, j % PT_RING, chunk, who], rhs,
                                         start=start, stop=stop, skip_group_check=True)
                    last.then_inc(valued, 1)

                for j in range(n_steps):
                    if j < n_t:
                        scores(j)
                    if 0 <= j - TURN < n_t:
                        turn(j - TURN)
                    if 0 <= j - VALUE < n_t:
                        values(j - VALUE)
                    for g in groups_at(j, VALUE + 2):
                        pe.wait_ge(mixed, g + 1)
                        if g:
                            pe.wait_ge(rest, g)
                        pe.transpose(BACK, rows[:, g % 2, :], c.k("ident")).then_inc(back, 1)

            def full_and_part(t):
                full = sum(n == P for _, n in t.chunks)
                return full, (t.chunks[full][1] if full < len(t.chunks) else 0)

            def move(eng, copy, j):
                t = tiles[j]
                eng.wait_ge(turned, j + 1)
                if j >= PT_RING:
                    eng.wait_ge(valued, j - PT_RING + 1)
                full, n = full_and_part(t)
                if full:
                    last = copy(probT[:, j % PT_RING, 0:full, :], TB(j)[:, 0:full * P].rearrange("p (k n) -> p k n", n=P))
                if n:
                    last = copy(probT[0:n, j % PT_RING, full, :], TB(j)[0:n, full * P:(full + 1) * P])
                last.then_inc(moved[t.mover], 1)

            @blk.vector
            def _(dve):
                if ahead:
                    ahead.split_lo(dve, 0)
                    ahead.split_lo(dve, 1)
                n_mix = 0
                for j in range(n_steps):
                    if j < n_t:
                        dve.wait_ge(scored, j + 1)
                        dve.tensor_reduce(peak[:, j:j + 1], S(j)[:, 0:tiles[j].n_keys], AX_X, ALU.max, negate=True).then_inc(peaked, 1)
                        dve.wait_ge(peaked, j + 1)
                        dve.tensor_scalar(shift[:, j:j + 1], peak[:, j:j + 1], BIG / 10, SCALE, ALU.min, ALU.mult).then_inc(scaled, 1)
                    if 0 <= j - TURN < n_t and tiles[j - TURN].mover == "dve":
                        move(dve, dve.tensor_copy, j - TURN)
                    for g in groups_at(j, 2):
                        dve.wait_ge(exped, last_of[g] + 1)
                        at = slice(g * per, (g + 1) * per)
                        dve.tensor_scalar(total1[:, at], total[:, at], 0.5, None, ALU.max).then_inc(guarded, 1)
                        dve.wait_ge(guarded, g + 1)
                        dve.reciprocal(inv[:, at], total1[:, at]).then_inc(inverted, 1)
                        if groups[g].gate is not None:
                            dve.wait_ge(inverted, g + 1)
                            view = lambda x: x[:, at].rearrange("p (s a) -> p s a", s=groups[g].n_seg)
                            dve.tensor_tensor(view(weight), view(inv), groups[g].gate, ALU.mult).then_inc(weighed, 1)
                    for g in groups_at(j, VALUE + 1):
                        x = groups[g]
                        w = inv if x.gate is None else weight
                        dve.wait_ge(inverted if x.gate is None else weighed, g + 1)
                        dve.wait_ge(valued, last_of[g] + 1)
                        if g >= 2:
                            dve.wait_ge(back, g - 1)
                        width = P // x.n_seg
                        for a in range(x.n_br):
                            if a:
                                dve.wait_ge(mixing, n_mix)
                            for s in range(x.n_seg):
                                o = OB(g)[:, (s * x.n_br + a) * width:(s * x.n_br + a + 1) * width]
                                r = rows[:, g % 2, s * width:(s + 1) * width]
                                f = w[:, g * per + s * x.n_br + a:g * per + s * x.n_br + a + 1]
                                if a == 0:
                                    last = dve.tensor_scalar(r, o, f, None, ALU.mult)
                                else:
                                    last = dve.scalar_tensor_tensor(r, o, f, r, ALU.mult, ALU.add)
                                if a < x.n_br - 1:
                                    last.then_inc(mixing, 1)
                                    n_mix += 1
                        last.then_inc(mixed, 1)
                    for g in groups_at(j, VALUE + 4):
                        dve.wait_ge(top, g + 1)
                        for place, part in groups[g].leaves:
                            last = dve.tensor_tensor(place(c.x_lo), part(BACK), place(c.x_hi).bitcast(F32), ALU.subtract)
                        last.then_inc(rest, 1)

            if beside:
                @blk.gpsimd
                def _(pool):
                    beside(pool)

            @blk.scalar
            def _(act):
                copy = lambda out, in_: act.activation(out, in_, ACT.Copy)
                if ahead:
                    ahead.split_hi(act, 0)
                    ahead.split_hi(act, 1)
                for j in range(n_steps):
                    if j < n_t:
                        act.wait_ge(scaled, j + 1)
                        if j >= P_RING:
                            act.wait_ge(turned, j - P_RING + 1)
                        n = tiles[j].n_keys
                        act.activation(prob[:, j % P_RING, 0:n], S(j)[:, 0:n], ACT.Exp, bias=shift[:, j:j + 1],
                                       scale=SCALE, accum_out=total[:, j:j + 1]).then_inc(exped, 1)
                    if 0 <= j - TURN < n_t and tiles[j - TURN].mover == "act":
                        move(act, copy, j - TURN)
                    for g in groups_at(j, VALUE + 3):
                        act.wait_ge(back, g + 1)
                        for place, part in groups[g].leaves:
                            last = copy(place(c.x_hi), part(BACK))
                        last.then_inc(top, 1)


class Stack:

    def __init__(self):
        self.hi, self.lo = [], []

    def queries(self, side, src, dst):
        own, other = rows_of(side), rows_of(1 - side)
        self.hi.append((dst[own], src))
        self.lo.append((dst[other], src, dst[own], len(self.hi)))

    def keys(self, side, src, hi, lo):
        own, other = rows_of(side), rows_of(1 - side)
        self.hi += [(hi[own], src), (hi[other], src)]
        self.lo += [(part, src, hi[own], len(self.hi)) for part in (lo[own], lo[other])]

    def fill_hi(self, copy, made, a, b):
        for dst, src in self.hi[a:b]:
            copy(dst, src).then_inc(made, 1)

    def fill_lo(self, eng, made, a, b, done=None):
        for dst, src, hi, n in self.lo[a:b]:
            eng.wait_ge(made, n)
            ins = eng.tensor_tensor(dst, src, hi.bitcast(F32), ALU.subtract)
            if done:
                ins.then_inc(done, 1)


def rows_of(side):
    return slice(side * HD, side * HD + HD)


def idle_slots(c):
    lines = [w[:, :, :, :].rearrange("p s k n -> p (s k n)") for w in (c.w_hi, c.w_lo)]
    return [line[:, e * SEQ:(e + 1) * SEQ] for line in lines for e in range(2 * KCH * P // SEQ)]


class Rows:

    def __init__(self, n, side, q, keys, bias, values, gate, group, mover, first, last):
        self.n, self.side, self.q, self.keys, self.bias, self.values = n, side, q, keys, bias, values
        self.gate, self.group, self.mover, self.first, self.last = gate, group, mover, first, last
        self.wide = n
        self.short = None
        self.n_chunk = n // P


class Short:

    def __init__(self, heads, bias, gate):
        self.heads, self.bias, self.gate, self.mover = heads, bias, gate, "act"
        self.wide, self.n_chunk = 8 * 32, 2


TURN_P = 3
VALUE_P = 5


def stage_attend_prompt(c, name, tiles, leaf, n_groups, late=None):
    nc = c.nc
    block, sem = stage(c, name)
    scored, peaked, scaled, exped, inverted, normed, turned, valued = (sem(s) for s in
        ("scored", "peaked", "scaled", "exped", "inverted", "normed", "turned", "valued"))
    moved = {"act": sem("moved_act"), "dve": sem("moved_dve")}
    top, rest, link, stacked, late_set = sem("top"), sem("rest"), sem("link"), sem("stacked"), sem("late_set")
    n_t, n_prob, n_probT = len(tiles), 5, 3
    shorts = [j for j, t in enumerate(tiles) if isinstance(t, Short)]
    group_end = [max(j for j, t in enumerate(tiles) if j not in shorts and t.group == g) for g in range(n_groups)]
    S = lambda j: c.ps[:, j % 4, :]
    TB = lambda j: c.ps[:, 4 + j % 2, :]
    OB = lambda g: c.ps[:, 6 + g % 2, 0:P]
    LAG = 2

    def wait_moved(eng, j):
        who = tiles[j].mover
        eng.wait_ge(moved[who], sum(t.mover == who for t in tiles[:j + 1]))

    def through(j):
        return sum(i not in shorts for i in range(j + 1))

    with ExitStack() as tmp:
        sb = lambda n, s: tmp.enter_context(nc.sbuf_tensor(f"{name}_{n}", s, F32))
        prob = sb("prob", [P, n_prob, SEQ])
        probT = sb("probT", [P, n_probT, NB, P])
        peak, shift, total, inv = (sb(n, [P, n_t]) for n in ("peak", "shift", "total", "inv"))
        if shorts:
            shortT = sb("shortT", [P, 2, 2, P])
            peak8, total8, inv8 = (sb(n, [P, 2, 8]) for n in ("peak8", "total8", "inv8"))
        by_head = lambda x: x.rearrange("p (h n) -> p h n", n=32)
        spread = lambda x: x.rearrange("p (h a) -> p h a", a=1).broadcast_to([P, 8, 32])
        with block as blk:
            @blk.tensor
            def _(pe):
                def scores(j):
                    t = tiles[j]
                    if j >= 4:
                        pe.wait_ge(scaled if j - 4 in shorts else exped, j - 3)
                    if late and j == n_t // 2:
                        pe.wait_ge(late_set, len(late.lo))
                    if j in shorts:
                        for h, (q, hi, lo) in enumerate(t.heads):
                            o = S(j)[:, 32 * h:32 * h + 32]
                            pe.matmul(o, q, hi, start=h == 0, stop=False, skip_group_check=True)
                            pe.matmul(o, q, lo, start=False, stop=False, skip_group_check=True)
                        last = pe.matmul(by_head(S(j)[:, 0:256]), c.ident_big[:, :], t.bias, start=False, stop=True,
                                         skip_group_check=True)
                    else:
                        n = max(t.n, 2 * P)
                        pe.matmul(S(j)[:, 0:n], t.q, t.keys[0][:, 0:n], start=True, stop=False, skip_group_check=True)
                        pe.matmul(S(j)[:, 0:n], t.q, t.keys[1][:, 0:n], start=False, stop=False, skip_group_check=True)
                        c0, w, rhs = t.bias
                        last = pe.matmul(S(j)[:, c0:c0 + w], c.ident_big[:, :], rhs, start=False, stop=True,
                                         skip_group_check=True)
                    last.then_inc(scored, 1)

                def turn(j):
                    pe.wait_ge(normed, j + 1)
                    if j >= 2:
                        wait_moved(pe, j - 2)
                    for i in range(tiles[j].n_chunk):
                        last = pe.transpose(TB(j)[:, i * P:(i + 1) * P], prob[:, j % n_prob, i * P:(i + 1) * P], c.k("ident"))
                    last.then_inc(turned, 1)

                def values(j):
                    wait_moved(pe, j)
                    if j in shorts:
                        return
                    t = tiles[j]
                    if t.group >= 2 and j and (j - 1 in shorts or tiles[j - 1].group != t.group):
                        pe.wait_ge(rest, t.group - 1)
                        pe.wait_ge(top, t.group - 1)
                    out = OB(t.group)[rows_of(t.side)]
                    products = [(lhsT, probT[:, j % n_probT, k, :]) for k, lhsT in t.values]
                    if t.short:
                        n, chunk, part, lhsT = t.short
                        products = [(lhsT, shortT[part, n % 2, chunk, :])] + products
                    for i, (lhsT, rhs) in enumerate(products):
                        last = pe.matmul(out, lhsT, rhs, start=t.first and i == 0,
                                         stop=t.last and i == len(products) - 1, skip_group_check=True)
                    last.then_inc(valued, 1)

                for j in range(n_t + VALUE_P):
                    if j < n_t:
                        scores(j)
                    if 0 <= j - TURN_P < n_t:
                        turn(j - TURN_P)
                    if j >= VALUE_P:
                        values(j - VALUE_P)

            def move(eng, copy, j):
                t = tiles[j]
                eng.wait_ge(turned, j + 1)
                if j in shorts:
                    n = shorts.index(j)
                    if n >= 2:
                        eng.wait_ge(valued, through(shorts[n - 1] - 1))
                    dst = shortT[:, n % 2]
                else:
                    if j >= n_probT and through(j - n_probT):
                        eng.wait_ge(valued, through(j - n_probT))
                    dst = probT[:, j % n_probT, 0:t.n_chunk, :]
                copy(dst, TB(j)[:, 0:t.n_chunk * P].rearrange("p (k n) -> p k n", n=P)).then_inc(moved[t.mover], 1)

            @blk.vector
            def _(dve):
                linked = Linked(dve, link)

                def peaks(j):
                    t = tiles[j]
                    dve.wait_ge(scored, j + 1)
                    if j in shorts:
                        n = shorts.index(j)
                        linked(dve.tensor_reduce(peak8[:, n % 2, :], by_head(S(j)[:, 0:256]), AX_X, ALU.max, negate=True))
                        linked(dve.tensor_scalar(peak8[:, n % 2, :], peak8[:, n % 2, :], BIG / 10, None, ALU.min))
                        if j >= n_prob:
                            dve.wait_ge(turned, j - n_prob + 1)
                        dve.tensor_tensor(by_head(prob[:, j % n_prob, 0:256]), by_head(S(j)[:, 0:256]),
                                          spread(peak8[:, n % 2, :]), ALU.add).then_inc(scaled, 1)
                    else:
                        dve.tensor_reduce(peak[:, j:j + 1], S(j)[:, 0:t.n], AX_X, ALU.max, negate=True).then_inc(peaked, 1)

                def shifts(j):
                    if j not in shorts:
                        dve.wait_ge(peaked, j + 1 - sum(i <= j for i in shorts))
                        dve.tensor_scalar(shift[:, j:j + 1], peak[:, j:j + 1], SCALE, None, ALU.mult).then_inc(scaled, 1)

                def invert(j):
                    dve.wait_ge(exped, j + 1)
                    if j in shorts:
                        n = shorts.index(j)
                        linked(dve.reduce_sum(total8[:, n % 2, :], by_head(prob[:, j % n_prob, 0:256]), AX_X))
                        linked(dve.tensor_scalar(total8[:, n % 2, :], total8[:, n % 2, :], 0.5, None, ALU.max))
                        linked(dve.reciprocal(inv8[:, n % 2, :], total8[:, n % 2, :]))
                        dve.tensor_tensor(inv8[:, n % 2, :].rearrange("p (s h) -> p s h", s=2),
                                          inv8[:, n % 2, :].rearrange("p (s h) -> p s h", s=2), tiles[j].gate, ALU.mult).then_inc(inverted, 1)
                    else:
                        dve.reciprocal(inv[:, j:j + 1], total[:, j:j + 1]).then_inc(inverted, 1)

                done = 0
                for j in range(n_t + VALUE_P + 2):
                    if j < n_t:
                        peaks(j)
                    if 0 <= j - TURN_P < n_t and tiles[j - TURN_P].mover == "dve":
                        move(dve, dve.tensor_copy, j - TURN_P)
                    if j < n_t:
                        shifts(j)
                    if late and j % 2 and LAG <= j // 2 < LAG + len(late.lo):
                        n = j // 2 - LAG
                        late.fill_lo(dve, stacked, n, n + 1, late_set)
                    if 0 <= j - 1 < n_t:
                        invert(j - 1)
                    while done < n_groups and group_end[done] <= j - VALUE_P - 1:
                        dve.wait_ge(top, done + 1)
                        place = leaf(done)
                        dve.tensor_tensor(place(c.x_lo), OB(done), place(c.x_hi).bitcast(F32), ALU.subtract).then_inc(rest, 1)
                        done += 1

            @blk.gpsimd
            def _(pool):
                for j, t in enumerate(tiles):
                    pool.wait_ge(inverted, j + 1)
                    w = prob[:, j % n_prob, 0:t.wide]
                    if j in shorts:
                        n = shorts.index(j)
                        pool.tensor_tensor(by_head(w), by_head(w), spread(inv8[:, n % 2, :]), ALU.mult).then_inc(normed, 1)
                    else:
                        pool.tensor_scalar(w, w, inv[:, j:j + 1], 1.0 if t.gate is None else t.gate, ALU.mult, ALU.mult).then_inc(normed, 1)

            @blk.scalar
            def _(act):
                copy = lambda out, in_: act.activation(out, in_, ACT.Copy)
                done = 0
                for j in range(n_t + VALUE_P + 2):
                    if j < n_t:
                        act.wait_ge(scaled, j + 1)
                        if j in shorts:
                            w = prob[:, j % n_prob, 0:256]
                            act.activation(w, w, ACT.Exp, scale=SCALE).then_inc(exped, 1)
                        else:
                            if j >= n_prob:
                                act.wait_ge(turned, j - n_prob + 1)
                            n = tiles[j].n
                            act.activation(prob[:, j % n_prob, 0:n], S(j)[:, 0:n], ACT.Exp, bias=shift[:, j:j + 1],
                                           scale=SCALE, accum_out=total[:, j:j + 1]).then_inc(exped, 1)
                    if 0 <= j - TURN_P < n_t and tiles[j - TURN_P].mover == "act":
                        move(act, copy, j - TURN_P)
                    if late and j % 2 and j // 2 < len(late.hi):
                        late.fill_hi(copy, stacked, j // 2, j // 2 + 1)
                    while done < n_groups and group_end[done] <= j - VALUE_P:
                        act.wait_ge(valued, through(group_end[done]))
                        copy(leaf(done)(c.x_hi), OB(done)).then_inc(top, 1)
                        done += 1


class Linked:

    def __init__(self, eng, link):
        self.eng, self.link, self.count = eng, link, 0

    def __call__(self, ins):
        self.count += 1
        ins.then_inc(self.link, 1)
        self.eng.wait_ge(self.link, self.count)


def prompt_tiles(sections, branches, short=None):
    tiles, n_groups, n_short, leaves = [], 0, 0, []
    for a in range(sections):
        for qb in range(NB):
            if short:
                tiles.append(short[0](a, qb))
            for i in range(4):
                pair = 4 * a + i
                for b, (q, keys, value, bias, gate, mover) in enumerate(branches):
                    for side in range(2):
                        t = Rows((qb + 1) * P, side, q(pair, side, qb), keys(a, side), bias(qb),
                                 [(k, value(a, side, k)) for k in range(qb + 1)], gate(pair, side, qb), n_groups,
                                 mover(side), b == 0, b == len(branches) - 1)
                        if short and b == 0:
                            t.short = (n_short, side, slice(32 * i, 32 * i + 32), short[1](a, side, i))
                        tiles.append(t)
                leaves.append(lambda x, pair=pair, qb=qb: x[:, pair, qb * P:(qb + 1) * P])
                n_groups += 1
            n_short += 1
    return tiles, lambda g: leaves[g], n_groups



def stage_index_prompt(c, projT, iw, sel, keep_rows, stacks):
    nc = c.nc
    block, sem = stage(c, "index")
    scored, relud, summed, link, iw_set = sem("scored"), sem("relud"), sem("summed"), sem("link"), sem("iw_set")
    with ExitStack() as tmp:
        relu = tmp.enter_context(nc.sbuf_tensor("ix_relu", [P, 2, SEQ], F32))
        score = tmp.enter_context(nc.sbuf_tensor("ix_score", [P, SEQ], F32))
        best = tmp.enter_context(nc.sbuf_tensor("ix_best", [P, 8], F32))
        jobs = [(qb, h) for qb in range(1, NB) for h in range(4)]
        stacked = sem("stacked")
        with block as blk:
            @blk.gpsimd
            def _(pool):
                stacks.fill_hi(pool.tensor_copy, stacked, 0, len(stacks.hi))
                stacks.fill_lo(pool, stacked, 0, len(stacks.lo))

            @blk.tensor
            def _(pe):
                for j, (qb, h) in enumerate(jobs):
                    if j >= 4:
                        pe.wait_ge(relud, j - 3)
                    rows = slice(h % 2 * HD, h % 2 * HD + HD)
                    n = (qb + 1) * P
                    pe.matmul(c.ps[:, j % 4, 0:n], projT[rows, 4 + h // 2, qb * P:(qb + 1) * P],
                              projT[rows, 7, 0:n], start=True, stop=True).then_inc(scored, 1)

            @blk.scalar
            def _(act):
                for j, (qb, h) in enumerate(jobs):
                    n = (qb + 1) * P
                    act.wait_ge(scored, j + 1)
                    if j >= 2:
                        act.wait_ge(summed, j - 1)
                    act.activation(relu[:, j % 2, 0:n], c.ps[:, j % 4, 0:n], ACT.Relu, scale=SCALE).then_inc(relud, 1)

            @blk.vector
            def _(dve):
                count = [0]

                def linked(ins):
                    count[0] += 1
                    ins.then_inc(link, 1)
                    dve.wait_ge(link, count[0])

                linked(dve.tensor_scalar(iw[:, 0:NB, :], keep_rows[:, 0:NB, :], 0.5, None, ALU.mult))
                linked(dve.tensor_scalar(iw[0:TS, NB, :], keep_rows[0:TS, NB, :], 0.5, None, ALU.mult))
                for j, (qb, h) in enumerate(jobs):
                    n = (qb + 1) * P
                    dve.wait_ge(relud, j + 1)
                    if h == 0:
                        dve.tensor_scalar(score[:, 0:n], relu[:, j % 2, 0:n], iw[:, qb, 0:1], None, ALU.mult).then_inc(summed, 1)
                    else:
                        dve.scalar_tensor_tensor(score[:, 0:n], relu[:, j % 2, 0:n], iw[:, qb, h:h + 1], score[:, 0:n],
                                                 ALU.mult, ALU.add).then_inc(summed, 1)
                    dve.wait_ge(summed, j + 1)
                    if h == 3:
                        own = score[:, qb * P:n]
                        linked(dve.scalar_tensor_tensor(own, c.k("causal"), BIG, own, ALU.mult, ALU.add))
                        for _ in range(TOPK_P // 8):
                            linked(dve.max(best[:, :], score[:, 0:n]))
                            linked(dve.match_replace(score[:, 0:n], best[:, :], score[:, 0:n], TAKEN))
                        linked(dve.tensor_scalar(sel[:, qb, 0:n], score[:, 0:n], TAKEN, 1.0, ALU.is_equal, ALU.subtract))


def stage_conv(c, projT):
    nc = c.nc
    block, sem = stage(c, "conv")
    loaded, turned, moved, gated, tail_t, tail_o, out = (sem(s) for s in
        ("loaded", "turned", "moved", "gated", "tail_t", "tail_o", "out"))
    link, top, prod = sem("link"), sem("top"), sem("prod")
    W = D // 2 // P
    with ExitStack() as tmp:
        sb = lambda n, s, d=F32: tmp.enter_context(nc.sbuf_tensor(n, s, d))
        state = sb("cv_state", [64, P])
        taps = sb("cv_taps", [12, P])
        tapsT = sb("cv_tapsT", [P, 3, W])
        u_p = sb("cv_u_p", [P, W, 2 + SEQ])
        u_s = sb("cv_u_s", [P, W, DEC_B, 2 + DEC_T])
        acc = sb("cv_acc", [P, W, T])
        tail = sb("cv_tail", [P, W, 18])
        tail_rows = sb("cv_tail_rows", [72, P])
        with block as blk:
            @blk.sync
            def _(sp):
                sp.dma_start(state[:, :], c.dram["state_b_conv"][0].rearrange("b j (k p) -> (b j k) p", p=P)).then_inc(loaded, 16)
                sp.dma_start(taps[:, :], c.dram["ab_conv_w"][0].rearrange("j (k p) -> (j k) p", p=P)).then_inc(loaded, 16)
                sp.wait_ge(tail_o, 1)
                for k in range(W):
                    sp.dma_start(c.dram["b_conv_s"][0].rearrange("b j d -> (b j) d")[:, k * P:(k + 1) * P],
                                 tail_rows[18 * k:18 * k + 16, :]).then_inc(out, 16)
                    sp.dma_start(c.dram["b_conv_p"][0, 0][:, k * P:(k + 1) * P], tail_rows[18 * k + 16:18 * k + 18, :]).then_inc(out, 16)
                sp.wait_ge(out, 16 * 2 * W)

            @blk.tensor
            def _(pe):
                pe.wait_ge(loaded, 32)
                pe.transpose(c.ps[:, 0, 0:64], state[:, :], c.k("ident")[0:64, 0:64])
                pe.transpose(c.ps[:, 1, 0:12], taps[:, :], c.k("ident")[0:12, 0:12]).then_inc(turned, 1)
                pe.wait_ge(tail_t, 1)
                pe.transpose(c.ps[0:72, 2, 0:P], tail[:, :, :].rearrange("p k n -> p (k n)"), c.k("ident")).then_inc(turned, 1)

            @blk.vector
            def _(dve):
                dve.wait_ge(turned, 1)
                dve.tensor_copy(u_s[:, :, :, 0:2].rearrange("p k b j -> p b j k"),
                                c.ps[:, 0, 0:64].rearrange("p (b j k) -> p b j k", b=DEC_B, j=2))
                dve.tensor_copy(tapsT[:, :, :], c.ps[:, 1, 0:12].rearrange("p (j k) -> p j k", k=W)).then_inc(moved, 1)
                count = [0]

                def linked(ins):
                    count[0] += 1
                    ins.then_inc(link, 1)
                    dve.wait_ge(link, count[0])

                dve.wait_ge(moved, 1)
                linked(dve.memset(u_p[:, :, 0:2], 0.0))
                for k in range(W):
                    linked(dve.tensor_tensor(u_p[:, k, 2:], projT[:, 14 + k, 0:SEQ], projT[:, 18 + k, 0:SEQ], ALU.mult))
                    linked(dve.tensor_tensor(u_s[:, k, :, 2:], projT[:, 14 + k, SEQ:T].rearrange("p (b t) -> p b t", b=DEC_B),
                                             projT[:, 18 + k, SEQ:T].rearrange("p (b t) -> p b t", b=DEC_B), ALU.mult))
                linked(dve.tensor_copy(tail[:, :, 0:16].rearrange("p k (b j) -> p k b j", j=2), u_s[:, :, :, 4:6]))
                dve.tensor_copy(tail[:, :, 16:18], u_p[:, :, SEQ:SEQ + 2]).then_inc(tail_t, 1)
                for k in range(W):
                    a_p = acc[:, k, 0:SEQ]
                    a_s = acc[:, k, SEQ:T].rearrange("p (b t) -> p b t", b=DEC_B)
                    for j in range(3):
                        w = tapsT[:, j, k:k + 1]
                        for a, u in ((a_p, u_p[:, k, j:j + SEQ]), (a_s, u_s[:, k, :, j:j + DEC_T])):
                            if j == 0:
                                linked(dve.tensor_scalar(a, u, w, None, ALU.mult))
                            else:
                                linked(dve.scalar_tensor_tensor(a, u, w, a, ALU.mult, ALU.add))
                    dve.tensor_tensor(acc[:, k, :], acc[:, k, :], projT[:, 10 + k, :], ALU.mult).then_inc(prod, 1)
                    dve.wait_ge(top, k + 1)
                    dve.tensor_tensor(c.x_lo[:, 4 + k, :], acc[:, k, :], c.x_hi[:, 4 + k, :].bitcast(F32), ALU.subtract)
                dve.wait_ge(turned, 2)
                dve.tensor_copy(tail_rows[:, :], c.ps[0:72, 2, 0:P]).then_inc(tail_o, 1)

            @blk.scalar
            def _(act):
                for k in range(W):
                    act.wait_ge(prod, k + 1)
                    act.activation(c.x_hi[:, 4 + k, :], acc[:, k, :], ACT.Copy).then_inc(top, 1)


def stage_index_sample(c, projT, iw_rows, ikT, sel_s, q_blk):
    nc = c.nc
    block, sem = stage(c, "index_s")
    q_set, scored, relud, mixed, picked, link = (sem(s) for s in ("q_set", "scored", "relud", "mixed", "picked", "link"))
    mix_set = sem("mix_set")
    with ExitStack() as tmp:
        sb = lambda n, s, d=F32: tmp.enter_context(nc.sbuf_tensor(n, s, d))
        iq = sb("is_iq", [P, DEC_B, 32])
        relu = sb("is_relu", [P, 2, NEW])
        mix = sb("is_mix", [P, 2, P])
        col = sb("is_col", [P, 2])
        hit = sb("is_hit", [P, 2, 4])
        score = sb("is_score", [P, NEW])
        best = sb("is_best", [P, 8])
        with block as blk:
            @blk.vector
            def _(dve):
                count = [0]

                def linked(ins):
                    count[0] += 1
                    ins.then_inc(link, 1)
                    dve.wait_ge(link, count[0])

                linked(dve.memset(iq[:, :, :], 0.0))
                linked(dve.memset(q_blk[:, :, :, :, :], 0.0))
                iq_v = iq[:, :, 0:16].rearrange("p b (s i t) -> p b s i t", s=2, i=2)
                for side in range(2):
                    rows = slice(side * HD, side * HD + HD)
                    for i in range(2):
                        linked(dve.tensor_copy(iq_v[rows, :, side, i, :], projT[rows, 4 + i, SEQ:T].rearrange("p (b t) -> p b t", t=DEC_T)))
                    for h in range(4):
                        linked(dve.tensor_copy(q_blk[rows, :, side, h, :], projT[rows, h, SEQ:T].rearrange("p (b t) -> p b t", t=DEC_T)))
                dve.wait_ge(picked, 1)
                for j in range(2):
                    linked(dve.tensor_tensor(hit[:, j, :], c.ps[:, 7, 4 * j:4 * j + 4], c.k("ihead"), ALU.mult))
                    linked(dve.reduce_sum(col[:, j:j + 1], hit[:, j, :], AX_X))
                    dve.tensor_scalar(mix[:, j, :], c.k("imix"), col[:, j:j + 1], None, ALU.mult).then_inc(mix_set, 1)
                dve.sem_inc(q_set, 1)
                for j in range(2):
                    dve.wait_ge(mixed, j + 1)
                    linked(dve.tensor_copy(score[:, :], c.ps[:, 2 + j, 0:NEW]))
                    own = score[:, PAST:NEW]
                    linked(dve.scalar_tensor_tensor(own, c.k("new")[:, j * TS:(j + 1) * TS], BIG, own, ALU.mult, ALU.add))
                    for r in range(TOPK_S // 8 + 1):
                        linked(dve.max(best[:, :], score[:, :]))
                        if r == TOPK_S // 8:
                            linked(dve.memset(best[:, TOPK_S % 8:8], TAKEN))
                        linked(dve.match_replace(score[:, :], best[:, :], score[:, :], TAKEN))
                    linked(dve.tensor_scalar(sel_s[:, j, :], score[:, :], TAKEN, 1.0, ALU.is_equal, ALU.subtract))

            @blk.tensor
            def _(pe):
                for j in range(2):
                    last = pe.matmul(c.ps[:, 7, 4 * j:4 * j + 4], c.k("pick")[0:TS, j * P:(j + 1) * P], iw_rows,
                                     start=(j == 0), stop=(j == 1), skip_group_check=True)
                last.then_inc(picked, 1)
                pe.wait_ge(mix_set, 2)
                for j in range(2):
                    for u in range(4):
                        b = 4 * j + u
                        pe.matmul(c.ps[32 * u:32 * u + 32, j, 0:PAST], iq[:, b, :], ikT[:, 0, b, :], start=True, stop=False, skip_group_check=True)
                        last = pe.matmul(c.ps[32 * u:32 * u + 32, j, PAST:NEW], iq[:, b, :], projT[:, 7, SEQ:T], start=False, stop=True, skip_group_check=True)
                    last.then_inc(scored, 1)
                for j in range(2):
                    pe.wait_ge(relud, j + 1)
                    pe.matmul(c.ps[:, 2 + j, 0:NEW], mix[:, j, :], relu[:, j, :], start=True, stop=True).then_inc(mixed, 1)

            @blk.scalar
            def _(act):
                for j in range(2):
                    act.wait_ge(scored, j + 1)
                    act.activation(relu[:, j, :], c.ps[:, j, 0:NEW], ACT.Relu, scale=SCALE).then_inc(relud, 1)


def sample_groups(n, units, branches, gate, leaves):
    out = []
    for j in range(n):
        tiles = []
        mine = units[4 * j:4 * j + 4]
        for a, (q, cached, n_old, new, bias, value) in enumerate(branches):
            scores = []
            for u, unit in enumerate(mine):
                scores.append((32 * u, 32 * u + 32, 0, n_old, q(unit), cached(unit)))
                if new:
                    scores.append((32 * u, 32 * u + 32, n_old, TS, q(unit), new(unit)))
            n_keys = n_old + (TS if new else 0)
            n_chunk = -(-n_keys // P)
            values = []
            for u, unit in enumerate(mine):
                for k in range(n_chunk):
                    values.append((32 * u, 32 * u + 32, a * P, P, slice(32 * u, 32 * u + 32), k,
                                   value(unit, k, min(P, n_keys - k * P)), a == 0 and k == 0,
                                   a == len(branches) - 1 and k == n_chunk - 1))
            tiles.append(Tile(scores, [bias(j)] if bias else [], n_keys, values, ("act", "dve")[a % 2]))
        out.append(Group(tiles, 1, len(branches), gate(j) if gate else None, leaves(j)))
    return out



def stage_compress(c, projT, k_cmpT, v_cmp_p, v_cmp_s, stacks):
    nc = c.nc
    block, sem = stage(c, "compress")
    d, tags = c.dram, ("k", "v")
    zeroed, table_in, small_in, pe_t, pe_m, placed, bias_m, gelu, outp, outm, win_out, v_clear = (sem(s) for s in
        ("zeroed", "table_in", "small_in", "pe_t", "pe_m", "placed", "bias_m", "gelu", "outp", "outm", "win_out", "v_clear"))
    w1_in, hid, turned, stacked = sem("w1_in"), sem("hid"), sem("turned"), sem("stacked")
    n_ring = 8
    land = [sem(f"land{i}") for i in range(n_ring)]
    evac = [sem("evac_dve"), sem("evac_act")]
    N = (2 * SEQ + 2 * DEC_B * PAST) // CMP_S
    OLD = 2 * SEQ
    steps = [(tag, b, g) for tag in range(2) for b in range(DEC_B) for g in range(NPAGE)]
    per = len(steps) // 2
    w1d = [x[:, 0:CMP_W // 2 * P].rearrange("p (j e) -> p j e", e=P) for x in
           (c.w_raw[:, :, :, :].rearrange("p s k n -> p (s k n)"), projT[:, 16:20, :].rearrange("p k n -> p (k n)"))]
    with ExitStack() as tmp:
        sb = lambda n, s, dt=F32: tmp.enter_context(nc.sbuf_tensor(n, s, dt))
        line = sb("cp_line", [P, N * CMP_S + CMP_W])
        table = sb("cp_table", [1, DEC_B * NPAGE], I32)
        ring = sb("cp_ring", [P, n_ring, 2 * P])
        w2d = sb("cp_w2", [P, 2, P])
        rows = sb("cp_pe_rows", [CMP_W, 2, P])
        bias = sb("cp_bias", [P, 2])
        hidT = sb("cp_hidT", [P, N])
        old = line[:, OLD:OLD + 2 * DEC_B * PAST].rearrange("p (a b n) -> p a b n", a=2, b=DEC_B)
        with block as blk:
            @blk.gpsimd
            def _(pool):
                for x in w1d:
                    pool.memset(x, 0.0).then_inc(zeroed, 1)
                pool.memset(w2d[:, :, :], 0.0).then_inc(zeroed, 1)

            @blk.sync
            def _(sp):
                sp.dma_start(table[:, :], d["page_table"].rearrange("(a b) g -> a (b g)", a=1)).then_inc(table_in, 16)
                sp.wait_ge(table_in, 16)

                def load_page(n):
                    tag, b, g = steps[n]
                    cache = d["cache_c_cmp_" + tags[tag]]
                    page = sp.value_load(table[0:1, b * NPAGE + g:b * NPAGE + g + 1], min_val=0, max_val=cache.shape[1] - 1)
                    if n >= n_ring:
                        sp.wait_ge(turned, n - n_ring + 1)
                    sp.dma_start(ring[:, n % n_ring, :], cache[0][bass.ds(page, 1)].rearrange("a p g e -> p (a g e)")).then_inc(land[n % n_ring], 16)

                def load_w1(tag):
                    w1 = d["c_cmp_w1_" + tags[tag]][0].rearrange("j d e -> d j e")
                    for s in range(2):
                        own = rows_of(s)
                        for half, x in enumerate(w1d):
                            at = slice(half * CMP_W // 2, (half + 1) * CMP_W // 2)
                            sp.dma_start(x[own, :, own], w1[:, at, :]).then_inc(w1_in, 16)

                for n in range(n_ring):
                    load_page(n)
                sp.wait_ge(zeroed, 3)
                load_w1(0)
                for tag in range(2):
                    for s in range(2):
                        own = rows_of(s)
                        sp.dma_start(w2d[own, tag, own], d["c_cmp_w2_" + tags[tag]][0]).then_inc(small_in, 16)
                        sp.dma_start(rows[:, tag, own], d["c_cmp_pe_" + tags[tag]][0]).then_inc(small_in, 16)
                for n in range(n_ring, per):
                    load_page(n)
                for tag in tags:
                    sp.dma_start(d[f"c_win_{tag}_s"][0][:, 0:PAST - DEC_T], d[f"state_c_win_{tag}"][0][:, DEC_T:PAST]).then_inc(win_out, 16)
                for n in range(per, per + n_ring):
                    load_page(n)
                sp.wait_ge(hid, 1)
                load_w1(1)
                for n in range(per + n_ring, 2 * per):
                    load_page(n)
                sp.wait_ge(win_out, 32)

            def second(pe, tag):
                pe.wait_ge(gelu, tag + 1)
                if tag == 0:
                    pe.matmul(c.ps[:, 2, 0:N], w2d[:, 0, :], hidT[:, :], start=True, stop=True).then_inc(outp, 1)
                    return
                pe.wait_ge(outm, 1)
                for i in range(2):
                    pe.matmul(c.ps[0:NCMP_P, 2, i * P:(i + 1) * P], hidT[:, 32 * i:32 * i + NCMP_P], w2d[:, 1, :],
                              start=(i == 0), stop=(i == 1), skip_group_check=True)
                for i in range(2 * DEC_B):
                    c0 = OLD // CMP_S + i * (PAST // CMP_S)
                    last = pe.matmul(c.ps[0:NCMP_S, 3 + i // 4, (i % 4) * P:(i % 4 + 1) * P], hidT[:, c0:c0 + NCMP_S], w2d[:, 1, :],
                                     start=(i % 4 == 0), stop=(i % 4 == 3), skip_group_check=True)
                last.then_inc(outp, 1)

            @blk.tensor
            def _(pe):
                for tag in range(2):
                    for n in range(tag * per, (tag + 1) * per):
                        if n >= 4:
                            pe.wait_ge(evac[n % 2], (n - 4) // 2 + 1)
                        pe.wait_ge(land[n % n_ring], 16 * (n // n_ring + 1))
                        for h in range(2):
                            last = pe.transpose(c.ps[:, 3 + n % 4, h * P:(h + 1) * P], ring[:, n % n_ring, h * P:(h + 1) * P], c.k("ident"))
                        last.then_inc(turned, 1)
                    if tag == 0:
                        pe.wait_ge(small_in, 16 * 8)
                    else:
                        second(pe, 0)
                    pe.transpose(c.ps[:, 1, tag * CMP_W:(tag + 1) * CMP_W], rows[:, tag, :], c.k("ident")[0:CMP_W, 0:CMP_W]).then_inc(pe_t, 1)
                    pe.wait_ge(pe_m, tag + 1)
                    pe.wait_ge(placed, 2 * (tag + 1))
                    for e in evac:
                        pe.wait_ge(e, (tag + 1) * per // 2)
                    pe.wait_ge(w1_in, 64 * (tag + 1))
                    for j in range(CMP_W):
                        last = pe.matmul(c.ps[:, 0, 0:N + 1], w1d[j // (CMP_W // 2)][:, j % (CMP_W // 2), :],
                                         line[:, j:j + N * CMP_S + 1:CMP_S], start=j == 0, stop=j == CMP_W - 1)
                    last.then_inc(hid, 1)
                second(pe, 1)

            def move(eng, copy, n):
                tag, b, g = steps[n]
                eng.wait_ge(turned, n + 1)
                copy(old[:, :, b, g * PAGE:(g + 1) * PAGE], c.ps[:, 3 + n % 4, 0:2 * P].rearrange("p (h n) -> p h n", n=P)).then_inc(evac[n % 2], 1)

            def place(eng, copy, tag, i):
                copy(line[:, i * SEQ:(i + 1) * SEQ], projT[:, (8, 14)[tag] + i, 0:SEQ]).then_inc(placed, 1)

            n_hi, n_lo = len(stacks.hi), len(stacks.lo)

            @blk.vector
            def _(dve):
                for tag in range(2):
                    if tag:
                        stacks.fill_lo(dve, stacked, 0, n_lo // 2)
                        dve.wait_ge(hid, 1)
                        dve.wait_ge(gelu, 1)
                    place(dve, dve.tensor_copy, tag, 0)
                    for n in range(tag * per, (tag + 1) * per, 2):
                        move(dve, dve.tensor_copy, n)
                    if tag:
                        dve.wait_ge(outp, 1)
                        dve.tensor_copy(k_cmpT[:, :], c.ps[:, 2, 0:N]).then_inc(outm, 1)
                    dve.wait_ge(pe_t, tag + 1)
                    dve.tensor_copy(line[:, N * CMP_S:N * CMP_S + CMP_W], c.ps[:, 1, tag * CMP_W:(tag + 1) * CMP_W]).then_inc(pe_m, 1)
                dve.memset(v_cmp_p[:, :], 0.0).then_inc(v_clear, 1)
                stacks.fill_lo(dve, stacked, n_lo // 2, n_lo)
                dve.wait_ge(v_clear, 1)
                dve.wait_ge(outp, 2)
                for i in range(4):
                    dve.tensor_copy(v_cmp_p[32 * i:32 * i + NCMP_P, :], c.ps[0:NCMP_P, 2, 0:2 * P])

            @blk.scalar
            def _(act):
                copy = lambda out, in_: act.activation(out, in_, ACT.Copy)
                for tag in range(2):
                    if tag:
                        act.wait_ge(hid, 1)
                    place(act, copy, tag, 1)
                    for n in range(tag * per + 1, (tag + 1) * per, 2):
                        move(act, copy, n)
                    stacks.fill_hi(copy, stacked, tag * n_hi // 2, (tag + 1) * n_hi // 2)
                    act.wait_ge(hid, tag + 1)
                    copy(bias[:, tag:tag + 1], c.ps[:, 0, N:N + 1]).then_inc(bias_m, 1)
                    act.wait_ge(bias_m, tag + 1)
                    if tag:
                        act.wait_ge(outp, 1)
                    act.activation(hidT[:, :], c.ps[:, 0, 0:N], ACT.Gelu_apprx_tanh, bias=bias[:, tag:tag + 1]).then_inc(gelu, 1)
                act.wait_ge(outp, 2)
                copy(v_cmp_s[0:NCMP_S, :].rearrange("p (a n) -> p a n", a=4), c.ps[0:NCMP_S, 3:7, :])


def stage_gates(c, projT, gate_sig, gate_s, q_blk, k_cmpT, kc2):
    nc = c.nc
    block, sem = stage(c, "gates")
    sig, picked, link = sem("sig"), sem("picked"), sem("link")
    with ExitStack() as tmp:
        hit = tmp.enter_context(nc.sbuf_tensor("gt_hit", [P, 3, 16], F32))
        cleared, stacked = sem("cleared"), sem("stacked")
        with block as blk:
            @blk.gpsimd
            def _(pool):
                pool.memset(kc2[:, :, :, :].bitcast(F32), 0.0).then_inc(cleared, 1)
                pool.wait_ge(cleared, 1)
                stacks = Stack()
                for a in range(2):
                    for side in range(2):
                        stacks.keys(side, k_cmpT[rows_of(side), 32 * a:32 * a + NCMP_P],
                                    kc2[:, 0, 2 * a + side, 0:NCMP_P], kc2[:, 1, 2 * a + side, 0:NCMP_P])
                stacks.fill_hi(pool.tensor_copy, stacked, 0, len(stacks.hi))
                stacks.fill_lo(pool, stacked, 0, len(stacks.lo))

            @blk.scalar
            def _(act):
                act.activation(gate_sig[:, 0:NB, :], gate_sig[:, 0:NB, :], ACT.Sigmoid)
                act.activation(gate_sig[0:TS, NB, :], gate_sig[0:TS, NB, :], ACT.Sigmoid).then_inc(sig, 1)

            @blk.tensor
            def _(pe):
                pe.wait_ge(sig, 1)
                for j in range(4):
                    last = pe.matmul(c.ps[:, 0, 48 * j:48 * j + 48], c.k("pick")[0:TS, (2 + j) * P:(3 + j) * P],
                                     gate_sig[0:TS, NB, :], start=(j == 0), stop=(j == 3), skip_group_check=True)
                last.then_inc(picked, 1)

            @blk.vector
            def _(dve):
                count = [0]

                def linked(ins):
                    count[0] += 1
                    ins.then_inc(link, 1)
                    dve.wait_ge(link, count[0])

                linked(dve.memset(q_blk[:, :, :, :, :, :], 0.0))
                for side in range(2):
                    rows = slice(side * HD, side * HD + HD)
                    for pair in range(2):
                        for h in range(4):
                            linked(dve.tensor_copy(q_blk[rows, :, pair, side, h, :],
                                                   projT[rows, 4 * pair + h, SEQ:T].rearrange("p (b t) -> p b t", t=DEC_T)))
                dve.wait_ge(picked, 1)
                for j in range(4):
                    g = c.ps[:, 0, 48 * j:48 * j + 48].rearrange("p (h a) -> p a h", a=3)
                    for a in range(3):
                        linked(dve.tensor_tensor(hit[:, a, :], g[:, a, :], c.k("chead"), ALU.mult))
                    linked(dve.reduce_sum(gate_s[:, j, :], hit[:, :, :], AX_X))



def program(nc, dram):
    with ExitStack() as ctx:
        c = setup_memory(nc, ctx, dram)
        d = dram
        pair = lambda a, b: [(0, a, HD), (HD, b, HD)]
        a_rope = [pair(A_Q + i * HD, A_Q + (4 + i) * HD) for i in range(4)]
        a_rope += [[(0, A_IQ, P)], [(0, A_IQ + P, P)], [(0, A_K, P)], pair(A_IK, A_IK)]
        a_plain = [[(0, A_V, P)], [(0, A_IW, P)]] + [[(0, A_GB + i * P, P)] for i in range(12)]
        c_rope = [pair(C_Q + p * 512 + h * HD, C_Q + p * 512 + 256 + h * HD) for p in range(2) for h in range(4)]
        c_rope += [[(0, col + i * P, P)] for col in (C_KC, C_KS, C_KW) for i in range(2)]
        c_plain = [[(0, col + i * P, P)] for col in (C_VC, C_VS, C_VW) for i in range(2)]
        c_plain += [[(0, C_G + 48 - P, P)]]
        stage_load(c, [(slab_pieces(d["ab_w_in"][0], a_rope[n]), KT) for n in range(2)])

        with ExitStack() as mem:
            sb = lambda n, s, dt=F32: mem.enter_context(nc.sbuf_tensor(n, s, dt))
            projT = sb("a_projT", [P, 22, T])
            stage_in_proj(c, "a_in", d["ab_w_in"][0], a_rope, a_plain, projT)
            v_rows = sb("a_v_rows", [P, NB + 1, P])
            iw_full = sb("a_iw_rows", [P, NB + 1, P])
            iw = sb("a_iw", [P, NB + 1, 4])
            p_rows = lambda name: d[name][0, 0].rearrange("t g e -> t (g e)")
            s_rows = lambda name: d[name][0].rearrange("b t g e -> (b t) (g e)")
            stage_rows(c, "a_rows", projT, [
                (6, None, [(0, p_rows("a_k_p"), s_rows("a_k_s"))]),
                (7, None, [(0, d["a_ik_p"][0, 0], d["a_ik_s"][0].rearrange("b t e -> (b t) e"))]),
                (8, v_rows, [(0, p_rows("a_v_p"), s_rows("a_v_s"))]),
                (9, iw_full, [])])
            sel = sb("a_sel", [P, NB, SEQ], BF16)
            reuse_semaphores(c)
            stage_conv(c, projT)
            a_more = sb("a_more_stacks", [P, 2, SEQ], F32R)
            slots = idle_slots(c) + [a_more[:, e, :] for e in range(2)]
            a_q2, a_k2 = slots[0:8], slots[8:12]
            stacks = Stack()
            for side in range(2):
                for i in range(4):
                    stacks.queries(side, projT[rows_of(side), i, 0:SEQ], a_q2[2 * i + side])
                stacks.keys(side, projT[rows_of(side), 6, 0:SEQ], a_k2[2 * side], a_k2[2 * side + 1])
            stage_index_prompt(c, projT, iw, sel, iw_full[:, :, 0:4], stacks)
            stage_attend_prompt(c, "a_att", *prompt_tiles(1, [(
                lambda i, s, qb: a_q2[2 * i + s][:, qb * P:(qb + 1) * P],
                lambda a, s: a_k2[2 * s:2 * s + 2],
                lambda a, s, k: v_rows[:, k, rows_of(s)],
                lambda qb: (0, (qb + 1) * P, sel[:, qb, 0:(qb + 1) * P]) if qb else (0, P, c.causal_bf[:, :]),
                lambda i, s, qb: None, lambda side: ("act", "dve")[side])]))

            kT = sb("a_kT", [P, 1, DEC_B, PAST])
            ikT = sb("a_ikT", [P, 1, DEC_B, PAST])
            v_old = sb("a_v_old", [P, DEC_B, NPAGE, P])
            page = lambda name: lambda r: d[name][0][bass.ds(r, 1)].rearrange("a p g e -> p (a g e)")
            stage_pages(c, "a_pages", list(range(DEC_B)), [
                (page("cache_a_k"), [(0, P)], kT),
                (lambda r: d["cache_a_ik"][0][bass.ds(r, 1)].rearrange("a p e -> p (a e)"), [(0, HD), (HD, HD)], ikT)],
                [(lambda b, g, r: page("cache_a_v")(r), lambda b, g: v_old[:, b, g, :])])
            sel_s = sb("a_sel_s", [P, 2, NEW], BF16)
            q_blk = sb("a_q_blk", [P, DEC_B, 2, 4, DEC_T])
            stage_index_sample(c, projT, iw[0:TS, NB, :], ikT, sel_s, q_blk)
            q_of = lambda b: q_blk[:, b].rearrange("p s h t -> p (s h t)")

            def a_leaves(j):
                def side(s):
                    place = lambda x: x[rows_of(s), 0:4, SEQ + 16 * j:SEQ + 16 * j + 16].rearrange("p h (u t) -> p u h t", t=DEC_T)
                    cols = lambda o: o[rows_of(s), 0:P].rearrange("p (u s h t) -> p u s h t", u=4, s=2, h=4)[:, :, s]
                    return [(lambda x, u=u: place(x)[:, u], lambda o, u=u: cols(o)[:, u]) for u in range(4)]
                return side(0) + side(1)

            def a_out_rows(w, cols):
                return [(lambda r: r[0:HD, 0:4, :], w[0:256, cols].rearrange("(k p) n -> p k n", p=HD)),
                        (lambda r: r[HD:P, 0:4, :], w[256:512, cols].rearrange("(k p) n -> p k n", p=HD)),
                        (lambda r: r[:, 4:8, :], w[512:1024, cols].rearrange("(k p) n -> p k n", p=P))]

            stage_attend(c, "a_att_s", sample_groups(2, list(range(DEC_B)), [(
                q_of, lambda b: kT[:, 0, b, :], PAST, lambda b: projT[:, 6, SEQ:T],
                lambda j: (0, NEW, sel_s[:, j, :]),
                lambda b, k, n: v_old[:, b, k, :] if k < NPAGE else v_rows[0:TS, NB, :])],
                None, a_leaves), [(a_out_rows(d["ab_w_out"][0], slice(n * P, (n + 1) * P)), KT) for n in range(2)])

            stage_out_proj(c, "a_out", d["ab_w_out"][0], a_out_rows)
        reuse_semaphores(c)
        finish_layer(c, 0, [(slab_pieces(d["c_w_in"][0], c_rope[n]), KT) for n in range(2)])
        reuse_semaphores(c)

        with ExitStack() as mem:
            sb = lambda n, s, dt=F32: mem.enter_context(nc.sbuf_tensor(n, s, dt))
            projT = sb("c_projT", [P, 21, T])
            stage_in_proj(c, "c_in", d["c_w_in"][0], c_rope, c_plain, projT)
            vs_rows = [sb(f"vs_rows{i}", [P, NB + 1, P]) for i in range(2)]
            vw_rows = [sb(f"vw_rows{i}", [P, NB + 1, P]) for i in range(2)]
            k_cmpT = sb("k_cmpT", [P, (2 * SEQ + 2 * DEC_B * PAST) // CMP_S])
            v_cmp_p = sb("v_cmp_p", [P, 2 * P])
            kc2 = sb("kc2", [P, 2, 4, 32], F32R)
            g_rows = sb("g_rows", [P, NB + 1, P])
            gate_s = sb("gate_s", [P, 4, 3])
            p_rows = lambda name, i: d[name][0, 0].rearrange("t g e -> t (g e)")[:, i * P:(i + 1) * P]
            s_rows = lambda name, i: d[name][0].rearrange("b t g e -> (b t) (g e)")[:, i * P:(i + 1) * P]
            w_new = lambda name, i: d[name][0][:, PAST - DEC_T:PAST].rearrange("b t g e -> b t (g e)")[:, :, i * P:(i + 1) * P]
            stage_rows(c, "c_rows", projT,
                       [(8 + i, None, [(0, p_rows("c_cmp_k_p", i), s_rows("c_cmp_k_s", i))]) for i in range(2)]
                       + [(10 + i, None, [(0, p_rows("c_slc_k_p", i), s_rows("c_slc_k_s", i))]) for i in range(2)]
                       + [(12 + i, None, [(0, p_rows("c_win_k_p", i), w_new("c_win_k_s", i))]) for i in range(2)]
                       + [(14 + i, None, [(0, p_rows("c_cmp_v_p", i), s_rows("c_cmp_v_s", i))]) for i in range(2)]
                       + [(16 + i, vs_rows[i], [(0, p_rows("c_slc_v_p", i), s_rows("c_slc_v_s", i))]) for i in range(2)]
                       + [(18 + i, vw_rows[i], [(0, p_rows("c_win_v_p", i), w_new("c_win_v_s", i))]) for i in range(2)]
                       + [(20, g_rows, [])])
            slots = idle_slots(c)

            def section_stacks(a, q2, k2):
                stacks = Stack()
                for side in range(2):
                    for i in range(4):
                        stacks.queries(side, projT[rows_of(side), 4 * a + i, 0:SEQ], q2[2 * i + side])
                    for b, slab in enumerate((10, 12)):
                        at = 4 * b + 2 * side
                        stacks.keys(side, projT[rows_of(side), slab + a, 0:SEQ], k2[at], k2[at + 1])
                return stacks

            q2_first, k2_first = [x[:, 4 + i, 0:SEQ] for i in range(4) for x in (c.x_hi, c.x_lo)], slots[0:8]
            stacks = section_stacks(0, q2_first, k2_first)
            v_cmp_s = projT[:, 14:18, :].rearrange("p k n -> p (k n)")[:, 0:2 * DEC_B * P]
            stage_compress(c, projT, k_cmpT, v_cmp_p, v_cmp_s, stacks)
            reuse_semaphores(c)
            gate_sig = g_rows[:, :, P - 48:P]
            q_blk = projT[:, 8, 0:SEQ].rearrange("p (b i s h t) -> p b i s h t", b=DEC_B, i=2, s=2, h=4)
            stage_gates(c, projT, gate_sig, gate_s, q_blk, k_cmpT, kc2)

            def c_out_rows(w, cols):
                v = w[:, cols].rearrange("(a s h p) n -> a s p h n", a=2, s=2, h=4)
                return [((lambda r, a=a, s=s: r[rows_of(s), 4 * a:4 * a + 4, :]), v[a, s]) for a in range(2) for s in range(2)]

            def gate(i, qb):
                g = gate_sig[:, qb, i // 4 * 24:i // 4 * 24 + 24].rearrange("p (s h a) -> p s h a", s=2, h=4)
                return g[:, :, i % 4, :]

            causal = lambda qb: (qb * P, P, c.causal_bf[:, :])
            till_samples = ExitStack()
            more = till_samples.enter_context(nc.sbuf_tensor("more_stacks", [P, 14, SEQ], F32R))
            slots += [more[:, e, :] for e in range(14)]
            c_q2, c_k2 = q2_first + slots[8:16], k2_first + slots[16:24]
            c_q = lambda i, s, qb: c_q2[2 * i + s][:, qb * P:(qb + 1) * P]
            c_gate = lambda branch: (lambda i, s, qb: gate(i, qb)[:, s, branch:branch + 1])
            kc = lambda part, a, s: kc2[:, part, 2 * a + s, :]
            short = lambda a, qb: Short(
                [(c_q(4 * a + h, s, qb), kc(0, a, s), kc(1, a, s)) for s in range(2) for h in range(4)],
                c.cmp_bf[:, qb * 32:qb * 32 + 32].rearrange("p (a n) -> p a n", a=1).broadcast_to([P, 8, 32]),
                gate_sig[:, qb, a * 24:a * 24 + 24].rearrange("p (s h b) -> p s h b", s=2, h=4)[:, :, :, 0])
            stage_attend_prompt(c, "c_att", *prompt_tiles(2, [
                (c_q, lambda a, s: c_k2[8 * a + 2 * s:8 * a + 2 * s + 2],
                 lambda a, s, k: vs_rows[a][:, k, rows_of(s)], causal, c_gate(1), lambda side: "act"),
                (c_q, lambda a, s: c_k2[8 * a + 4 + 2 * s:8 * a + 6 + 2 * s],
                 lambda a, s, k: vw_rows[a][:, k, rows_of(s)], causal, c_gate(2), lambda side: ("act", "dve")[side])],
                (short, lambda a, s, i: v_cmp_p[32 * i:32 * i + 32, a * P + s * HD:a * P + (s + 1) * HD])),
                late=section_stacks(1, c_q2[8:16], c_k2[8:16]))

            till_samples.close()
            for half in range(2):
                seqs = list(range(4 * half, 4 * half + 4))
                with ExitStack() as tmp:
                    sbt = lambda n, s: tmp.enter_context(nc.sbuf_tensor(f"{n}{half}", s, F32))
                    ksT = sbt("ksT", [P, 2, 4, PAST])
                    kwT = sbt("kwT", [P, 2, 4, PAST])
                    vs_old = sbt("vs_old", [P, 4, NPAGE, 2 * P])
                    vw_old = sbt("vw_old", [P, 4, NPAGE, 2 * P])
                    stage_pages_c(c, f"c_pages{half}", seqs, ksT, kwT, vs_old, vw_old)
                    units = [(b, p) for b in seqs for p in range(2)]
                    q_of = lambda u: q_blk[:, u[0], u[1]].rearrange("p s h t -> p (s h t)")
                    new_bias = lambda j: (PAST, TS, c.new_bf[:, (2 + 2 * half + j) * TS:(3 + 2 * half + j) * TS])
                    g_of = lambda j: gate_s[:, 2 * half + j:2 * half + j + 1, :]

                    def c_leaves(j):
                        out = []
                        for s in range(2):
                            for u in range(4):
                                b, p = units[4 * j + u]
                                out.append((lambda x, s=s, b=b, p=p: x[rows_of(s), 4 * p:4 * p + 4, SEQ + 4 * b:SEQ + 4 * b + 4],
                                            lambda o, s=s, u=u: o[rows_of(s), 32 * u + 16 * s:32 * u + 16 * s + 16]
                                            .rearrange("p (h t) -> p h t", t=DEC_T)))
                        return out

                    old_v = lambda old, new: (lambda u, k, n: old[:, seqs.index(u[0]), k, u[1] * P:(u[1] + 1) * P]
                                              if k < NPAGE else new[u[1]][0:TS, NB, :])
                    cmp_at = lambda u: 2 * SEQ // CMP_S + (u[1] * DEC_B + u[0]) * PAST // CMP_S
                    stage_attend(c, f"c_att_s{half}", sample_groups(2, units, [
                        (q_of, lambda u: k_cmpT[:, cmp_at(u):cmp_at(u) + NCMP_S], NCMP_S, None, None,
                         lambda u, k, n: v_cmp_s[0:NCMP_S, (u[1] * DEC_B + u[0]) * P:(u[1] * DEC_B + u[0] + 1) * P]),
                        (q_of, lambda u: ksT[:, u[1], seqs.index(u[0]), :], PAST, lambda u: projT[:, 10 + u[1], SEQ:T],
                         new_bias, old_v(vs_old, vs_rows)),
                        (q_of, lambda u: kwT[:, u[1], seqs.index(u[0]), :], PAST, lambda u: projT[:, 12 + u[1], SEQ:T],
                         new_bias, old_v(vw_old, vw_rows))], g_of, c_leaves),
                        [(c_out_rows(d["c_w_out"][0], slice(n * P, (n + 1) * P)), KT) for n in range(2)] if half else None)

            stage_out_proj(c, "c_out", d["c_w_out"][0], c_out_rows)
        reuse_semaphores(c)
        finish_layer(c, 1, None)
        stage_store(c)


def stage_pages_c(c, name, seqs, ksT, kwT, vs_old, vw_old):
    d = c.dram
    by_page = lambda n: lambda r: d[n][0][bass.ds(r, 1)].rearrange("a p g e -> p (a g e)")
    by_seq = lambda n: lambda b, g: d[n][0, b, g * PAGE:(g + 1) * PAGE].rearrange("p g e -> p (g e)")
    stage_pages(c, name, seqs, [(by_page("cache_c_slc_k"), [(0, 2 * P)], ksT)],
                [(lambda b, g, r: by_page("cache_c_slc_v")(r), lambda b, g: vs_old[:, seqs.index(b), g, :]),
                 (lambda b, g, r: by_seq("state_c_win_v")(b, g), lambda b, g: vw_old[:, seqs.index(b), g, :])])
    stage_turn_rows(c, name + "w", seqs, by_seq("state_c_win_k"), kwT)


def stage_turn_rows(c, name, seqs, src, dst):
    nc = c.nc
    block, sem = stage(c, name)
    land = [sem(f"land{i}") for i in range(4)]
    turned, evac = sem("turned"), sem("evac")
    steps = [(b, g) for b in seqs for g in range(NPAGE)]
    with ExitStack() as tmp:
        ring = tmp.enter_context(nc.sbuf_tensor(f"{name}_ring", [P, 4, 2 * P], F32))
        with block as blk:
            @blk.sync
            def _(sp):
                for n, (b, g) in enumerate(steps):
                    if n >= 4:
                        sp.wait_ge(turned, n - 3)
                    sp.dma_start(ring[:, n % 4, :], src(b, g)).then_inc(land[n % 4], 16)

            @blk.tensor
            def _(pe):
                for n in range(len(steps)):
                    pe.wait_ge(land[n % 4], 16 * (n // 4 + 1))
                    if n >= 4:
                        pe.wait_ge(evac, n - 3)
                    for h in range(2):
                        last = pe.transpose(c.ps[:, n % 4, h * P:(h + 1) * P], ring[:, n % 4, h * P:(h + 1) * P], c.k("ident"))
                    last.then_inc(turned, 1)

            @blk.vector
            def _(dve):
                for n, (b, g) in enumerate(steps):
                    dve.wait_ge(turned, n + 1)
                    dve.tensor_copy(dst[:, :, seqs.index(b), g * PAGE:(g + 1) * PAGE],
                                    c.ps[:, n % 4, 0:2 * P].rearrange("p (h n) -> p h n", n=P)).then_inc(evac, 1)


def finish_layer(c, layer, next_units):
    nc = c.nc
    first = slice(0, P)
    stage_norm(c, f"norm{layer}a", layer, [(up_pieces(c.dram["ffn_w_gate"][layer], first), KT),
                                           (up_pieces(c.dram["ffn_w_up"][layer], first), KT)])
    with ExitStack() as mem:
        h_hi = mem.enter_context(nc.sbuf_tensor(f"h_hi{layer}", [P, FT, T], F32R))
        h_lo = mem.enter_context(nc.sbuf_tensor(f"h_lo{layer}", [P, FT, T], F32R))
        stage_ffn_up(c, layer, h_hi, h_lo)
        stage_ffn_down(c, layer, h_hi, h_lo)
    stage_norm(c, f"norm{layer}b", 2 + layer, next_units)


INPUTS = ["x_prompt", "x_sample", "cache_a_k", "cache_a_v", "cache_a_ik", "state_b_conv", "cache_c_cmp_k",
          "cache_c_cmp_v", "cache_c_slc_k", "cache_c_slc_v", "state_c_win_k", "state_c_win_v", "page_table",
          "ab_w_in", "ab_conv_w", "ab_w_out", "c_w_in", "c_cmp_pe_k", "c_cmp_w1_k", "c_cmp_w2_k", "c_cmp_pe_v",
          "c_cmp_w1_v", "c_cmp_w2_v", "c_w_out", "ffn_w_gate", "ffn_w_up", "ffn_w_down", "ln1_g", "ln1_b",
          "ln2_g", "ln2_b"]
_A = (1, 1, SEQ, 2, HD)
_C = (1, 1, SEQ, 4, HD)
_AS = (1, DEC_B, DEC_T, 2, HD)
_CS = (1, DEC_B, DEC_T, 4, HD)
OUTPUTS = {"y_prompt": (1, SEQ, D), "y_sample": (DEC_B, DEC_T, D),
           "a_k_p": _A, "a_v_p": _A, "a_ik_p": (1, 1, SEQ, HD), "b_conv_p": (1, 1, 2, D // 2),
           "c_cmp_k_p": _C, "c_cmp_v_p": _C, "c_slc_k_p": _C, "c_slc_v_p": _C, "c_win_k_p": _C, "c_win_v_p": _C,
           "a_k_s": _AS, "a_v_s": _AS, "a_ik_s": (1, DEC_B, DEC_T, HD), "b_conv_s": (1, DEC_B, 2, D // 2),
           "c_cmp_k_s": _CS, "c_cmp_v_s": _CS, "c_slc_k_s": _CS, "c_slc_v_s": _CS,
           "c_win_k_s": (1, DEC_B, PAST, 4, HD), "c_win_v_s": (1, DEC_B, PAST, 4, HD)}


def kernel(**inputs):
    import concourse.bacc as bacc
    from concourse.bass_utils import run_bass_kernel_spmd as run

    nc = bacc.Bacc("TRN2", target_bir_lowering=False, num_devices=1)
    arrays, dram = {}, {}
    for name in INPUTS:
        a = np.ascontiguousarray(inputs[name])
        arrays[f"in_{name}"] = a
        dram[name] = nc.dram_tensor(f"in_{name}", a.shape, mybir.dt.from_np(a.dtype), kind="ExternalInput").ap()
    arrays["in_const"] = CONST
    dram["const"] = nc.dram_tensor("in_const", CONST.shape, F32, kind="ExternalInput").ap()
    for name, shape in OUTPUTS.items():
        dram[name] = nc.dram_tensor(f"out_{name}", shape, F32, kind="ExternalOutput").ap()
    program(nc, dram)
    r = run(nc, [arrays], core_ids=[0])
    return tuple(r.results[0][f"out_{name}"] for name in OUTPUTS)
```

```python
from contextlib import ExitStack

import numpy as np

import concourse.bass as bass
from concourse import mybir

ALU = mybir.AluOpType
ACT = mybir.ActivationFunctionType
AX_X = mybir.AxisListType.X
F32 = mybir.dt.float32
F32R = mybir.dt.float32r
BF16 = mybir.dt.bfloat16
I32 = mybir.dt.int32

P = 128
D = 1024
KT = D // P
SEQ = 512
NB = SEQ // P
DEC_B = 8
DEC_T = 4
PAST = 256
PAGE = 128
NPAGE = PAST // PAGE
TS = DEC_B * DEC_T
T = SEQ + TS
HALF = T // 2
HD = 64
FF = 2816
FT = FF // P
KCH = FT // 2
TOPK_P = 128
TOPK_S = 65
CMP_W = 32
CMP_S = 16
NCMP_P = (SEQ - CMP_W) // CMP_S + 1
NCMP_S = (PAST + DEC_T - CMP_W) // CMP_S + 1
ALPHA = 4 ** 0.25
EPS = 1e-5
SCALE = HD ** -0.5
BIG = 1e30
TAKEN = -2.0 ** 127
NEW = PAST + TS

A_Q, A_K, A_V, A_IQ, A_IK, A_IW, A_GB, A_GC, A_H = 0, 512, 640, 768, 1024, 1088, 1092, 1604, 2116
C_Q, C_KC, C_VC, C_KS, C_VS, C_KW, C_VW, C_G = 0, 1024, 1280, 1536, 1792, 2048, 2304, 2560


def constants():
    pos = np.concatenate([np.arange(SEQ), PAST + np.tile(np.arange(DEC_T), DEC_B)]).astype(np.float32)
    inv = np.float32(10000.0) ** (-np.arange(HD // 2, dtype=np.float32) / np.float32(HD // 2))
    ang = inv[:, None].astype(np.float32) * pos[None, :]
    cos, sin = np.cos(ang), np.sin(ang)
    parts = {}
    parts["cos"] = np.tile(cos, (4, 1))
    parts["sin"] = np.concatenate([-sin, sin, -sin, sin], 0)
    parts["ident"] = np.eye(P)
    parts["mean"] = np.full((P, P), 1.0 / D)
    q, k = np.arange(P)[:, None], np.arange(P)[None, :]
    parts["causal"] = -1.0 * (k > q)
    row = np.arange(P)
    u, side, head, t = row // 32, row // 16 % 2, row // 4 % 4, row % 4
    new = np.zeros((P, 6, TS))
    pick = np.zeros((P, 6, P))
    for j in range(6):
        b = 4 * j + u if j < 2 else 2 * (j - 2) + u // 2
        tok = np.arange(TS)[None, :]
        new[:, j] = -1.0 * ~((tok // 4 == b[:, None]) & (tok % 4 <= t[:, None]))
        pick[b * 4 + t, j, row] = 1.0
    parts["new"] = new.reshape(P, -1)
    parts["pick"] = pick.reshape(P, -1)
    r = row % 32
    iside, itile = r // 8, r // 4 % 2
    parts["ihead"] = (r < 16)[:, None] * (np.arange(4)[None, :] == (2 * itile + iside)[:, None])
    parts["imix"] = ((r < 16)[:, None] & (u[:, None] == u[None, :]) & (t[:, None] == t[None, :]))
    parts["chead"] = np.arange(16)[None, :] == ((2 * (u % 2) + side) * 4 + head)[:, None]
    cend = np.arange(32)[None, None, :] * CMP_S + CMP_W - 1
    tt = (np.arange(NB)[None, :] * P + row[:, None])[:, :, None]
    parts["cmp"] = (-1.0 * (cend > tt)).reshape(P, -1)
    at, n = {}, 0
    for name, a in parts.items():
        at[name] = (n, n + a.shape[1])
        n += a.shape[1]
    return np.concatenate([a.astype(np.float32) for a in parts.values()], 1), at


CONST, AT = constants()


class Core:
    pass


def setup_memory(nc, ctx, dram):
    c = Core()
    c.nc, c.dram = nc, dram
    c.n_stage = 0
    sb = lambda n, s, d=F32: ctx.enter_context(nc.sbuf_tensor(n, s, d))
    c.sems = []
    c.const = sb("tables", [P, CONST.shape[1]])
    c.causal_bf = sb("causal_bf", [P, P], BF16)
    c.cmp_bf = sb("cmp_bf", [P, NB * 32], BF16)
    c.new_bf = sb("new_bf", [P, 6 * TS], BF16)
    c.ident_big = sb("ident_big", [P, P], BF16)
    c.xT = sb("xT", [P, KT, T])
    c.x_sum = sb("x_sum", [P, T])
    c.x_hi = sb("x_hi", [P, KT, T], F32R)
    c.x_lo = sb("x_lo", [P, KT, T], F32R)
    c.ln_gb = sb("ln_gb", [P, 4, 2, KT])
    c.w_raw = sb("w_raw", [P, 2, KCH, P])
    c.w_hi = sb("w_hi", [P, 2, KCH, P], F32R)
    c.w_lo = sb("w_lo", [P, 2, KCH, P], F32R)
    c.ps = ctx.enter_context(nc.psum_tensor("ps", [P, 8, 512], F32))
    c.k = lambda name: c.const[:, AT[name][0]:AT[name][1]]
    return c


def stage(c, name):
    c.n_stage += 1
    tag = f"{name}{c.n_stage}"


    def sem(signal):
        c.sems.append(c.nc.alloc_semaphore(name=f"{tag}_{signal}"))
        return c.sems[-1]
    return c.nc.Block(tag), sem


def reuse_semaphores(c):
    c.nc.clear_and_free_semaphores(c.sems)
    c.sems = []
    c.nc.all_engine_barrier()


def halves(ap):
    return ap.rearrange("p (h n) -> p h n", h=2)



def load_unit(c, sp, slot, pieces, raw_in):
    for place, src in pieces:
        sp.dma_start(place(c.w_raw[:, slot]), src).then_inc(raw_in, 16)


class Ahead:

    def __init__(self, c, sem, units):
        self.c, self.units = c, units
        self.raw_in = [sem("ahead_raw0"), sem("ahead_raw1")]
        self.hi_made = sem("ahead_hi")

    def load(self, sp):
        for slot, (pieces, _) in enumerate(self.units):
            load_unit(self.c, sp, slot, pieces, self.raw_in[slot])

    def split_hi(self, act, slot):
        pieces, kt = self.units[slot]
        act.wait_ge(self.raw_in[slot], 16 * len(pieces))
        split_hi(self.c, act, slot, kt).then_inc(self.hi_made, 1)

    def split_lo(self, dve, slot):
        dve.wait_ge(self.hi_made, slot + 1)
        split_lo(self.c, dve, slot, self.units[slot][1])


def pe_first_unit(c, pe, start):
    for k in range(KT):
        start.wait_tile(pe, k)
        for h in range(2):
            cols = slice(h * HALF, (h + 1) * HALF)
            out = c.ps[:, h, 0:HALF]
            pe.matmul(out, c.w_hi[:, 0, k, :], c.x_hi[:, k, cols], start=k == 0, stop=False)
            pe.matmul(out, c.w_hi[:, 0, k, :], c.x_lo[:, k, cols], start=False, stop=False)
            last = pe.matmul(out, c.w_lo[:, 0, k, :], c.x_hi[:, k, cols], start=False, stop=k == KT - 1)
    return last


def pe_unit(c, pe, slot, kt, k0, x_hi, x_lo, bank, start, stop):
    for h in range(2):
        cols = slice(h * HALF, (h + 1) * HALF)
        out = c.ps[:, bank + h, 0:HALF]
        for k in range(kt):
            first, end = start and k == 0, stop and k == kt - 1
            pe.matmul(out, c.w_hi[:, slot, k, :], x_hi[:, k0 + k, cols], start=first, stop=False)
            pe.matmul(out, c.w_hi[:, slot, k, :], x_lo[:, k0 + k, cols], start=False, stop=False)
            last = pe.matmul(out, c.w_lo[:, slot, k, :], x_hi[:, k0 + k, cols], start=False, stop=end)
    return last


def split_hi(c, act, slot, kt):
    return act.activation(c.w_hi[:, slot, 0:kt, :], c.w_raw[:, slot, 0:kt, :], ACT.Copy)


def split_lo(c, dve, slot, kt):
    return dve.tensor_tensor(c.w_lo[:, slot, 0:kt, :], c.w_raw[:, slot, 0:kt, :],
                             c.w_hi[:, slot, 0:kt, :].bitcast(F32), ALU.subtract)


def w_rows(w, cols, k0=0, kt=KT):
    return w[k0 * P:(k0 + kt) * P, cols].rearrange("(k p) n -> p k n", p=P)


def slab_pieces(w, slab):
    return [(lambda r, d0=d0, n=n: r[:, 0:KT, d0:d0 + n], w_rows(w, slice(col, col + n))) for d0, col, n in slab]


def up_pieces(w, cols):
    return [(lambda r: r[:, 0:KT, :], w_rows(w, cols))]


def down_pieces(w, s, cols):
    return [(lambda r: r[:, :, :], w_rows(w, cols, s * KCH, KCH))]



class Load:

    def __init__(self, c, sem, tmp):
        self.c = c
        self.x_nat = tmp.enter_context(c.nc.sbuf_tensor("x_nat", [P, NB + 1, D], F32))
        self.ln_nat = tmp.enter_context(c.nc.sbuf_tensor("ln_nat", [64, P], F32))
        self.const_in, self.ln_in, self.turned, self.evac, self.hi, self.lo, self.ln_t, self.ln_e, self.masks = (sem(s) for s in
            ("const_in", "ln_in", "turned", "evac", "x_hi_set", "x_lo_set", "ln_turned", "ln_evac", "masks"))
        self.x_in = [sem(f"x_in{i}") for i in range(KT // 2)]

    def sync(self, sp):
        c = self.c
        sp.dma_start(c.const[:, :], c.dram["const"]).then_inc(self.const_in, 16)
        for i in range(KT // 2):
            cols = slice(2 * i * P, 2 * (i + 1) * P)
            sp.dma_start(self.x_nat[:, 0:NB, cols], c.dram["x_prompt"][0][:, cols].rearrange("(b p) d -> p b d", p=P)).then_inc(self.x_in[i], 16)
            sp.dma_start(self.x_nat[0:TS, NB, cols], c.dram["x_sample"].rearrange("b t d -> (b t) d")[:, cols]).then_inc(self.x_in[i], 16)

    def sync_late(self, sp):
        c = self.c
        for i, name in enumerate(("ln1_g", "ln1_b", "ln2_g", "ln2_b")):
            sp.dma_start(self.ln_nat[16 * i:16 * i + 16, :], c.dram[name].rearrange("l (k p) -> (l k) p", p=P)).then_inc(self.ln_in, 16)

    def pe(self, pe):
        c = self.c
        pe.wait_ge(self.const_in, 16)
        for k in range(KT):
            pe.wait_ge(self.x_in[k // 2], 32)
            if k >= 3:
                pe.wait_ge(self.evac, k - 2)
            b0 = 2 + 2 * (k % 3)
            for b in range(NB):
                pe.transpose(c.ps[:, b0, b * P:(b + 1) * P], self.x_nat[:, b, k * P:(k + 1) * P], c.k("ident"))
            pe.transpose(c.ps[:, b0 + 1, 0:TS], self.x_nat[0:TS, NB, k * P:(k + 1) * P],
                         c.k("ident")[0:TS, 0:TS]).then_inc(self.turned, 1)
        pe.wait_ge(self.ln_in, 64)
        pe.transpose(c.ps[:, 0, 0:64], self.ln_nat[:, :], c.k("ident")[0:64, 0:64]).then_inc(self.ln_t, 1)
        pe.wait_ge(self.ln_e, 1)

    def dve(self, dve, split):
        c = self.c
        for k in range(KT):
            dve.wait_ge(self.turned, k + 1)
            b0 = 2 + 2 * (k % 3)
            dve.tensor_copy(c.xT[:, k, 0:SEQ], c.ps[:, b0, :])
            dve.tensor_copy(c.xT[:, k, SEQ:T], c.ps[:, b0 + 1, 0:TS]).then_inc(self.evac, 1)
            if k >= 1:
                self.low(dve, k - 1)
            if k >= KT - 2:
                split(k - KT + 2)
        self.low(dve, KT - 1)
        dve.wait_ge(self.ln_t, 1)
        dve.tensor_copy(c.ln_gb[:, :, :, :].rearrange("p (w l) g k -> p w g l k", w=2),
                        c.ps[:, 0, 0:64].rearrange("p (w g l k) -> p w g l k", w=2, g=2, l=2)).then_inc(self.ln_e, 1)

    def low(self, dve, k):
        c = self.c
        dve.wait_ge(self.hi, k + 1)
        dve.tensor_tensor(c.x_lo[:, k, :], c.xT[:, k, :], c.x_hi[:, k, :].bitcast(F32), ALU.subtract).then_inc(self.lo, 1)

    def act(self, act, split):
        for k in range(KT):
            act.wait_ge(self.evac, k + 1)
            act.activation(self.c.x_hi[:, k, :], self.c.xT[:, k, :], ACT.Copy).then_inc(self.hi, 1)
            if k >= KT - 3 and k < KT - 1:
                split(k - KT + 3)

    def pool(self, pool):
        c = self.c
        pool.wait_ge(self.const_in, 16)
        pool.tensor_copy(c.causal_bf[:, :], c.k("causal"))
        pool.tensor_copy(c.cmp_bf[:, :], c.k("cmp"))
        pool.tensor_copy(c.new_bf[:, :], c.k("new"))
        pool.tensor_scalar(c.ident_big[:, :], c.k("ident"), BIG, None, ALU.mult)

    def wait_tile(self, pe, k):
        pe.wait_ge(self.lo, k + 1)


class Norm:

    def __init__(self, c, sem, tmp, which):
        self.c, self.which = c, which
        sb = lambda n, s: tmp.enter_context(c.nc.sbuf_tensor(f"norm{which}_{n}", s, F32))
        self.sq, self.std, self.rstd, self.eps = sb("sq", [P, 2, T]), sb("std", [P, T]), sb("rstd", [P, T]), sb("eps", [P, 1])
        self.mean_done, self.centred, self.squared, self.var_done, self.rooted, self.inverted, self.scaled, self.eps_set = (
            sem(s) for s in ("mean_done", "centred", "squared", "var_done", "rooted", "inverted", "scaled", "eps_set"))
        self.hi, self.lo = sem("x_hi_set"), [sem("x_lo_set_dve"), sem("x_lo_set_pool")]
        self.done = sem("x_done")

    def sync(self, sp):
        pass

    sync_late = sync

    def pe(self, pe):
        c = self.c
        for h in range(2):
            last = pe.matmul(c.ps[:, 4 + h, 0:HALF], c.k("mean"), c.x_sum[:, h * HALF:(h + 1) * HALF], start=True, stop=True)
        last.then_inc(self.mean_done, 1)
        for k in range(KT):
            pe.wait_ge(self.squared, k + 1)
            for h in range(2):
                last = pe.matmul(c.ps[:, 6 + h, 0:HALF], c.k("mean"), self.sq[:, k % 2, h * HALF:(h + 1) * HALF],
                                 start=(k == 0), stop=(k == KT - 1))
            last.then_inc(self.var_done, 1)

    def dve(self, dve, split=None):
        c = self.c
        dve.memset(self.eps[:, :], EPS).then_inc(self.eps_set, 1)
        dve.wait_ge(self.mean_done, 1)
        for k in range(KT):
            dve.tensor_tensor(halves(c.xT[:, k, :]), halves(c.xT[:, k, :]), c.ps[:, 4:6, 0:HALF], ALU.subtract).then_inc(self.centred, 1)
        if split:
            split(0)
            split(1)
        dve.wait_ge(self.rooted, 1)
        dve.reciprocal(self.rstd[:, :], self.std[:, :]).then_inc(self.inverted, 1)
        dve.wait_ge(self.inverted, 1)
        dve.wait_ge(self.squared, KT)
        for k in range(KT):
            dve.scalar_tensor_tensor(c.xT[:, k, :], c.xT[:, k, :], c.ln_gb[:, self.which, 0, k:k + 1], self.rstd[:, :],
                                     ALU.mult, ALU.mult).then_inc(self.scaled, 1)
            if split and k >= 2 and k % 2 == 0:
                self.low(dve, k - 2)
        if split:
            self.low(dve, KT - 2)

    def low(self, dve, k):
        c = self.c
        dve.wait_ge(self.hi, k + 1)
        dve.scalar_tensor_tensor(c.x_lo[:, k, :], c.xT[:, k, :], c.ln_gb[:, self.which, 1, k:k + 1],
                                 c.x_hi[:, k, :].bitcast(F32), ALU.add, ALU.subtract).then_inc(self.lo[0], 1)

    def wait_tile(self, pe, k):
        pe.wait_ge(self.lo[k % 2], k // 2 + 1)

    def pool(self, pool):
        c = self.c
        for k in range(1, KT, 2):
            pool.wait_ge(self.done, k // 2 + 1)
            pool.tensor_tensor(c.x_lo[:, k, :], c.xT[:, k, :], c.x_hi[:, k, :].bitcast(F32), ALU.subtract).then_inc(self.lo[1], 1)

    def act(self, act, split=None):
        c = self.c
        for k in range(KT):
            act.wait_ge(self.centred, k + 1)
            if k >= 2:
                act.wait_ge(self.var_done, k - 1)
            act.activation(self.sq[:, k % 2, :], c.xT[:, k, :], ACT.Square).then_inc(self.squared, 1)
            if split and k in (4, 6):
                split((k - 4) // 2)
        act.wait_ge(self.var_done, KT)
        act.wait_ge(self.eps_set, 1)
        act.activation(halves(self.std[:, :]), c.ps[:, 6:8, 0:HALF], ACT.Sqrt, bias=self.eps[:, :]).then_inc(self.rooted, 1)
        shift = lambda out, k: act.activation(out, c.xT[:, k, :], ACT.Identity, bias=c.ln_gb[:, self.which, 1, k:k + 1])
        if split:
            for k in range(KT + 1):
                if k < KT:
                    act.wait_ge(self.scaled, k + 1)
                    shift(c.x_hi[:, k, :], k).then_inc(self.hi, 1)
                if k >= 2 and k % 2 == 0:
                    act.wait_ge(self.hi, k)
                    shift(c.xT[:, k - 1, :], k - 1).then_inc(self.done, 1)
            for k in range(0, KT, 2):
                self.wait_tile(act, k)
                shift(c.xT[:, k, :], k).then_inc(self.done, 1)
        else:
            for k in range(KT):
                act.wait_ge(self.scaled, k + 1)
                shift(c.xT[:, k, :], k).then_inc(self.done, 1)


def stage_in_proj(c, name, begin, w, rope_slabs, plain_slabs, projT):
    nc = c.nc
    block, sem = stage(c, name)
    slabs = rope_slabs + plain_slabs
    n_rope = len(rope_slabs)
    raw_loaded = [sem("raw0"), sem("raw1")]
    hi_made, lo_made, unit_used = sem("hi_made"), sem("lo_made"), sem("unit_used")
    swapped, cosed, sined, summed = sem("swapped"), sem("cosed"), sem("sined"), sem("summed")
    with ExitStack() as tmp:
        swap = tmp.enter_context(nc.sbuf_tensor(f"{name}_swap", [P, 2, T], F32))
        n_dma = [0, 0]
        loads = []
        for n, slab in enumerate(slabs):
            n_dma[n % 2] += len(slab)
            loads.append(16 * n_dma[n % 2])
        start = begin(sem, tmp)
        with block as blk:
            @blk.sync
            def _(sp):
                start.sync(sp)
                for n, slab in enumerate(slabs):
                    if n == 2:
                        start.sync_late(sp)
                    if n >= 2:
                        sp.wait_ge(hi_made, n - 1)
                        sp.wait_ge(lo_made, n - 1)
                    load_unit(c, sp, n % 2, slab_pieces(w, slab), raw_loaded[n % 2])

            @blk.gpsimd
            def _(pool):
                start.pool(pool)

            def psum_of(n):
                return c.ps[:, 2 * (n % 4):2 * (n % 4) + 2, 0:HALF]

            @blk.scalar
            def _(act):
                def hi(n):
                    act.wait_ge(raw_loaded[n % 2], loads[n])
                    if n >= 2:
                        act.wait_ge(unit_used, n - 1)
                    split_hi(c, act, n % 2, KT).then_inc(hi_made, 1)

                start.act(act, hi)
                for n in range(len(slabs)):
                    if 2 <= n + 1 < len(slabs):
                        hi(n + 1)
                    act.wait_ge(unit_used, n + 1)
                    if n < n_rope:
                        if n >= 2:
                            act.wait_ge(summed, n - 1)
                        for qd in range(4):
                            o = 32 * (qd ^ 1)
                            last = act.activation(halves(swap[32 * qd:32 * qd + 32, n % 2, :]),
                                                  psum_of(n)[o:o + 32], ACT.Copy)
                        last.then_inc(swapped, 1)
                    else:
                        act.activation(halves(projT[:, n, :]), psum_of(n), ACT.Copy).then_inc(swapped, 1)

            @blk.vector
            def _(dve):
                def lo(n):
                    dve.wait_ge(hi_made, n + 1)
                    split_lo(c, dve, n % 2, KT).then_inc(lo_made, 1)

                start.dve(dve, lo)
                for n in range(len(slabs)):
                    if 2 <= n + 1 < len(slabs):
                        lo(n + 1)
                    if n < n_rope:
                        dve.wait_ge(swapped, n + 1)
                        dve.tensor_tensor(halves(projT[:, n, :]), psum_of(n), halves(c.k("cos")), ALU.mult).then_inc(cosed, 1)
                        dve.tensor_tensor(swap[:, n % 2, :], swap[:, n % 2, :], c.k("sin"), ALU.mult).then_inc(sined, 1)
                        dve.wait_ge(cosed, n + 1)
                        dve.wait_ge(sined, n + 1)
                        dve.tensor_tensor(projT[:, n, :], projT[:, n, :], swap[:, n % 2, :], ALU.add).then_inc(summed, 1)

            @blk.tensor
            def _(pe):
                start.pe(pe)
                pe.wait_ge(lo_made, 1)
                pe_first_unit(c, pe, start).then_inc(unit_used, 1)
                for n in range(1, len(slabs)):
                    pe.wait_ge(lo_made, n + 1)
                    if n >= 4:
                        pe.wait_ge(swapped, n - 3)
                        pe.wait_ge(cosed, min(n - 3, n_rope))
                    pe_unit(c, pe, n % 2, KT, 0, c.x_hi, c.x_lo, 2 * (n % 4), True, True).then_inc(unit_used, 1)


def stage_out_proj(c, name, w, row_of):
    block, sem = stage(c, name)
    raw_loaded = [sem("raw0"), sem("raw1")]
    hi_made, lo_made, unit_used, added = sem("hi_made"), sem("lo_made"), sem("unit_used"), sem("added")
    x_summed = sem("x_summed")
    with block as blk:
        @blk.sync
        def _(sp):
            for n in range(2, KT):
                sp.wait_ge(hi_made, n - 1)
                sp.wait_ge(lo_made, n - 1)
                load_unit(c, sp, n % 2, row_of(w, slice(n * P, (n + 1) * P)), raw_loaded[n % 2])
        n_piece = len(row_of(w, slice(0, P)))

        @blk.scalar
        def _(act):
            act.sem_inc(hi_made, 2)
            for n in range(2, KT):
                act.wait_ge(raw_loaded[n % 2], 16 * n_piece * (n // 2))
                act.wait_ge(unit_used, n - 1)
                split_hi(c, act, n % 2, KT).then_inc(hi_made, 1)

        @blk.vector
        def _(dve):
            def lo(n):
                dve.wait_ge(hi_made, n + 1)
                split_lo(c, dve, n % 2, KT).then_inc(lo_made, 1)

            dve.sem_inc(lo_made, 2)
            for n in range(KT):
                if 2 <= n + 1 < KT:
                    lo(n + 1)
                dve.wait_ge(unit_used, n + 1)
                dve.scalar_tensor_tensor(halves(c.xT[:, n, :]), halves(c.xT[:, n, :]), ALPHA,
                                         c.ps[:, 2 * (n % 4):2 * (n % 4) + 2, 0:HALF], ALU.mult, ALU.add).then_inc(added, 1)

        @blk.gpsimd
        def _(pool):
            for n in range(KT):
                pool.wait_ge(added, n + 1)
                if n == 0:
                    pool.tensor_copy(c.x_sum[:, :], c.xT[:, 0, :]).then_inc(x_summed, 1)
                else:
                    pool.wait_ge(x_summed, n)
                    pool.tensor_tensor(c.x_sum[:, :], c.x_sum[:, :], c.xT[:, n, :], ALU.add).then_inc(x_summed, 1)

        @blk.tensor
        def _(pe):
            for n in range(KT):
                pe.wait_ge(lo_made, n + 1)
                if n >= 4:
                    pe.wait_ge(added, n - 3)
                pe_unit(c, pe, n % 2, KT, 0, c.x_hi, c.x_lo, 2 * (n % 4), True, True).then_inc(unit_used, 1)


def stage_ffn_up(c, layer, begin, h_hi, h_lo):
    nc = c.nc
    wg, wu = c.dram["ffn_w_gate"][layer], c.dram["ffn_w_up"][layer]
    block, sem = stage(c, "up")
    g_raw, u_raw = sem("gate_raw_in"), sem("up_raw_in")
    g_hi, u_hi, g_lo, u_lo = sem("gate_hi"), sem("up_hi"), sem("gate_lo"), sem("up_lo")
    g_used, u_used = sem("gate_used"), sem("up_used")
    ahead = Ahead(c, sem, [(down_pieces(c.dram["ffn_w_down"][layer], s, slice(0, P)), KCH) for s in range(2)])
    silu, prod, h_top, h_rest = sem("silu"), sem("prod"), sem("h_top"), sem("h_rest")
    with ExitStack() as tmp:
        act_g = tmp.enter_context(nc.sbuf_tensor(f"silu{layer}", [P, T], F32))
        h_f = tmp.enter_context(nc.sbuf_tensor(f"h_f{layer}", [P, T], F32))
        start = begin(sem, tmp)
        with block as blk:
            @blk.sync
            def _(sp):
                start.sync(sp)
                load_unit(c, sp, 0, up_pieces(wg, slice(0, P)), g_raw)
                load_unit(c, sp, 1, up_pieces(wu, slice(0, P)), u_raw)
                with sp.Fori(1, FT) as f:
                    cols = bass.ds(f * P, P)
                    sp.wait_ge(g_lo, f)
                    load_unit(c, sp, 0, up_pieces(wg, cols), g_raw)
                    sp.wait_ge(u_lo, f)
                    load_unit(c, sp, 1, up_pieces(wu, cols), u_raw)
                sp.wait_ge(g_lo, FT)
                sp.wait_ge(u_lo, FT)
                ahead.load(sp)

            @blk.scalar
            def _(act):
                def gate_hi(f, first=False):
                    act.wait_ge(g_raw, 16 * f + 16)
                    if not first:
                        act.wait_ge(g_used, f)
                    split_hi(c, act, 0, KT).then_inc(g_hi, 1)

                def up_hi(f, first=False):
                    act.wait_ge(u_raw, 16 * f + 16)
                    if not first:
                        act.wait_ge(u_used, f)
                    split_hi(c, act, 1, KT).then_inc(u_hi, 1)

                def gate_act(f, first=False):
                    act.wait_ge(g_used, f + 1)
                    if not first:
                        act.wait_ge(prod, f)
                    act.activation(halves(act_g[:, :]), c.ps[:, 0:2, 0:HALF], ACT.Silu).then_inc(silu, 1)

                def top(f):
                    act.wait_ge(prod, f + 1)
                    act.activation(h_hi[:, bass.ds(f, 1), :], h_f[:, :].rearrange("p (a n) -> p a n", a=1),
                                   ACT.Copy).then_inc(h_top, 1)

                start.act(act, lambda n: (gate_hi, up_hi)[n](0, True))
                gate_hi(1)
                gate_act(0, True)
                up_hi(1)
                top(0)
                with act.Fori(1, FT - 1) as f:
                    gate_hi(f + 1)
                    gate_act(f)
                    up_hi(f + 1)
                    top(f)
                gate_act(FT - 1)
                ahead.split_hi(act, 0)
                top(FT - 1)
                ahead.split_hi(act, 1)

            @blk.vector
            def _(dve):
                def gate_lo(f):
                    dve.wait_ge(g_hi, f + 1)
                    split_lo(c, dve, 0, KT).then_inc(g_lo, 1)

                def up_lo(f):
                    dve.wait_ge(u_hi, f + 1)
                    split_lo(c, dve, 1, KT).then_inc(u_lo, 1)

                def mul(f, first=False):
                    if not first:
                        dve.wait_ge(h_rest, f)
                    dve.wait_ge(silu, f + 1)
                    dve.wait_ge(u_used, f + 1)
                    dve.tensor_tensor(halves(h_f[:, :]), halves(act_g[:, :]), c.ps[:, 2:4, 0:HALF], ALU.mult).then_inc(prod, 1)

                def low(f):
                    dve.wait_ge(h_top, f + 1)
                    at = bass.ds(f, 1)
                    dve.tensor_tensor(h_lo[:, at, :], h_f[:, :].rearrange("p (a n) -> p a n", a=1),
                                      h_hi[:, at, :].bitcast(F32), ALU.subtract).then_inc(h_rest, 1)

                start.dve(dve, lambda n: (gate_lo, up_lo)[n](0))

                def tile(f, first=False):
                    gate_lo(f + 1)
                    mul(f, first)
                    up_lo(f + 1)
                    low(f)

                tile(0, True)
                with dve.Fori(1, FT - 1) as f:
                    tile(f)
                ahead.split_lo(dve, 0)
                mul(FT - 1)
                low(FT - 1)
                ahead.split_lo(dve, 1)

            @blk.gpsimd
            def _(pool):
                start.pool(pool)

            @blk.tensor
            def _(pe):
                def tile(f, first=False):
                    pe.wait_ge(g_lo, f + 1)
                    if first:
                        pe_first_unit(c, pe, start).then_inc(g_used, 1)
                    else:
                        pe.wait_ge(silu, f)
                        pe_unit(c, pe, 0, KT, 0, c.x_hi, c.x_lo, 0, True, True).then_inc(g_used, 1)
                    pe.wait_ge(u_lo, f + 1)
                    if not first:
                        pe.wait_ge(prod, f)
                    pe_unit(c, pe, 1, KT, 0, c.x_hi, c.x_lo, 2, True, True).then_inc(u_used, 1)

                start.pe(pe)
                tile(0, True)
                with pe.Fori(1, FT) as f:
                    tile(f)


def stage_ffn_down(c, layer, h_hi, h_lo):
    wd = c.dram["ffn_w_down"][layer]
    block, sem = stage(c, "down")
    raw = [sem("raw_a_in"), sem("raw_b_in")]
    hi = [sem("hi_a"), sem("hi_b")]
    lo = [sem("lo_a"), sem("lo_b")]
    used = [sem("used_a"), sem("used_b")]
    added, x_summed = sem("added"), sem("x_summed")
    with block as blk:
        @blk.gpsimd
        def _(pool):
            pool.wait_ge(added, 1)
            pool.tensor_copy(c.x_sum[:, :], c.xT[:, 0, :]).then_inc(x_summed, 1)
            with pool.Fori(1, KT) as n:
                pool.wait_ge(added, n + 1)
                pool.wait_ge(x_summed, n)
                line = c.x_sum[:, :].rearrange("p (a n) -> p a n", a=1)
                pool.tensor_tensor(line, line, c.xT[:, bass.ds(n, 1), :], ALU.add).then_inc(x_summed, 1)

        @blk.sync
        def _(sp):
            with sp.Fori(1, KT) as n:
                for s in range(2):
                    sp.wait_ge(lo[s], n)
                    load_unit(c, sp, s, down_pieces(wd, s, bass.ds(n * P, P)), raw[s])

        @blk.scalar
        def _(act):
            act.sem_inc(hi[0], 1)
            act.sem_inc(hi[1], 1)
            with act.Fori(1, KT) as n:
                for s in range(2):
                    act.wait_ge(raw[s], 16 * n)
                    act.wait_ge(used[s], n)
                    split_hi(c, act, s, KCH).then_inc(hi[s], 1)

        @blk.vector
        def _(dve):
            def split(n, s):
                dve.wait_ge(hi[s], n + 1)
                split_lo(c, dve, s, KCH).then_inc(lo[s], 1)

            def add(n, bank):
                dve.wait_ge(used[1], n + 1)
                at = bass.ds(n, 1)
                x = c.xT[:, at, :].rearrange("p a (h n) -> p (a h) n", h=2)
                dve.scalar_tensor_tensor(x, x, ALPHA, c.ps[:, bank:bank + 2, 0:HALF], ALU.mult, ALU.add).then_inc(added, 1)

            dve.sem_inc(lo[0], 1)
            dve.sem_inc(lo[1], 1)

            def pair(n):
                for j in range(2):
                    split(n + j + 1, 0)
                    split(n + j + 1, 1)
                    add(n + j, 2 * j)

            with dve.Fori(0, KT - 2, 2) as n:
                pair(n)
            split(KT - 1, 0)
            split(KT - 1, 1)
            add(KT - 2, 0)
            add(KT - 1, 2)

        @blk.tensor
        def _(pe):
            def tile(n, bank, first=False):
                pe.wait_ge(lo[0], n + 1)
                if not first:
                    pe.wait_ge(added, n - 1)
                pe_unit(c, pe, 0, KCH, 0, h_hi, h_lo, bank, True, False).then_inc(used[0], 1)
                pe.wait_ge(lo[1], n + 1)
                pe_unit(c, pe, 1, KCH, KCH, h_hi, h_lo, bank, False, True).then_inc(used[1], 1)
            tile(0, 0, True)
            tile(1, 2, True)
            with pe.Fori(2, KT, 2) as n:
                tile(n, 0)
                tile(n + 1, 2)


def stage_store(c, begin):
    nc = c.nc
    block, sem = stage(c, "store")
    turned, evac, evac_s, out = sem("turned"), sem("evac"), sem("evac_s"), sem("out")
    with ExitStack() as tmp:
        y = tmp.enter_context(nc.sbuf_tensor("y_nat", [P, NB + 1, D], F32))
        start = begin(sem, tmp)
        with block as blk:
            @blk.tensor
            def _(pe):
                start.pe(pe)
                for k in range(KT):
                    pe.wait_ge(start.done, k + 1)
                    if k >= 2:
                        pe.wait_ge(evac, k - 1)
                        pe.wait_ge(evac_s, k - 1)
                    b0 = 2 * (k % 2)
                    for b in range(NB):
                        pe.transpose(c.ps[:, b0, b * P:(b + 1) * P], c.xT[:, k, b * P:(b + 1) * P], c.k("ident"))
                    pe.transpose(c.ps[0:TS, b0 + 1, 0:P], c.xT[:, k, SEQ:T], c.k("ident")).then_inc(turned, 1)

            @blk.vector
            def _(dve):
                start.dve(dve)
                for k in range(KT):
                    dve.wait_ge(turned, k + 1)
                    dve.tensor_copy(y[:, 0:NB, k * P:(k + 1) * P], c.ps[:, 2 * (k % 2), :].rearrange("p (b n) -> p b n", b=NB)).then_inc(evac, 1)

            @blk.scalar
            def _(act):
                start.act(act)
                for k in range(KT):
                    act.wait_ge(turned, k + 1)
                    act.activation(y[0:TS, NB, k * P:(k + 1) * P], c.ps[0:TS, 2 * (k % 2) + 1, 0:P], ACT.Copy).then_inc(evac_s, 1)

            @blk.sync
            def _(sp):
                for i in range(KT // 2):
                    cols = slice(2 * i * P, 2 * (i + 1) * P)
                    sp.wait_ge(evac, 2 * i + 2)
                    sp.dma_start(c.dram["y_prompt"][0][:, cols].rearrange("(b p) d -> p b d", p=P), y[:, 0:NB, cols]).then_inc(out, 16)
                    sp.wait_ge(evac_s, 2 * i + 2)
                    sp.dma_start(c.dram["y_sample"].rearrange("b t d -> (b t) d")[:, cols], y[0:TS, NB, cols]).then_inc(out, 16)
                sp.wait_ge(out, 16 * KT)



def stage_rows(c, name, projT, items):
    nc = c.nc
    block, sem = stage(c, name)
    turned, evac_p, evac_s = sem("turned"), sem("evac_p"), sem("evac_s")
    n_ring = min(4, len(items))
    out = [sem(f"out{i}") for i in range(n_ring)]
    with ExitStack() as tmp:
        ring = tmp.enter_context(nc.sbuf_tensor(f"{name}_rows", [P, n_ring, NB + 1, P], F32))
        dst = [ring[:, n % n_ring] if keep is None else keep for n, (_, keep, _) in enumerate(items)]
        sent, before = [0] * n_ring, []
        for n, (_, _, stores) in enumerate(items):
            before.append(sent[n % n_ring])
            sent[n % n_ring] += 32 * len(stores)
        with block as blk:
            @blk.tensor
            def _(pe):
                for n, (slab, _, _) in enumerate(items):
                    if n >= 3:
                        pe.wait_ge(evac_p, n - 2)
                        pe.wait_ge(evac_s, n - 2)
                    bank = 2 * (n % 3)
                    for b in range(NB):
                        pe.transpose(c.ps[:, bank, b * P:(b + 1) * P], projT[:, slab, b * P:(b + 1) * P], c.k("ident"))
                    pe.transpose(c.ps[0:TS, bank + 1, 0:P], projT[:, slab, SEQ:T], c.k("ident")).then_inc(turned, 1)

            @blk.vector
            def _(dve):
                for n in range(len(items)):
                    dve.wait_ge(turned, n + 1)
                    if n >= n_ring and before[n]:
                        dve.wait_ge(out[n % n_ring], before[n])
                    dve.tensor_copy(dst[n][:, 0:NB, :], c.ps[:, 2 * (n % 3), :].rearrange("p (b n) -> p b n", b=NB)).then_inc(evac_p, 1)

            @blk.scalar
            def _(act):
                for n in range(len(items)):
                    act.wait_ge(turned, n + 1)
                    if n >= n_ring and before[n]:
                        act.wait_ge(out[n % n_ring], before[n])
                    act.activation(dst[n][0:TS, NB, :], c.ps[0:TS, 2 * (n % 3) + 1, 0:P], ACT.Copy).then_inc(evac_s, 1)

            @blk.sync
            def _(sp):
                for n, (_, _, stores) in enumerate(items):
                    if stores:
                        sp.wait_ge(evac_p, n + 1)
                        sp.wait_ge(evac_s, n + 1)
                    for col, prompt, sample in stores:
                        w = prompt.shape[-1]
                        sp.dma_start(prompt.rearrange("(b p) n -> p b n", p=P), dst[n][:, 0:NB, col:col + w]).then_inc(out[n % n_ring], 16)
                        sp.dma_start(sample, dst[n][0:TS, NB, col:col + w]).then_inc(out[n % n_ring], 16)
                for s in range(n_ring):
                    if sent[s]:
                        sp.wait_ge(out[s], sent[s])


def stage_pages(c, name, seqs, turn, copy):
    nc = c.nc
    block, sem = stage(c, name)
    table_in, rest_in, turned = (sem(s) for s in ("table_in", "rest_in", "turned"))
    evac = [sem("evac_dve"), sem("evac_act")]
    pages = [(b, g) for b in seqs for g in range(NPAGE)]
    n_turn = len(turn)
    steps = [(i, b, g, t) for i, (b, g) in enumerate(pages) for t in range(n_turn)]
    land = [sem(f"land{i}") for i in range(4)]
    with ExitStack() as tmp:
        table = tmp.enter_context(nc.sbuf_tensor(f"{name}_table", [1, DEC_B * NPAGE], I32))
        ring = tmp.enter_context(nc.sbuf_tensor(f"{name}_ring", [P, 4, 2 * P], F32))
        loads, count = [], [0] * 4
        for n, (_, _, _, t) in enumerate(steps):
            count[n % 4] += 16 * len(turn[t][1])
            loads.append(count[n % 4])
        with block as blk:
            @blk.sync
            def _(sp):
                sp.dma_start(table[:, :], c.dram["page_table"].rearrange("(a b) g -> a (b g)", a=1)).then_inc(table_in, 16)
                sp.wait_ge(table_in, 16)
                n = n_rest = 0
                n_pool = c.dram["cache_a_k"].shape[1]
                for i, (b, g) in enumerate(pages):
                    page = sp.value_load(table[0:1, b * NPAGE + g:b * NPAGE + g + 1], min_val=0, max_val=n_pool - 1)
                    for t, (src, places, _) in enumerate(turn):
                        if n >= 4:
                            sp.wait_ge(turned, n - 3)
                        for col, w in places:
                            sp.dma_start(ring[:, n % 4, col:col + w], src(page)).then_inc(land[n % 4], 16)
                        n += 1
                    for src, dst in copy:
                        sp.dma_start(dst(b, g), src(b, g, page)).then_inc(rest_in, 16)
                        n_rest += 1
                sp.wait_ge(rest_in, 16 * n_rest) if n_rest else None

            @blk.tensor
            def _(pe):
                for n, (i, b, g, t) in enumerate(steps):
                    if n >= 4:
                        pe.wait_ge(evac[n % 2], (n - 4) // 2 + 1)
                    pe.wait_ge(land[n % 4], loads[n])
                    wide = sum(w for _, w in turn[t][1])
                    for h in range(wide // P):
                        last = pe.transpose(c.ps[:, n % 4, h * P:(h + 1) * P], ring[:, n % 4, h * P:(h + 1) * P], c.k("ident"))
                    last.then_inc(turned, 1)

            def move(eng, n):
                i, b, g, t = steps[n]
                wide = sum(w for _, w in turn[t][1])
                src = c.ps[:, n % 4, 0:wide].rearrange("p (h n) -> p h n", n=P)
                dst = turn[t][2][:, :, seqs.index(b), g * PAGE:(g + 1) * PAGE]
                eng.wait_ge(turned, n + 1)
                return dst, src

            @blk.vector
            def _(dve):
                for n in range(0, len(steps), 2):
                    dst, src = move(dve, n)
                    dve.tensor_copy(dst, src).then_inc(evac[0], 1)

            @blk.scalar
            def _(act):
                for n in range(1, len(steps), 2):
                    dst, src = move(act, n)
                    act.activation(dst, src, ACT.Copy).then_inc(evac[1], 1)



class Tile:

    def __init__(self, scores, biases, n_keys, values, mover):
        self.scores, self.biases, self.n_keys, self.values, self.mover = scores, biases, n_keys, values, mover
        self.chunks = [(c0, min(P, n_keys - c0)) for c0 in range(0, n_keys, P)]


class Group:

    def __init__(self, tiles, n_seg, n_br, gate, leaves):
        self.tiles, self.n_seg, self.n_br, self.gate, self.leaves = tiles, n_seg, n_br, gate, leaves


TURN = 3
VALUE = 5
S_RING, P_RING, PT_RING = 3, 4, 3


def stage_attend(c, name, groups, ahead_units=None, beside=None):
    nc = c.nc
    block, sem = stage(c, name)
    scored, peaked, scaled, exped, turned, valued = (sem(s) for s in
        ("scored", "peaked", "scaled", "exped", "turned", "valued"))
    moved = {"act": sem("moved_act"), "dve": sem("moved_dve")}
    guarded, inverted, weighed, mixing, mixed, back, top, rest = (sem(s) for s in
        ("guarded", "inverted", "weighed", "mixing", "mixed", "back", "top", "rest"))
    ahead = Ahead(c, sem, ahead_units) if ahead_units else None
    tiles = [t for g in groups for t in g.tiles]
    group_of = [g for g, x in enumerate(groups) for _ in x.tiles]
    last_of = [max(j for j, x in enumerate(group_of) if x == g) for g in range(len(groups))]
    n_t, per = len(tiles), len(groups[0].tiles)
    n_steps = n_t + VALUE + 5
    S = lambda j: c.ps[:, j % S_RING, :]
    TB = lambda j: c.ps[:, 3 + j % 2, :]
    OB = lambda g: c.ps[:, 5 + g % 2, :]
    BACK = c.ps[:, 7, 0:P]

    def wait_moved(eng, j):
        who = tiles[j].mover
        eng.wait_ge(moved[who], sum(t.mover == who for t in tiles[:j + 1]))

    def groups_at(j, lag):
        return [g for g in range(len(groups)) if last_of[g] == j - lag]

    with ExitStack() as tmp:
        sb = lambda n, s: tmp.enter_context(nc.sbuf_tensor(f"{name}_{n}", s, F32))
        prob = sb("prob", [P, P_RING, max(t.n_keys for t in tiles)])
        probT = sb("probT", [P, PT_RING, max(len(t.chunks) for t in tiles), P])
        peak, shift, total, total1, inv, weight = (sb(n, [P, n_t]) for n in
            ("peak", "shift", "total", "total1", "inv", "weight"))
        rows = sb("rows", [P, 2, P])
        with block as blk:
            if ahead:
                @blk.sync
                def _(sp):
                    ahead.load(sp)

            @blk.tensor
            def _(pe):
                def scores(j):
                    t = tiles[j]
                    if j >= S_RING:
                        pe.wait_ge(exped, j - S_RING + 1)
                    mm = t.scores + [(0, P, c0, n, c.ident_big[:, :], rhs) for c0, n, rhs in t.biases]
                    opened = set()
                    for i, (p0, p1, c0, n, lhsT, rhs) in enumerate(mm):
                        last = pe.matmul(S(j)[p0:p1, c0:c0 + n], lhsT, rhs, start=p0 not in opened,
                                         stop=i == len(mm) - 1, skip_group_check=True)
                        opened |= set(range(p0, p1, 32))
                    last.then_inc(scored, 1)

                def turn(j):
                    pe.wait_ge(exped, j + 1)
                    if j >= 2:
                        wait_moved(pe, j - 2)
                    for i, (c0, n) in enumerate(tiles[j].chunks):
                        last = pe.transpose(TB(j)[0:n, i * P:(i + 1) * P], prob[:, j % P_RING, c0:c0 + n], c.k("ident"))
                    last.then_inc(turned, 1)

                def values(j):
                    t, g = tiles[j], group_of[j]
                    wait_moved(pe, j)
                    if g >= 2 and group_of[j - 1] != g:
                        pe.wait_ge(mixed, g - 1)
                    for p0, p1, c0, n, who, chunk, rhs, start, stop in t.values:
                        keys = t.chunks[chunk][1]
                        last = pe.matmul(OB(g)[p0:p1, c0:c0 + n], probT[0:keys, j % PT_RING, chunk, who], rhs,
                                         start=start, stop=stop, skip_group_check=True)
                    last.then_inc(valued, 1)

                for j in range(n_steps):
                    if j < n_t:
                        scores(j)
                    if 0 <= j - TURN < n_t:
                        turn(j - TURN)
                    if 0 <= j - VALUE < n_t:
                        values(j - VALUE)
                    for g in groups_at(j, VALUE + 2):
                        pe.wait_ge(mixed, g + 1)
                        if g:
                            pe.wait_ge(rest, g)
                        pe.transpose(BACK, rows[:, g % 2, :], c.k("ident")).then_inc(back, 1)

            def full_and_part(t):
                full = sum(n == P for _, n in t.chunks)
                return full, (t.chunks[full][1] if full < len(t.chunks) else 0)

            def move(eng, copy, j):
                t = tiles[j]
                eng.wait_ge(turned, j + 1)
                if j >= PT_RING:
                    eng.wait_ge(valued, j - PT_RING + 1)
                full, n = full_and_part(t)
                if full:
                    last = copy(probT[:, j % PT_RING, 0:full, :], TB(j)[:, 0:full * P].rearrange("p (k n) -> p k n", n=P))
                if n:
                    last = copy(probT[0:n, j % PT_RING, full, :], TB(j)[0:n, full * P:(full + 1) * P])
                last.then_inc(moved[t.mover], 1)

            @blk.vector
            def _(dve):
                if ahead:
                    ahead.split_lo(dve, 0)
                    ahead.split_lo(dve, 1)
                n_mix = 0
                for j in range(n_steps):
                    if j < n_t:
                        dve.wait_ge(scored, j + 1)
                        dve.tensor_reduce(peak[:, j:j + 1], S(j)[:, 0:tiles[j].n_keys], AX_X, ALU.max, negate=True).then_inc(peaked, 1)
                        dve.wait_ge(peaked, j + 1)
                        dve.tensor_scalar(shift[:, j:j + 1], peak[:, j:j + 1], BIG / 10, SCALE, ALU.min, ALU.mult).then_inc(scaled, 1)
                    if 0 <= j - TURN < n_t and tiles[j - TURN].mover == "dve":
                        move(dve, dve.tensor_copy, j - TURN)
                    for g in groups_at(j, 2):
                        dve.wait_ge(exped, last_of[g] + 1)
                        at = slice(g * per, (g + 1) * per)
                        dve.tensor_scalar(total1[:, at], total[:, at], 0.5, None, ALU.max).then_inc(guarded, 1)
                        dve.wait_ge(guarded, g + 1)
                        dve.reciprocal(inv[:, at], total1[:, at]).then_inc(inverted, 1)
                        if groups[g].gate is not None:
                            dve.wait_ge(inverted, g + 1)
                            view = lambda x: x[:, at].rearrange("p (s a) -> p s a", s=groups[g].n_seg)
                            dve.tensor_tensor(view(weight), view(inv), groups[g].gate, ALU.mult).then_inc(weighed, 1)
                    for g in groups_at(j, VALUE + 1):
                        x = groups[g]
                        w = inv if x.gate is None else weight
                        dve.wait_ge(inverted if x.gate is None else weighed, g + 1)
                        dve.wait_ge(valued, last_of[g] + 1)
                        if g >= 2:
                            dve.wait_ge(back, g - 1)
                        width = P // x.n_seg
                        for a in range(x.n_br):
                            if a:
                                dve.wait_ge(mixing, n_mix)
                            for s in range(x.n_seg):
                                o = OB(g)[:, (s * x.n_br + a) * width:(s * x.n_br + a + 1) * width]
                                r = rows[:, g % 2, s * width:(s + 1) * width]
                                f = w[:, g * per + s * x.n_br + a:g * per + s * x.n_br + a + 1]
                                if a == 0:
                                    last = dve.tensor_scalar(r, o, f, None, ALU.mult)
                                else:
                                    last = dve.scalar_tensor_tensor(r, o, f, r, ALU.mult, ALU.add)
                                if a < x.n_br - 1:
                                    last.then_inc(mixing, 1)
                                    n_mix += 1
                        last.then_inc(mixed, 1)
                    for g in groups_at(j, VALUE + 4):
                        dve.wait_ge(top, g + 1)
                        for place, part in groups[g].leaves:
                            last = dve.tensor_tensor(place(c.x_lo), part(BACK), place(c.x_hi).bitcast(F32), ALU.subtract)
                        last.then_inc(rest, 1)

            if beside:
                @blk.gpsimd
                def _(pool):
                    beside(pool)

            @blk.scalar
            def _(act):
                copy = lambda out, in_: act.activation(out, in_, ACT.Copy)
                if ahead:
                    ahead.split_hi(act, 0)
                    ahead.split_hi(act, 1)
                for j in range(n_steps):
                    if j < n_t:
                        act.wait_ge(scaled, j + 1)
                        if j >= P_RING:
                            act.wait_ge(turned, j - P_RING + 1)
                        n = tiles[j].n_keys
                        act.activation(prob[:, j % P_RING, 0:n], S(j)[:, 0:n], ACT.Exp, bias=shift[:, j:j + 1],
                                       scale=SCALE, accum_out=total[:, j:j + 1]).then_inc(exped, 1)
                    if 0 <= j - TURN < n_t and tiles[j - TURN].mover == "act":
                        move(act, copy, j - TURN)
                    for g in groups_at(j, VALUE + 3):
                        act.wait_ge(back, g + 1)
                        for place, part in groups[g].leaves:
                            last = copy(place(c.x_hi), part(BACK))
                        last.then_inc(top, 1)


class Stack:

    def __init__(self):
        self.hi, self.lo = [], []

    def queries(self, side, src, dst):
        own, other = rows_of(side), rows_of(1 - side)
        self.hi.append((dst[own], src))
        self.lo.append((dst[other], src, dst[own], len(self.hi)))

    def keys(self, side, src, hi, lo):
        own, other = rows_of(side), rows_of(1 - side)
        self.hi += [(hi[own], src), (hi[other], src)]
        self.lo += [(part, src, hi[own], len(self.hi)) for part in (lo[own], lo[other])]

    def fill_hi(self, copy, made, a, b):
        for dst, src in self.hi[a:b]:
            copy(dst, src).then_inc(made, 1)

    def fill_lo(self, eng, made, a, b, done=None):
        for dst, src, hi, n in self.lo[a:b]:
            eng.wait_ge(made, n)
            ins = eng.tensor_tensor(dst, src, hi.bitcast(F32), ALU.subtract)
            if done:
                ins.then_inc(done, 1)


def rows_of(side):
    return slice(side * HD, side * HD + HD)


def idle_slots(c):
    lines = [w[:, :, :, :].rearrange("p s k n -> p (s k n)") for w in (c.w_hi, c.w_lo)]
    return [line[:, e * SEQ:(e + 1) * SEQ] for line in lines for e in range(2 * KCH * P // SEQ)]


class Rows:

    def __init__(self, n, side, q, keys, bias, values, gate, group, mover, first, last):
        self.n, self.side, self.q, self.keys, self.bias, self.values = n, side, q, keys, bias, values
        self.gate, self.group, self.mover, self.first, self.last = gate, group, mover, first, last
        self.wide = n
        self.short = None
        self.n_chunk = n // P


class Short:

    def __init__(self, heads, bias, gate):
        self.heads, self.bias, self.gate, self.mover = heads, bias, gate, "act"
        self.wide, self.n_chunk = 8 * 32, 2


TURN_P = 3
VALUE_P = 5


def stage_attend_prompt(c, name, tiles, leaf, n_groups, late=None):
    nc = c.nc
    block, sem = stage(c, name)
    scored, peaked, scaled, exped, inverted, normed, turned, valued = (sem(s) for s in
        ("scored", "peaked", "scaled", "exped", "inverted", "normed", "turned", "valued"))
    moved = {"act": sem("moved_act"), "dve": sem("moved_dve")}
    top, rest, link, stacked, late_set = sem("top"), sem("rest"), sem("link"), sem("stacked"), sem("late_set")
    n_t, n_prob, n_probT = len(tiles), 5, 3
    shorts = [j for j, t in enumerate(tiles) if isinstance(t, Short)]
    group_end = [max(j for j, t in enumerate(tiles) if j not in shorts and t.group == g) for g in range(n_groups)]
    S = lambda j: c.ps[:, j % 4, :]
    TB = lambda j: c.ps[:, 4 + j % 2, :]
    OB = lambda g: c.ps[:, 6 + g % 2, 0:P]
    LAG = 2

    def wait_moved(eng, j):
        who = tiles[j].mover
        eng.wait_ge(moved[who], sum(t.mover == who for t in tiles[:j + 1]))

    def through(j):
        return sum(i not in shorts for i in range(j + 1))

    with ExitStack() as tmp:
        sb = lambda n, s: tmp.enter_context(nc.sbuf_tensor(f"{name}_{n}", s, F32))
        prob = sb("prob", [P, n_prob, SEQ])
        probT = sb("probT", [P, n_probT, NB, P])
        peak, shift, total, inv = (sb(n, [P, n_t]) for n in ("peak", "shift", "total", "inv"))
        if shorts:
            shortT = sb("shortT", [P, 2, 2, P])
            peak8, total8, inv8 = (sb(n, [P, 2, 8]) for n in ("peak8", "total8", "inv8"))
        by_head = lambda x: x.rearrange("p (h n) -> p h n", n=32)
        spread = lambda x: x.rearrange("p (h a) -> p h a", a=1).broadcast_to([P, 8, 32])
        with block as blk:
            @blk.tensor
            def _(pe):
                def scores(j):
                    t = tiles[j]
                    if j >= 4:
                        pe.wait_ge(scaled if j - 4 in shorts else exped, j - 3)
                    if late and j == n_t // 2:
                        pe.wait_ge(late_set, len(late.lo))
                    if j in shorts:
                        for h, (q, hi, lo) in enumerate(t.heads):
                            o = S(j)[:, 32 * h:32 * h + 32]
                            pe.matmul(o, q, hi, start=h == 0, stop=False, skip_group_check=True)
                            pe.matmul(o, q, lo, start=False, stop=False, skip_group_check=True)
                        last = pe.matmul(by_head(S(j)[:, 0:256]), c.ident_big[:, :], t.bias, start=False, stop=True,
                                         skip_group_check=True)
                    else:
                        n = max(t.n, 2 * P)
                        pe.matmul(S(j)[:, 0:n], t.q, t.keys[0][:, 0:n], start=True, stop=False, skip_group_check=True)
                        pe.matmul(S(j)[:, 0:n], t.q, t.keys[1][:, 0:n], start=False, stop=False, skip_group_check=True)
                        c0, w, rhs = t.bias
                        last = pe.matmul(S(j)[:, c0:c0 + w], c.ident_big[:, :], rhs, start=False, stop=True,
                                         skip_group_check=True)
                    last.then_inc(scored, 1)

                def turn(j):
                    pe.wait_ge(normed, j + 1)
                    if j >= 2:
                        wait_moved(pe, j - 2)
                    for i in range(tiles[j].n_chunk):
                        last = pe.transpose(TB(j)[:, i * P:(i + 1) * P], prob[:, j % n_prob, i * P:(i + 1) * P], c.k("ident"))
                    last.then_inc(turned, 1)

                def values(j):
                    wait_moved(pe, j)
                    if j in shorts:
                        return
                    t = tiles[j]
                    if t.group >= 2 and j and (j - 1 in shorts or tiles[j - 1].group != t.group):
                        pe.wait_ge(rest, t.group - 1)
                        pe.wait_ge(top, t.group - 1)
                    out = OB(t.group)[rows_of(t.side)]
                    products = [(lhsT, probT[:, j % n_probT, k, :]) for k, lhsT in t.values]
                    if t.short:
                        n, chunk, part, lhsT = t.short
                        products = [(lhsT, shortT[part, n % 2, chunk, :])] + products
                    for i, (lhsT, rhs) in enumerate(products):
                        last = pe.matmul(out, lhsT, rhs, start=t.first and i == 0,
                                         stop=t.last and i == len(products) - 1, skip_group_check=True)
                    last.then_inc(valued, 1)

                for j in range(n_t + VALUE_P):
                    if j < n_t:
                        scores(j)
                    if 0 <= j - TURN_P < n_t:
                        turn(j - TURN_P)
                    if j >= VALUE_P:
                        values(j - VALUE_P)

            def move(eng, copy, j):
                t = tiles[j]
                eng.wait_ge(turned, j + 1)
                if j in shorts:
                    n = shorts.index(j)
                    if n >= 2:
                        eng.wait_ge(valued, through(shorts[n - 1] - 1))
                    dst = shortT[:, n % 2]
                else:
                    if j >= n_probT and through(j - n_probT):
                        eng.wait_ge(valued, through(j - n_probT))
                    dst = probT[:, j % n_probT, 0:t.n_chunk, :]
                copy(dst, TB(j)[:, 0:t.n_chunk * P].rearrange("p (k n) -> p k n", n=P)).then_inc(moved[t.mover], 1)

            @blk.vector
            def _(dve):
                linked = Linked(dve, link)

                def peaks(j):
                    t = tiles[j]
                    dve.wait_ge(scored, j + 1)
                    if j in shorts:
                        n = shorts.index(j)
                        linked(dve.tensor_reduce(peak8[:, n % 2, :], by_head(S(j)[:, 0:256]), AX_X, ALU.max, negate=True))
                        linked(dve.tensor_scalar(peak8[:, n % 2, :], peak8[:, n % 2, :], BIG / 10, None, ALU.min))
                        if j >= n_prob:
                            dve.wait_ge(turned, j - n_prob + 1)
                        dve.tensor_tensor(by_head(prob[:, j % n_prob, 0:256]), by_head(S(j)[:, 0:256]),
                                          spread(peak8[:, n % 2, :]), ALU.add).then_inc(scaled, 1)
                    else:
                        dve.tensor_reduce(peak[:, j:j + 1], S(j)[:, 0:t.n], AX_X, ALU.max, negate=True).then_inc(peaked, 1)

                def shifts(j):
                    if j not in shorts:
                        dve.wait_ge(peaked, j + 1 - sum(i <= j for i in shorts))
                        dve.tensor_scalar(shift[:, j:j + 1], peak[:, j:j + 1], SCALE, None, ALU.mult).then_inc(scaled, 1)

                def invert(j):
                    dve.wait_ge(exped, j + 1)
                    if j in shorts:
                        n = shorts.index(j)
                        linked(dve.reduce_sum(total8[:, n % 2, :], by_head(prob[:, j % n_prob, 0:256]), AX_X))
                        linked(dve.tensor_scalar(total8[:, n % 2, :], total8[:, n % 2, :], 0.5, None, ALU.max))
                        linked(dve.reciprocal(inv8[:, n % 2, :], total8[:, n % 2, :]))
                        dve.tensor_tensor(inv8[:, n % 2, :].rearrange("p (s h) -> p s h", s=2),
                                          inv8[:, n % 2, :].rearrange("p (s h) -> p s h", s=2), tiles[j].gate, ALU.mult).then_inc(inverted, 1)
                    else:
                        dve.reciprocal(inv[:, j:j + 1], total[:, j:j + 1]).then_inc(inverted, 1)

                done = 0
                for j in range(n_t + VALUE_P + 2):
                    if j < n_t:
                        peaks(j)
                    if 0 <= j - TURN_P < n_t and tiles[j - TURN_P].mover == "dve":
                        move(dve, dve.tensor_copy, j - TURN_P)
                    if j < n_t:
                        shifts(j)
                    if late and j % 2 and LAG <= j // 2 < LAG + len(late.lo):
                        n = j // 2 - LAG
                        late.fill_lo(dve, stacked, n, n + 1, late_set)
                    if 0 <= j - 1 < n_t:
                        invert(j - 1)
                    while done < n_groups and group_end[done] <= j - VALUE_P - 1:
                        dve.wait_ge(top, done + 1)
                        place = leaf(done)
                        dve.tensor_tensor(place(c.x_lo), OB(done), place(c.x_hi).bitcast(F32), ALU.subtract).then_inc(rest, 1)
                        done += 1

            @blk.gpsimd
            def _(pool):
                for j, t in enumerate(tiles):
                    pool.wait_ge(inverted, j + 1)
                    w = prob[:, j % n_prob, 0:t.wide]
                    if j in shorts:
                        n = shorts.index(j)
                        pool.tensor_tensor(by_head(w), by_head(w), spread(inv8[:, n % 2, :]), ALU.mult).then_inc(normed, 1)
                    else:
                        pool.tensor_scalar(w, w, inv[:, j:j + 1], 1.0 if t.gate is None else t.gate, ALU.mult, ALU.mult).then_inc(normed, 1)

            @blk.scalar
            def _(act):
                copy = lambda out, in_: act.activation(out, in_, ACT.Copy)
                done = 0
                for j in range(n_t + VALUE_P + 2):
                    if j < n_t:
                        act.wait_ge(scaled, j + 1)
                        if j in shorts:
                            w = prob[:, j % n_prob, 0:256]
                            act.activation(w, w, ACT.Exp, scale=SCALE).then_inc(exped, 1)
                        else:
                            if j >= n_prob:
                                act.wait_ge(turned, j - n_prob + 1)
                            n = tiles[j].n
                            act.activation(prob[:, j % n_prob, 0:n], S(j)[:, 0:n], ACT.Exp, bias=shift[:, j:j + 1],
                                           scale=SCALE, accum_out=total[:, j:j + 1]).then_inc(exped, 1)
                    if 0 <= j - TURN_P < n_t and tiles[j - TURN_P].mover == "act":
                        move(act, copy, j - TURN_P)
                    if late and j % 2 and j // 2 < len(late.hi):
                        late.fill_hi(copy, stacked, j // 2, j // 2 + 1)
                    while done < n_groups and group_end[done] <= j - VALUE_P:
                        act.wait_ge(valued, through(group_end[done]))
                        copy(leaf(done)(c.x_hi), OB(done)).then_inc(top, 1)
                        done += 1


class Linked:

    def __init__(self, eng, link):
        self.eng, self.link, self.count = eng, link, 0

    def __call__(self, ins):
        self.count += 1
        ins.then_inc(self.link, 1)
        self.eng.wait_ge(self.link, self.count)


def prompt_tiles(sections, branches, short=None):
    tiles, n_groups, n_short, leaves = [], 0, 0, []
    for a in range(sections):
        for qb in range(NB):
            if short:
                tiles.append(short[0](a, qb))
            for i in range(4):
                pair = 4 * a + i
                for b, (q, keys, value, bias, gate, mover) in enumerate(branches):
                    for side in range(2):
                        t = Rows((qb + 1) * P, side, q(pair, side, qb), keys(a, side), bias(qb),
                                 [(k, value(a, side, k)) for k in range(qb + 1)], gate(pair, side, qb), n_groups,
                                 mover(side), b == 0, b == len(branches) - 1)
                        if short and b == 0:
                            t.short = (n_short, side, slice(32 * i, 32 * i + 32), short[1](a, side, i))
                        tiles.append(t)
                leaves.append(lambda x, pair=pair, qb=qb: x[:, pair, qb * P:(qb + 1) * P])
                n_groups += 1
            n_short += 1
    return tiles, lambda g: leaves[g], n_groups



def take_best(dve, linked, scores, bests, n_take):
    n, sem, start = len(scores), linked.link, linked.count
    done = 0

    def step(ins):
        nonlocal done
        ins.then_inc(sem, 1)
        done += 1

    def after_own():
        if done >= n:
            dve.wait_ge(sem, start + done - n + 1)

    for r in range(-(-n_take // 8)):
        left = n_take - 8 * r
        for x, best in zip(scores, bests):
            after_own()
            step(dve.max(best, x))
        if left < 8:
            for best in bests:
                after_own()
                step(dve.memset(best[:, left:8], TAKEN))
        for x, best in zip(scores, bests):
            after_own()
            step(dve.match_replace(x, best, x, TAKEN))
    linked.count = start + done
    dve.wait_ge(sem, linked.count)


def stage_prepare(c, projT, iw, sel, keep_rows, stacks, kikT, v_old):
    nc, d = c.nc, c.dram
    block, sem = stage(c, "prepare")
    scored, relud, summed, link = sem("scored"), sem("relud"), sem("summed"), sem("link")
    table_in, v_in, page_turned, page_moved = sem("table_in"), sem("v_in"), sem("page_turned"), sem("page_moved")
    conv_in, conv_turned, conv_moved, tail_set, tail_turned, tail_moved, conv_out = (sem(s) for s in
        ("conv_in", "conv_turned", "conv_moved", "tail_set", "tail_turned", "tail_moved", "conv_out"))
    conv_link, prod, top, rest, stacked = sem("conv_link"), sem("prod"), sem("top"), sem("rest"), sem("stacked")
    W = D // 2 // P
    n_ring = 4
    land = [sem(f"land{i}") for i in range(n_ring)]
    jobs = [(qb, h) for qb in range(1, NB) for h in range(4)]
    pages = [(b, g) for b in range(DEC_B) for g in range(NPAGE)]
    with ExitStack() as tmp:
        sb = lambda n, s, dt=F32: tmp.enter_context(nc.sbuf_tensor(n, s, dt))
        relu = sb("ix_relu", [P, 2, SEQ])
        first = [sum((q + 1) * P for q in range(1, qb)) for qb in range(1, NB + 1)]
        score = sb("ix_score", [P, first[-1]])
        best = sb("ix_best", [P, NB - 1, 8])
        table = sb("pg_table", [1, DEC_B * NPAGE], I32)
        ring = sb("pg_ring", [P, n_ring, 2 * P])
        state = sb("cv_state", [64, P])
        taps = sb("cv_taps", [12, P])
        tapsT = sb("cv_tapsT", [P, 3, W])
        u_p = sb("cv_u_p", [P, 2, 2 + SEQ])
        u_s = sb("cv_u_s", [P, W, DEC_B, 2 + DEC_T])
        acc = sb("cv_acc", [P, 2, T])
        term = sb("cv_term", [P, T])
        tail = sb("cv_tail", [P, W, 18])
        tail_rows = sb("cv_tail_rows", [72, P])
        with block as blk:
            @blk.sync
            def _(sp):
                sp.dma_start(table[:, :], d["page_table"].rearrange("(a b) g -> a (b g)", a=1)).then_inc(table_in, 16)
                sp.dma_start(state[:, :], d["state_b_conv"][0].rearrange("b j (k p) -> (b j k) p", p=P)).then_inc(conv_in, 16)
                sp.dma_start(taps[:, :], d["ab_conv_w"][0].rearrange("j (k p) -> (j k) p", p=P)).then_inc(conv_in, 16)
                sp.wait_ge(table_in, 16)
                n_pool = d["cache_a_k"].shape[1]
                for n, (b, g) in enumerate(pages):
                    page = sp.value_load(table[0:1, b * NPAGE + g:b * NPAGE + g + 1], min_val=0, max_val=n_pool - 1)
                    if n >= n_ring:
                        sp.wait_ge(page_turned, n - n_ring + 1)
                    sp.dma_start(ring[:, n % n_ring, 0:P], d["cache_a_k"][0][bass.ds(page, 1)]
                                 .rearrange("a p g e -> p (a g e)")).then_inc(land[n % n_ring], 16)
                    for s in range(2):
                        sp.dma_start(ring[:, n % n_ring, P + s * HD:P + (s + 1) * HD], d["cache_a_ik"][0][bass.ds(page, 1)]
                                     .rearrange("a p e -> p (a e)")).then_inc(land[n % n_ring], 16)
                    sp.dma_start(v_old[:, b, g, :], d["cache_a_v"][0][bass.ds(page, 1)]
                                 .rearrange("a p g e -> p (a g e)")).then_inc(v_in, 16)
                sp.wait_ge(tail_moved, 1)
                for k in range(W):
                    sp.dma_start(d["b_conv_s"][0].rearrange("b j d -> (b j) d")[:, k * P:(k + 1) * P],
                                 tail_rows[18 * k:18 * k + 16, :]).then_inc(conv_out, 16)
                    sp.dma_start(d["b_conv_p"][0, 0][:, k * P:(k + 1) * P], tail_rows[18 * k + 16:18 * k + 18, :]).then_inc(conv_out, 16)
                sp.wait_ge(v_in, 16 * len(pages))
                sp.wait_ge(conv_out, 16 * 2 * W)

            @blk.tensor
            def _(pe):
                for qb in range(1, NB):
                    for h in range(4):
                        j = 4 * (qb - 1) + h
                        if j >= 4:
                            pe.wait_ge(relud, j - 3)
                        rows = rows_of(h % 2)
                        n = (qb + 1) * P
                        pe.matmul(c.ps[:, j % 4, 0:n], projT[rows, 4 + h // 2, qb * P:(qb + 1) * P],
                                  projT[rows, 7, 0:n], start=True, stop=True).then_inc(scored, 1)
                pe.wait_ge(conv_in, 32)
                pe.transpose(c.ps[:, 7, 0:64], state[:, :], c.k("ident")[0:64, 0:64])
                pe.transpose(c.ps[:, 7, 64:76], taps[:, :], c.k("ident")[0:12, 0:12]).then_inc(conv_turned, 1)
                for n in range(len(pages)):
                    if n >= 3:
                        pe.wait_ge(page_moved, n - 2)
                    pe.wait_ge(land[n % n_ring], 48 * (n // n_ring + 1))
                    for h in range(2):
                        last = pe.transpose(c.ps[:, 4 + n % 3, h * P:(h + 1) * P], ring[:, n % n_ring, h * P:(h + 1) * P], c.k("ident"))
                    last.then_inc(page_turned, 1)
                pe.wait_ge(tail_set, 1)
                pe.transpose(c.ps[0:72, 7, P:2 * P], tail[:, :, :].rearrange("p k n -> p (k n)"), c.k("ident")).then_inc(tail_turned, 1)

            @blk.scalar
            def _(act):
                copy = lambda out, in_: act.activation(out, in_, ACT.Copy)
                for qb in range(1, NB):
                    for h in range(4):
                        j = 4 * (qb - 1) + h
                        n = (qb + 1) * P
                        act.wait_ge(scored, j + 1)
                        if j >= 2:
                            act.wait_ge(summed, j - 1)
                        act.activation(relu[:, j % 2, 0:n], c.ps[:, j % 4, 0:n], ACT.Relu, scale=SCALE).then_inc(relud, 1)
                act.wait_ge(conv_turned, 1)
                copy(u_s[:, :, :, 0:2].rearrange("p k b j -> p b j k"), c.ps[:, 7, 0:64].rearrange("p (b j k) -> p b j k", b=DEC_B, j=2))
                copy(tapsT[:, :, :], c.ps[:, 7, 64:76].rearrange("p (j k) -> p j k", k=W)).then_inc(conv_moved, 1)
                stacks.fill_hi(copy, stacked, 0, len(stacks.hi))
                for i in range(2):
                    for n in range(i * len(pages) // 2, (i + 1) * len(pages) // 2):
                        b, g = pages[n]
                        act.wait_ge(page_turned, n + 1)
                        copy(kikT[:, :, b, g * PAGE:(g + 1) * PAGE], c.ps[:, 4 + n % 3, 0:2 * P].rearrange("p (h n) -> p h n", n=P)).then_inc(page_moved, 1)
                    for k in (2 * i, 2 * i + 1):
                        act.wait_ge(prod, k + 1)
                        copy(c.x_hi[:, 4 + k, :], acc[:, k % 2, :]).then_inc(top, 1)
                act.wait_ge(tail_turned, 1)
                copy(tail_rows[:, :], c.ps[0:72, 7, P:2 * P]).then_inc(tail_moved, 1)

            @blk.vector
            def _(dve):
                linked = Linked(dve, link)
                linked(dve.tensor_scalar(iw[:, 0:NB, :], keep_rows[:, 0:NB, :], 0.5, None, ALU.mult))
                linked(dve.tensor_scalar(iw[0:TS, NB, :], keep_rows[0:TS, NB, :], 0.5, None, ALU.mult))
                scores = [score[:, first[i]:first[i + 1]] for i in range(NB - 1)]
                for j, (qb, h) in enumerate(jobs):
                    n = (qb + 1) * P
                    x = scores[qb - 1]
                    dve.wait_ge(relud, j + 1)
                    if h == 0:
                        dve.tensor_scalar(x, relu[:, j % 2, 0:n], iw[:, qb, 0:1], None, ALU.mult).then_inc(summed, 1)
                    else:
                        dve.wait_ge(summed, j)
                        dve.scalar_tensor_tensor(x, relu[:, j % 2, 0:n], iw[:, qb, h:h + 1], x, ALU.mult, ALU.add).then_inc(summed, 1)
                dve.wait_ge(summed, len(jobs))
                for qb in range(1, NB):
                    own = scores[qb - 1][:, qb * P:(qb + 1) * P]
                    linked(dve.scalar_tensor_tensor(own, c.k("causal"), BIG, own, ALU.mult, ALU.add))
                take_best(dve, linked, scores, [best[:, i, :] for i in range(NB - 1)], TOPK_P)
                for i, x in enumerate(scores):
                    dve.tensor_scalar(sel[:, i + 1, 0:(i + 2) * P], x, TAKEN, 1.0, ALU.is_equal, ALU.subtract)

            @blk.gpsimd
            def _(pool):
                linked = Linked(pool, conv_link)
                linked(pool.memset(u_p[:, :, 0:2], 0.0))
                seq = lambda slab: projT[:, slab, SEQ:T].rearrange("p (b t) -> p b t", b=DEC_B)
                pool.wait_ge(conv_moved, 1)
                for k in range(W):
                    linked(pool.tensor_tensor(u_p[:, k % 2, 2:], projT[:, 14 + k, 0:SEQ], projT[:, 18 + k, 0:SEQ], ALU.mult))
                    linked(pool.tensor_tensor(u_s[:, k, :, 2:], seq(14 + k), seq(18 + k), ALU.mult))
                    linked(pool.tensor_copy(tail[:, k, 16:18], u_p[:, k % 2, SEQ:SEQ + 2]))
                    if k >= 2:
                        pool.wait_ge(top, k - 1)
                        pool.tensor_tensor(c.x_lo[:, 2 + k, :], acc[:, k % 2, :], c.x_hi[:, 2 + k, :].bitcast(F32), ALU.subtract).then_inc(rest, 1)
                        pool.wait_ge(rest, k - 1)
                    a_p = acc[:, k % 2, 0:SEQ]
                    a_s = acc[:, k % 2, SEQ:T].rearrange("p (b t) -> p b t", b=DEC_B)
                    for j in range(3):
                        w, u_prompt = tapsT[:, j, k:k + 1], u_p[:, k % 2, j:j + SEQ]
                        for a, u in ((a_p, u_prompt), (a_s, u_s[:, k, :, j:j + DEC_T])):
                            if j == 0:
                                linked(pool.tensor_scalar(a, u, w, None, ALU.mult))
                            else:
                                part = term[:, 0:SEQ] if u is u_prompt else term[:, SEQ:T].rearrange("p (b t) -> p b t", b=DEC_B)
                                linked(pool.tensor_scalar(part, u, w, None, ALU.mult))
                                linked(pool.tensor_tensor(a, a, part, ALU.add))
                    pool.tensor_tensor(acc[:, k % 2, :], acc[:, k % 2, :], projT[:, 10 + k, :], ALU.mult).then_inc(prod, 1)
                pool.tensor_copy(tail[:, :, 0:16].rearrange("p k (b j) -> p k b j", j=2), u_s[:, :, :, 4:6]).then_inc(tail_set, 1)
                for k in range(2, W):
                    pool.wait_ge(top, k + 1)
                    pool.tensor_tensor(c.x_lo[:, 4 + k, :], acc[:, k % 2, :], c.x_hi[:, 4 + k, :].bitcast(F32), ALU.subtract).then_inc(rest, 1)
                    pool.wait_ge(rest, k + 1)
                stacks.fill_lo(pool, stacked, 0, len(stacks.lo))


def stage_index_sample(c, projT, iw_rows, ikT, sel_s, q_blk):
    nc = c.nc
    block, sem = stage(c, "index_s")
    q_set, scored, relud, mixed, picked, link = (sem(s) for s in ("q_set", "scored", "relud", "mixed", "picked", "link"))
    mix_set = sem("mix_set")
    with ExitStack() as tmp:
        sb = lambda n, s, d=F32: tmp.enter_context(nc.sbuf_tensor(n, s, d))
        iq = sb("is_iq", [P, DEC_B, 32])
        relu = sb("is_relu", [P, 2, NEW])
        mix = sb("is_mix", [P, 2, P])
        col = sb("is_col", [P, 2])
        hit = sb("is_hit", [P, 2, 4])
        score = sb("is_score", [P, 2, NEW])
        best = sb("is_best", [P, 2, 8])
        with block as blk:
            @blk.vector
            def _(dve):
                linked = Linked(dve, link)

                linked(dve.memset(iq[:, :, :], 0.0))
                linked(dve.memset(q_blk[:, :, :, :, :], 0.0))
                iq_v = iq[:, :, 0:16].rearrange("p b (s i t) -> p b s i t", s=2, i=2)
                for side in range(2):
                    rows = slice(side * HD, side * HD + HD)
                    for i in range(2):
                        linked(dve.tensor_copy(iq_v[rows, :, side, i, :], projT[rows, 4 + i, SEQ:T].rearrange("p (b t) -> p b t", t=DEC_T)))
                    for h in range(4):
                        linked(dve.tensor_copy(q_blk[rows, :, side, h, :], projT[rows, h, SEQ:T].rearrange("p (b t) -> p b t", t=DEC_T)))
                dve.wait_ge(picked, 1)
                for j in range(2):
                    linked(dve.tensor_tensor(hit[:, j, :], c.ps[:, 7, 4 * j:4 * j + 4], c.k("ihead"), ALU.mult))
                    linked(dve.reduce_sum(col[:, j:j + 1], hit[:, j, :], AX_X))
                    dve.tensor_scalar(mix[:, j, :], c.k("imix"), col[:, j:j + 1], None, ALU.mult).then_inc(mix_set, 1)
                dve.sem_inc(q_set, 1)
                for j in range(2):
                    dve.wait_ge(mixed, j + 1)
                    linked(dve.tensor_copy(score[:, j, :], c.ps[:, 2 + j, 0:NEW]))
                    own = score[:, j, PAST:NEW]
                    linked(dve.scalar_tensor_tensor(own, c.k("new")[:, j * TS:(j + 1) * TS], BIG, own, ALU.mult, ALU.add))
                take_best(dve, linked, [score[:, j, :] for j in range(2)], [best[:, j, :] for j in range(2)], TOPK_S)
                for j in range(2):
                    dve.tensor_scalar(sel_s[:, j, :], score[:, j, :], TAKEN, 1.0, ALU.is_equal, ALU.subtract)

            @blk.tensor
            def _(pe):
                for j in range(2):
                    last = pe.matmul(c.ps[:, 7, 4 * j:4 * j + 4], c.k("pick")[0:TS, j * P:(j + 1) * P], iw_rows,
                                     start=(j == 0), stop=(j == 1), skip_group_check=True)
                last.then_inc(picked, 1)
                pe.wait_ge(mix_set, 2)
                for j in range(2):
                    for u in range(4):
                        b = 4 * j + u
                        pe.matmul(c.ps[32 * u:32 * u + 32, j, 0:PAST], iq[:, b, :], ikT[:, 0, b, :], start=True, stop=False, skip_group_check=True)
                        last = pe.matmul(c.ps[32 * u:32 * u + 32, j, PAST:NEW], iq[:, b, :], projT[:, 7, SEQ:T], start=False, stop=True, skip_group_check=True)
                    last.then_inc(scored, 1)
                for j in range(2):
                    pe.wait_ge(relud, j + 1)
                    pe.matmul(c.ps[:, 2 + j, 0:NEW], mix[:, j, :], relu[:, j, :], start=True, stop=True).then_inc(mixed, 1)

            @blk.scalar
            def _(act):
                for j in range(2):
                    act.wait_ge(scored, j + 1)
                    act.activation(relu[:, j, :], c.ps[:, j, 0:NEW], ACT.Relu, scale=SCALE).then_inc(relud, 1)


def sample_groups(n, units, branches, gate, leaves):
    out = []
    for j in range(n):
        tiles = []
        mine = units[4 * j:4 * j + 4]
        for a, (q, cached, n_old, new, bias, value) in enumerate(branches):
            scores = []
            for u, unit in enumerate(mine):
                scores.append((32 * u, 32 * u + 32, 0, n_old, q(unit), cached(unit)))
                if new:
                    scores.append((32 * u, 32 * u + 32, n_old, TS, q(unit), new(unit)))
            n_keys = n_old + (TS if new else 0)
            n_chunk = -(-n_keys // P)
            values = []
            for u, unit in enumerate(mine):
                for k in range(n_chunk):
                    values.append((32 * u, 32 * u + 32, a * P, P, slice(32 * u, 32 * u + 32), k,
                                   value(unit, k, min(P, n_keys - k * P)), a == 0 and k == 0,
                                   a == len(branches) - 1 and k == n_chunk - 1))
            tiles.append(Tile(scores, [bias(j)] if bias else [], n_keys, values, ("act", "dve")[a % 2]))
        out.append(Group(tiles, 1, len(branches), gate(j) if gate else None, leaves(j)))
    return out



def stage_compress(c, projT, k_cmpT, v_cmp_p, v_cmp_s, stacks):
    nc = c.nc
    block, sem = stage(c, "compress")
    d, tags = c.dram, ("k", "v")
    zeroed, table_in, small_in, pe_t, pe_m, placed, bias_m, gelu, outp, outm, win_out, v_clear = (sem(s) for s in
        ("zeroed", "table_in", "small_in", "pe_t", "pe_m", "placed", "bias_m", "gelu", "outp", "outm", "win_out", "v_clear"))
    w1_in, hid, turned, stacked = sem("w1_in"), sem("hid"), sem("turned"), sem("stacked")
    n_ring = 8
    land = [sem(f"land{i}") for i in range(n_ring)]
    evac = [sem("evac_dve"), sem("evac_act")]
    N = (2 * SEQ + 2 * DEC_B * PAST) // CMP_S
    OLD = 2 * SEQ
    steps = [(tag, b, g) for tag in range(2) for b in range(DEC_B) for g in range(NPAGE)]
    per = len(steps) // 2
    w1d = [x[:, 0:CMP_W // 2 * P].rearrange("p (j e) -> p j e", e=P) for x in
           (c.w_raw[:, :, :, :].rearrange("p s k n -> p (s k n)"), projT[:, 16:20, :].rearrange("p k n -> p (k n)"))]
    with ExitStack() as tmp:
        sb = lambda n, s, dt=F32: tmp.enter_context(nc.sbuf_tensor(n, s, dt))
        line = sb("cp_line", [P, N * CMP_S + CMP_W])
        table = sb("cp_table", [1, DEC_B * NPAGE], I32)
        ring = sb("cp_ring", [P, n_ring, 2 * P])
        w2d = sb("cp_w2", [P, 2, P])
        rows = sb("cp_pe_rows", [CMP_W, 2, P])
        bias = sb("cp_bias", [P, 2])
        hidT = sb("cp_hidT", [P, N])
        old = line[:, OLD:OLD + 2 * DEC_B * PAST].rearrange("p (a b n) -> p a b n", a=2, b=DEC_B)
        with block as blk:
            @blk.gpsimd
            def _(pool):
                for x in w1d:
                    pool.memset(x, 0.0).then_inc(zeroed, 1)
                pool.memset(w2d[:, :, :], 0.0).then_inc(zeroed, 1)

            @blk.sync
            def _(sp):
                sp.dma_start(table[:, :], d["page_table"].rearrange("(a b) g -> a (b g)", a=1)).then_inc(table_in, 16)
                sp.wait_ge(table_in, 16)

                def load_page(n):
                    tag, b, g = steps[n]
                    cache = d["cache_c_cmp_" + tags[tag]]
                    page = sp.value_load(table[0:1, b * NPAGE + g:b * NPAGE + g + 1], min_val=0, max_val=cache.shape[1] - 1)
                    if n >= n_ring:
                        sp.wait_ge(turned, n - n_ring + 1)
                    sp.dma_start(ring[:, n % n_ring, :], cache[0][bass.ds(page, 1)].rearrange("a p g e -> p (a g e)")).then_inc(land[n % n_ring], 16)

                def load_w1(tag):
                    w1 = d["c_cmp_w1_" + tags[tag]][0].rearrange("j d e -> d j e")
                    for s in range(2):
                        own = rows_of(s)
                        for half, x in enumerate(w1d):
                            at = slice(half * CMP_W // 2, (half + 1) * CMP_W // 2)
                            sp.dma_start(x[own, :, own], w1[:, at, :]).then_inc(w1_in, 16)

                for n in range(n_ring):
                    load_page(n)
                sp.wait_ge(zeroed, 3)
                load_w1(0)
                for tag in range(2):
                    for s in range(2):
                        own = rows_of(s)
                        sp.dma_start(w2d[own, tag, own], d["c_cmp_w2_" + tags[tag]][0]).then_inc(small_in, 16)
                        sp.dma_start(rows[:, tag, own], d["c_cmp_pe_" + tags[tag]][0]).then_inc(small_in, 16)
                for n in range(n_ring, per):
                    load_page(n)
                for tag in tags:
                    sp.dma_start(d[f"c_win_{tag}_s"][0][:, 0:PAST - DEC_T], d[f"state_c_win_{tag}"][0][:, DEC_T:PAST]).then_inc(win_out, 16)
                for n in range(per, per + n_ring):
                    load_page(n)
                sp.wait_ge(hid, 1)
                load_w1(1)
                for n in range(per + n_ring, 2 * per):
                    load_page(n)
                sp.wait_ge(win_out, 32)

            def second(pe, tag):
                pe.wait_ge(gelu, tag + 1)
                if tag == 0:
                    pe.matmul(c.ps[:, 2, 0:N], w2d[:, 0, :], hidT[:, :], start=True, stop=True).then_inc(outp, 1)
                    return
                pe.wait_ge(outm, 1)
                for i in range(2):
                    pe.matmul(c.ps[0:NCMP_P, 2, i * P:(i + 1) * P], hidT[:, 32 * i:32 * i + NCMP_P], w2d[:, 1, :],
                              start=(i == 0), stop=(i == 1), skip_group_check=True)
                for i in range(2 * DEC_B):
                    c0 = OLD // CMP_S + i * (PAST // CMP_S)
                    last = pe.matmul(c.ps[0:NCMP_S, 3 + i // 4, (i % 4) * P:(i % 4 + 1) * P], hidT[:, c0:c0 + NCMP_S], w2d[:, 1, :],
                                     start=(i % 4 == 0), stop=(i % 4 == 3), skip_group_check=True)
                last.then_inc(outp, 1)

            @blk.tensor
            def _(pe):
                for tag in range(2):
                    for n in range(tag * per, (tag + 1) * per):
                        if n >= 4:
                            pe.wait_ge(evac[n % 2], (n - 4) // 2 + 1)
                        pe.wait_ge(land[n % n_ring], 16 * (n // n_ring + 1))
                        for h in range(2):
                            last = pe.transpose(c.ps[:, 3 + n % 4, h * P:(h + 1) * P], ring[:, n % n_ring, h * P:(h + 1) * P], c.k("ident"))
                        last.then_inc(turned, 1)
                    if tag == 0:
                        pe.wait_ge(small_in, 16 * 8)
                    else:
                        second(pe, 0)
                    pe.transpose(c.ps[:, 1, tag * CMP_W:(tag + 1) * CMP_W], rows[:, tag, :], c.k("ident")[0:CMP_W, 0:CMP_W]).then_inc(pe_t, 1)
                    pe.wait_ge(pe_m, tag + 1)
                    pe.wait_ge(placed, 2 * (tag + 1))
                    for e in evac:
                        pe.wait_ge(e, (tag + 1) * per // 2)
                    pe.wait_ge(w1_in, 64 * (tag + 1))
                    for j in range(CMP_W):
                        last = pe.matmul(c.ps[:, 0, 0:N + 1], w1d[j // (CMP_W // 2)][:, j % (CMP_W // 2), :],
                                         line[:, j:j + N * CMP_S + 1:CMP_S], start=j == 0, stop=j == CMP_W - 1)
                    last.then_inc(hid, 1)
                second(pe, 1)

            def move(eng, copy, n):
                tag, b, g = steps[n]
                eng.wait_ge(turned, n + 1)
                copy(old[:, :, b, g * PAGE:(g + 1) * PAGE], c.ps[:, 3 + n % 4, 0:2 * P].rearrange("p (h n) -> p h n", n=P)).then_inc(evac[n % 2], 1)

            def place(eng, copy, tag, i):
                copy(line[:, i * SEQ:(i + 1) * SEQ], projT[:, (8, 14)[tag] + i, 0:SEQ]).then_inc(placed, 1)

            n_hi, n_lo = len(stacks.hi), len(stacks.lo)

            @blk.vector
            def _(dve):
                for tag in range(2):
                    if tag:
                        stacks.fill_lo(dve, stacked, 0, n_lo // 2)
                        dve.wait_ge(hid, 1)
                        dve.wait_ge(gelu, 1)
                    place(dve, dve.tensor_copy, tag, 0)
                    for n in range(tag * per, (tag + 1) * per, 2):
                        move(dve, dve.tensor_copy, n)
                    if tag:
                        dve.wait_ge(outp, 1)
                        dve.tensor_copy(k_cmpT[:, :], c.ps[:, 2, 0:N]).then_inc(outm, 1)
                    dve.wait_ge(pe_t, tag + 1)
                    dve.tensor_copy(line[:, N * CMP_S:N * CMP_S + CMP_W], c.ps[:, 1, tag * CMP_W:(tag + 1) * CMP_W]).then_inc(pe_m, 1)
                dve.memset(v_cmp_p[:, :], 0.0).then_inc(v_clear, 1)
                stacks.fill_lo(dve, stacked, n_lo // 2, n_lo)
                dve.wait_ge(v_clear, 1)
                dve.wait_ge(outp, 2)
                for i in range(4):
                    dve.tensor_copy(v_cmp_p[32 * i:32 * i + NCMP_P, :], c.ps[0:NCMP_P, 2, 0:2 * P])

            @blk.scalar
            def _(act):
                copy = lambda out, in_: act.activation(out, in_, ACT.Copy)
                for tag in range(2):
                    if tag:
                        act.wait_ge(hid, 1)
                    place(act, copy, tag, 1)
                    for n in range(tag * per + 1, (tag + 1) * per, 2):
                        move(act, copy, n)
                    stacks.fill_hi(copy, stacked, tag * n_hi // 2, (tag + 1) * n_hi // 2)
                    act.wait_ge(hid, tag + 1)
                    copy(bias[:, tag:tag + 1], c.ps[:, 0, N:N + 1]).then_inc(bias_m, 1)
                    act.wait_ge(bias_m, tag + 1)
                    if tag:
                        act.wait_ge(outp, 1)
                    act.activation(hidT[:, :], c.ps[:, 0, 0:N], ACT.Gelu_apprx_tanh, bias=bias[:, tag:tag + 1]).then_inc(gelu, 1)
                act.wait_ge(outp, 2)
                copy(v_cmp_s[0:NCMP_S, :].rearrange("p (a n) -> p a n", a=4), c.ps[0:NCMP_S, 3:7, :])


def stage_gates(c, projT, gate_sig, gate_s, q_blk, k_cmpT, kc2):
    nc = c.nc
    block, sem = stage(c, "gates")
    sig, picked, link = sem("sig"), sem("picked"), sem("link")
    with ExitStack() as tmp:
        hit = tmp.enter_context(nc.sbuf_tensor("gt_hit", [P, 3, 16], F32))
        cleared, stacked = sem("cleared"), sem("stacked")
        with block as blk:
            @blk.gpsimd
            def _(pool):
                pool.memset(kc2[:, :, :, :].bitcast(F32), 0.0).then_inc(cleared, 1)
                pool.wait_ge(cleared, 1)
                stacks = Stack()
                for a in range(2):
                    for side in range(2):
                        stacks.keys(side, k_cmpT[rows_of(side), 32 * a:32 * a + NCMP_P],
                                    kc2[:, 0, 2 * a + side, 0:NCMP_P], kc2[:, 1, 2 * a + side, 0:NCMP_P])
                stacks.fill_hi(pool.tensor_copy, stacked, 0, len(stacks.hi))
                stacks.fill_lo(pool, stacked, 0, len(stacks.lo))

            @blk.scalar
            def _(act):
                act.activation(gate_sig[:, 0:NB, :], gate_sig[:, 0:NB, :], ACT.Sigmoid)
                act.activation(gate_sig[0:TS, NB, :], gate_sig[0:TS, NB, :], ACT.Sigmoid).then_inc(sig, 1)

            @blk.tensor
            def _(pe):
                pe.wait_ge(sig, 1)
                for j in range(4):
                    last = pe.matmul(c.ps[:, 0, 48 * j:48 * j + 48], c.k("pick")[0:TS, (2 + j) * P:(3 + j) * P],
                                     gate_sig[0:TS, NB, :], start=(j == 0), stop=(j == 3), skip_group_check=True)
                last.then_inc(picked, 1)

            @blk.vector
            def _(dve):
                linked = Linked(dve, link)

                linked(dve.memset(q_blk[:, :, :, :, :, :], 0.0))
                for side in range(2):
                    rows = slice(side * HD, side * HD + HD)
                    for pair in range(2):
                        for h in range(4):
                            linked(dve.tensor_copy(q_blk[rows, :, pair, side, h, :],
                                                   projT[rows, 4 * pair + h, SEQ:T].rearrange("p (b t) -> p b t", t=DEC_T)))
                dve.wait_ge(picked, 1)
                for j in range(4):
                    g = c.ps[:, 0, 48 * j:48 * j + 48].rearrange("p (h a) -> p a h", a=3)
                    for a in range(3):
                        linked(dve.tensor_tensor(hit[:, a, :], g[:, a, :], c.k("chead"), ALU.mult))
                    linked(dve.reduce_sum(gate_s[:, j, :], hit[:, :, :], AX_X))



def program(nc, dram):
    with ExitStack() as ctx:
        c = setup_memory(nc, ctx, dram)
        d = dram
        pair = lambda a, b: [(0, a, HD), (HD, b, HD)]
        a_rope = [pair(A_Q + i * HD, A_Q + (4 + i) * HD) for i in range(4)]
        a_rope += [[(0, A_IQ, P)], [(0, A_IQ + P, P)], [(0, A_K, P)], pair(A_IK, A_IK)]
        a_plain = [[(0, A_V, P)], [(0, A_IW, P)]] + [[(0, A_GB + i * P, P)] for i in range(12)]
        c_rope = [pair(C_Q + p * 512 + h * HD, C_Q + p * 512 + 256 + h * HD) for p in range(2) for h in range(4)]
        c_rope += [[(0, col + i * P, P)] for col in (C_KC, C_KS, C_KW) for i in range(2)]
        c_plain = [[(0, col + i * P, P)] for col in (C_VC, C_VS, C_VW) for i in range(2)]
        c_plain += [[(0, C_G + 48 - P, P)]]

        with ExitStack() as mem:
            sb = lambda n, s, dt=F32: mem.enter_context(nc.sbuf_tensor(n, s, dt))
            projT = sb("a_projT", [P, 22, T])
            stage_in_proj(c, "a_in", lambda sem, tmp: Load(c, sem, tmp), d["ab_w_in"][0], a_rope, a_plain, projT)
            v_rows = sb("a_v_rows", [P, NB + 1, P])
            iw_full = sb("a_iw_rows", [P, NB + 1, P])
            iw = sb("a_iw", [P, NB + 1, 4])
            p_rows = lambda name: d[name][0, 0].rearrange("t g e -> t (g e)")
            s_rows = lambda name: d[name][0].rearrange("b t g e -> (b t) (g e)")
            stage_rows(c, "a_rows", projT, [
                (6, None, [(0, p_rows("a_k_p"), s_rows("a_k_s"))]),
                (7, None, [(0, d["a_ik_p"][0, 0], d["a_ik_s"][0].rearrange("b t e -> (b t) e"))]),
                (8, v_rows, [(0, p_rows("a_v_p"), s_rows("a_v_s"))]),
                (9, iw_full, [])])
            sel = sb("a_sel", [P, NB, SEQ], BF16)
            reuse_semaphores(c)
            a_more = sb("a_more_stacks", [P, 2, SEQ], F32R)
            slots = idle_slots(c) + [a_more[:, e, :] for e in range(2)]
            a_q2, a_k2 = slots[0:8], slots[8:12]
            stacks = Stack()
            for side in range(2):
                for i in range(4):
                    stacks.queries(side, projT[rows_of(side), i, 0:SEQ], a_q2[2 * i + side])
                stacks.keys(side, projT[rows_of(side), 6, 0:SEQ], a_k2[2 * side], a_k2[2 * side + 1])
            kikT = sb("a_kikT", [P, 2, DEC_B, PAST])
            v_old = sb("a_v_old", [P, DEC_B, NPAGE, P])
            stage_prepare(c, projT, iw, sel, iw_full[:, :, 0:4], stacks, kikT, v_old)
            stage_attend_prompt(c, "a_att", *prompt_tiles(1, [(
                lambda i, s, qb: a_q2[2 * i + s][:, qb * P:(qb + 1) * P],
                lambda a, s: a_k2[2 * s:2 * s + 2],
                lambda a, s, k: v_rows[:, k, rows_of(s)],
                lambda qb: (0, (qb + 1) * P, sel[:, qb, 0:(qb + 1) * P]) if qb else (0, P, c.causal_bf[:, :]),
                lambda i, s, qb: None, lambda side: ("act", "dve")[side])]))

            sel_s = sb("a_sel_s", [P, 2, NEW], BF16)
            q_blk = sb("a_q_blk", [P, DEC_B, 2, 4, DEC_T])
            stage_index_sample(c, projT, iw[0:TS, NB, :], kikT[:, 1:2], sel_s, q_blk)
            q_of = lambda b: q_blk[:, b].rearrange("p s h t -> p (s h t)")

            def a_leaves(j):
                def side(s):
                    place = lambda x: x[rows_of(s), 0:4, SEQ + 16 * j:SEQ + 16 * j + 16].rearrange("p h (u t) -> p u h t", t=DEC_T)
                    cols = lambda o: o[rows_of(s), 0:P].rearrange("p (u s h t) -> p u s h t", u=4, s=2, h=4)[:, :, s]
                    return [(lambda x, u=u: place(x)[:, u], lambda o, u=u: cols(o)[:, u]) for u in range(4)]
                return side(0) + side(1)

            def a_out_rows(w, cols):
                return [(lambda r: r[0:HD, 0:4, :], w[0:256, cols].rearrange("(k p) n -> p k n", p=HD)),
                        (lambda r: r[HD:P, 0:4, :], w[256:512, cols].rearrange("(k p) n -> p k n", p=HD)),
                        (lambda r: r[:, 4:8, :], w[512:1024, cols].rearrange("(k p) n -> p k n", p=P))]

            stage_attend(c, "a_att_s", sample_groups(2, list(range(DEC_B)), [(
                q_of, lambda b: kikT[:, 0, b, :], PAST, lambda b: projT[:, 6, SEQ:T],
                lambda j: (0, NEW, sel_s[:, j, :]),
                lambda b, k, n: v_old[:, b, k, :] if k < NPAGE else v_rows[0:TS, NB, :])],
                None, a_leaves), [(a_out_rows(d["ab_w_out"][0], slice(n * P, (n + 1) * P)), KT) for n in range(2)])

            stage_out_proj(c, "a_out", d["ab_w_out"][0], a_out_rows)
        reuse_semaphores(c)
        channel_mixer(c, 0)
        reuse_semaphores(c)

        with ExitStack() as mem:
            sb = lambda n, s, dt=F32: mem.enter_context(nc.sbuf_tensor(n, s, dt))
            projT = sb("c_projT", [P, 21, T])
            stage_in_proj(c, "c_in", lambda sem, tmp: Norm(c, sem, tmp, 2), d["c_w_in"][0], c_rope, c_plain, projT)
            vs_rows = [sb(f"vs_rows{i}", [P, NB + 1, P]) for i in range(2)]
            vw_rows = [sb(f"vw_rows{i}", [P, NB + 1, P]) for i in range(2)]
            k_cmpT = sb("k_cmpT", [P, (2 * SEQ + 2 * DEC_B * PAST) // CMP_S])
            v_cmp_p = sb("v_cmp_p", [P, 2 * P])
            kc2 = sb("kc2", [P, 2, 4, 32], F32R)
            g_rows = sb("g_rows", [P, NB + 1, P])
            gate_s = sb("gate_s", [P, 4, 3])
            p_rows = lambda name, i: d[name][0, 0].rearrange("t g e -> t (g e)")[:, i * P:(i + 1) * P]
            s_rows = lambda name, i: d[name][0].rearrange("b t g e -> (b t) (g e)")[:, i * P:(i + 1) * P]
            w_new = lambda name, i: d[name][0][:, PAST - DEC_T:PAST].rearrange("b t g e -> b t (g e)")[:, :, i * P:(i + 1) * P]
            stage_rows(c, "c_rows", projT,
                       [(8 + i, None, [(0, p_rows("c_cmp_k_p", i), s_rows("c_cmp_k_s", i))]) for i in range(2)]
                       + [(10 + i, None, [(0, p_rows("c_slc_k_p", i), s_rows("c_slc_k_s", i))]) for i in range(2)]
                       + [(12 + i, None, [(0, p_rows("c_win_k_p", i), w_new("c_win_k_s", i))]) for i in range(2)]
                       + [(14 + i, None, [(0, p_rows("c_cmp_v_p", i), s_rows("c_cmp_v_s", i))]) for i in range(2)]
                       + [(16 + i, vs_rows[i], [(0, p_rows("c_slc_v_p", i), s_rows("c_slc_v_s", i))]) for i in range(2)]
                       + [(18 + i, vw_rows[i], [(0, p_rows("c_win_v_p", i), w_new("c_win_v_s", i))]) for i in range(2)]
                       + [(20, g_rows, [])])
            slots = idle_slots(c)

            def section_stacks(a, q2, k2):
                stacks = Stack()
                for side in range(2):
                    for i in range(4):
                        stacks.queries(side, projT[rows_of(side), 4 * a + i, 0:SEQ], q2[2 * i + side])
                    for b, slab in enumerate((10, 12)):
                        at = 4 * b + 2 * side
                        stacks.keys(side, projT[rows_of(side), slab + a, 0:SEQ], k2[at], k2[at + 1])
                return stacks

            q2_first, k2_first = [x[:, 4 + i, 0:SEQ] for i in range(4) for x in (c.x_hi, c.x_lo)], slots[0:8]
            stacks = section_stacks(0, q2_first, k2_first)
            v_cmp_s = projT[:, 14:18, :].rearrange("p k n -> p (k n)")[:, 0:2 * DEC_B * P]
            stage_compress(c, projT, k_cmpT, v_cmp_p, v_cmp_s, stacks)
            reuse_semaphores(c)
            gate_sig = g_rows[:, :, P - 48:P]
            q_blk = projT[:, 8, 0:SEQ].rearrange("p (b i s h t) -> p b i s h t", b=DEC_B, i=2, s=2, h=4)
            stage_gates(c, projT, gate_sig, gate_s, q_blk, k_cmpT, kc2)

            def c_out_rows(w, cols):
                v = w[:, cols].rearrange("(a s h p) n -> a s p h n", a=2, s=2, h=4)
                return [((lambda r, a=a, s=s: r[rows_of(s), 4 * a:4 * a + 4, :]), v[a, s]) for a in range(2) for s in range(2)]

            def gate(i, qb):
                g = gate_sig[:, qb, i // 4 * 24:i // 4 * 24 + 24].rearrange("p (s h a) -> p s h a", s=2, h=4)
                return g[:, :, i % 4, :]

            causal = lambda qb: (qb * P, P, c.causal_bf[:, :])
            till_samples = ExitStack()
            more = till_samples.enter_context(nc.sbuf_tensor("more_stacks", [P, 14, SEQ], F32R))
            slots += [more[:, e, :] for e in range(14)]
            c_q2, c_k2 = q2_first + slots[8:16], k2_first + slots[16:24]
            c_q = lambda i, s, qb: c_q2[2 * i + s][:, qb * P:(qb + 1) * P]
            c_gate = lambda branch: (lambda i, s, qb: gate(i, qb)[:, s, branch:branch + 1])
            kc = lambda part, a, s: kc2[:, part, 2 * a + s, :]
            short = lambda a, qb: Short(
                [(c_q(4 * a + h, s, qb), kc(0, a, s), kc(1, a, s)) for s in range(2) for h in range(4)],
                c.cmp_bf[:, qb * 32:qb * 32 + 32].rearrange("p (a n) -> p a n", a=1).broadcast_to([P, 8, 32]),
                gate_sig[:, qb, a * 24:a * 24 + 24].rearrange("p (s h b) -> p s h b", s=2, h=4)[:, :, :, 0])
            stage_attend_prompt(c, "c_att", *prompt_tiles(2, [
                (c_q, lambda a, s: c_k2[8 * a + 2 * s:8 * a + 2 * s + 2],
                 lambda a, s, k: vs_rows[a][:, k, rows_of(s)], causal, c_gate(1), lambda side: "act"),
                (c_q, lambda a, s: c_k2[8 * a + 4 + 2 * s:8 * a + 6 + 2 * s],
                 lambda a, s, k: vw_rows[a][:, k, rows_of(s)], causal, c_gate(2), lambda side: ("act", "dve")[side])],
                (short, lambda a, s, i: v_cmp_p[32 * i:32 * i + 32, a * P + s * HD:a * P + (s + 1) * HD])),
                late=section_stacks(1, c_q2[8:16], c_k2[8:16]))

            till_samples.close()
            for half in range(2):
                seqs = list(range(4 * half, 4 * half + 4))
                with ExitStack() as tmp:
                    sbt = lambda n, s: tmp.enter_context(nc.sbuf_tensor(f"{n}{half}", s, F32))
                    ksT = sbt("ksT", [P, 2, 4, PAST])
                    kwT = sbt("kwT", [P, 2, 4, PAST])
                    vs_old = sbt("vs_old", [P, 4, NPAGE, 2 * P])
                    vw_old = sbt("vw_old", [P, 4, NPAGE, 2 * P])
                    stage_pages_c(c, f"c_pages{half}", seqs, ksT, kwT, vs_old, vw_old)
                    units = [(b, p) for b in seqs for p in range(2)]
                    q_of = lambda u: q_blk[:, u[0], u[1]].rearrange("p s h t -> p (s h t)")
                    new_bias = lambda j: (PAST, TS, c.new_bf[:, (2 + 2 * half + j) * TS:(3 + 2 * half + j) * TS])
                    g_of = lambda j: gate_s[:, 2 * half + j:2 * half + j + 1, :]

                    def c_leaves(j):
                        out = []
                        for s in range(2):
                            for u in range(4):
                                b, p = units[4 * j + u]
                                out.append((lambda x, s=s, b=b, p=p: x[rows_of(s), 4 * p:4 * p + 4, SEQ + 4 * b:SEQ + 4 * b + 4],
                                            lambda o, s=s, u=u: o[rows_of(s), 32 * u + 16 * s:32 * u + 16 * s + 16]
                                            .rearrange("p (h t) -> p h t", t=DEC_T)))
                        return out

                    old_v = lambda old, new: (lambda u, k, n: old[:, seqs.index(u[0]), k, u[1] * P:(u[1] + 1) * P]
                                              if k < NPAGE else new[u[1]][0:TS, NB, :])
                    cmp_at = lambda u: 2 * SEQ // CMP_S + (u[1] * DEC_B + u[0]) * PAST // CMP_S
                    stage_attend(c, f"c_att_s{half}", sample_groups(2, units, [
                        (q_of, lambda u: k_cmpT[:, cmp_at(u):cmp_at(u) + NCMP_S], NCMP_S, None, None,
                         lambda u, k, n: v_cmp_s[0:NCMP_S, (u[1] * DEC_B + u[0]) * P:(u[1] * DEC_B + u[0] + 1) * P]),
                        (q_of, lambda u: ksT[:, u[1], seqs.index(u[0]), :], PAST, lambda u: projT[:, 10 + u[1], SEQ:T],
                         new_bias, old_v(vs_old, vs_rows)),
                        (q_of, lambda u: kwT[:, u[1], seqs.index(u[0]), :], PAST, lambda u: projT[:, 12 + u[1], SEQ:T],
                         new_bias, old_v(vw_old, vw_rows))], g_of, c_leaves),
                        [(c_out_rows(d["c_w_out"][0], slice(n * P, (n + 1) * P)), KT) for n in range(2)] if half else None)

            stage_out_proj(c, "c_out", d["c_w_out"][0], c_out_rows)
        reuse_semaphores(c)
        channel_mixer(c, 1)
        reuse_semaphores(c)
        stage_store(c, lambda sem, tmp: Norm(c, sem, tmp, 3))


def stage_pages_c(c, name, seqs, ksT, kwT, vs_old, vw_old):
    d = c.dram
    by_page = lambda n: lambda r: d[n][0][bass.ds(r, 1)].rearrange("a p g e -> p (a g e)")
    by_seq = lambda n: lambda b, g: d[n][0, b, g * PAGE:(g + 1) * PAGE].rearrange("p g e -> p (g e)")
    stage_pages(c, name, seqs, [(by_page("cache_c_slc_k"), [(0, 2 * P)], ksT)],
                [(lambda b, g, r: by_page("cache_c_slc_v")(r), lambda b, g: vs_old[:, seqs.index(b), g, :]),
                 (lambda b, g, r: by_seq("state_c_win_v")(b, g), lambda b, g: vw_old[:, seqs.index(b), g, :])])
    stage_turn_rows(c, name + "w", seqs, by_seq("state_c_win_k"), kwT)


def stage_turn_rows(c, name, seqs, src, dst):
    nc = c.nc
    block, sem = stage(c, name)
    land = [sem(f"land{i}") for i in range(4)]
    turned, evac = sem("turned"), sem("evac")
    steps = [(b, g) for b in seqs for g in range(NPAGE)]
    with ExitStack() as tmp:
        ring = tmp.enter_context(nc.sbuf_tensor(f"{name}_ring", [P, 4, 2 * P], F32))
        with block as blk:
            @blk.sync
            def _(sp):
                for n, (b, g) in enumerate(steps):
                    if n >= 4:
                        sp.wait_ge(turned, n - 3)
                    sp.dma_start(ring[:, n % 4, :], src(b, g)).then_inc(land[n % 4], 16)

            @blk.tensor
            def _(pe):
                for n in range(len(steps)):
                    pe.wait_ge(land[n % 4], 16 * (n // 4 + 1))
                    if n >= 4:
                        pe.wait_ge(evac, n - 3)
                    for h in range(2):
                        last = pe.transpose(c.ps[:, n % 4, h * P:(h + 1) * P], ring[:, n % 4, h * P:(h + 1) * P], c.k("ident"))
                    last.then_inc(turned, 1)

            @blk.vector
            def _(dve):
                for n, (b, g) in enumerate(steps):
                    dve.wait_ge(turned, n + 1)
                    dve.tensor_copy(dst[:, :, seqs.index(b), g * PAGE:(g + 1) * PAGE],
                                    c.ps[:, n % 4, 0:2 * P].rearrange("p (h n) -> p h n", n=P)).then_inc(evac, 1)


def channel_mixer(c, layer):
    with ExitStack() as mem:
        h_hi = mem.enter_context(c.nc.sbuf_tensor(f"h_hi{layer}", [P, FT, T], F32R))
        h_lo = mem.enter_context(c.nc.sbuf_tensor(f"h_lo{layer}", [P, FT, T], F32R))
        stage_ffn_up(c, layer, lambda sem, tmp: Norm(c, sem, tmp, layer), h_hi, h_lo)
        stage_ffn_down(c, layer, h_hi, h_lo)


INPUTS = ["x_prompt", "x_sample", "cache_a_k", "cache_a_v", "cache_a_ik", "state_b_conv", "cache_c_cmp_k",
          "cache_c_cmp_v", "cache_c_slc_k", "cache_c_slc_v", "state_c_win_k", "state_c_win_v", "page_table",
          "ab_w_in", "ab_conv_w", "ab_w_out", "c_w_in", "c_cmp_pe_k", "c_cmp_w1_k", "c_cmp_w2_k", "c_cmp_pe_v",
          "c_cmp_w1_v", "c_cmp_w2_v", "c_w_out", "ffn_w_gate", "ffn_w_up", "ffn_w_down", "ln1_g", "ln1_b",
          "ln2_g", "ln2_b"]
_A = (1, 1, SEQ, 2, HD)
_C = (1, 1, SEQ, 4, HD)
_AS = (1, DEC_B, DEC_T, 2, HD)
_CS = (1, DEC_B, DEC_T, 4, HD)
OUTPUTS = {"y_prompt": (1, SEQ, D), "y_sample": (DEC_B, DEC_T, D),
           "a_k_p": _A, "a_v_p": _A, "a_ik_p": (1, 1, SEQ, HD), "b_conv_p": (1, 1, 2, D // 2),
           "c_cmp_k_p": _C, "c_cmp_v_p": _C, "c_slc_k_p": _C, "c_slc_v_p": _C, "c_win_k_p": _C, "c_win_v_p": _C,
           "a_k_s": _AS, "a_v_s": _AS, "a_ik_s": (1, DEC_B, DEC_T, HD), "b_conv_s": (1, DEC_B, 2, D // 2),
           "c_cmp_k_s": _CS, "c_cmp_v_s": _CS, "c_slc_k_s": _CS, "c_slc_v_s": _CS,
           "c_win_k_s": (1, DEC_B, PAST, 4, HD), "c_win_v_s": (1, DEC_B, PAST, 4, HD)}


def kernel(**inputs):
    import concourse.bacc as bacc
    from concourse.bass_utils import run_bass_kernel_spmd as run

    nc = bacc.Bacc("TRN2", target_bir_lowering=False, num_devices=1)
    arrays, dram = {}, {}
    for name in INPUTS:
        a = np.ascontiguousarray(inputs[name])
        arrays[f"in_{name}"] = a
        dram[name] = nc.dram_tensor(f"in_{name}", a.shape, mybir.dt.from_np(a.dtype), kind="ExternalInput").ap()
    arrays["in_const"] = CONST
    dram["const"] = nc.dram_tensor("in_const", CONST.shape, F32, kind="ExternalInput").ap()
    for name, shape in OUTPUTS.items():
        dram[name] = nc.dram_tensor(f"out_{name}", shape, F32, kind="ExternalOutput").ap()
    program(nc, dram)
    r = run(nc, [arrays], core_ids=[0])
    return tuple(r.results[0][f"out_{name}"] for name in OUTPUTS)
```

```python
from contextlib import ExitStack

import numpy as np

import concourse.bass as bass
from concourse import mybir

ALU = mybir.AluOpType
ACT = mybir.ActivationFunctionType
AX_X = mybir.AxisListType.X
F32 = mybir.dt.float32
F32R = mybir.dt.float32r
BF16 = mybir.dt.bfloat16
I32 = mybir.dt.int32

P = 128
D = 1024
KT = D // P
SEQ = 512
NB = SEQ // P
DEC_B = 8
DEC_T = 4
PAST = 256
PAGE = 128
NPAGE = PAST // PAGE
TS = DEC_B * DEC_T
T = SEQ + TS
HALF = T // 2
HD = 64
FF = 2816
FT = FF // P
KCH = FT // 2
TOPK_P = 128
TOPK_S = 65
CMP_W = 32
CMP_S = 16
NCMP_P = (SEQ - CMP_W) // CMP_S + 1
NCMP_S = (PAST + DEC_T - CMP_W) // CMP_S + 1
ALPHA = 4 ** 0.25
EPS = 1e-5
SCALE = HD ** -0.5
BIG = 1e30
TAKEN = -2.0 ** 127
NEW = PAST + TS

A_Q, A_K, A_V, A_IQ, A_IK, A_IW, A_GB, A_GC, A_H = 0, 512, 640, 768, 1024, 1088, 1092, 1604, 2116
C_Q, C_KC, C_VC, C_KS, C_VS, C_KW, C_VW, C_G = 0, 1024, 1280, 1536, 1792, 2048, 2304, 2560


def constants():
    pos = np.concatenate([np.arange(SEQ), PAST + np.tile(np.arange(DEC_T), DEC_B)]).astype(np.float32)
    inv = np.float32(10000.0) ** (-np.arange(HD // 2, dtype=np.float32) / np.float32(HD // 2))
    ang = inv[:, None].astype(np.float32) * pos[None, :]
    cos, sin = np.cos(ang), np.sin(ang)
    parts = {}
    parts["ident"] = np.eye(P)
    parts["cos"] = np.tile(cos, (4, 1))
    parts["sin"] = np.concatenate([-sin, sin, -sin, sin], 0)
    parts["mean"] = np.full((P, P), 1.0 / D)
    q, k = np.arange(P)[:, None], np.arange(P)[None, :]
    parts["causal"] = -1.0 * (k > q)
    row = np.arange(P)
    u, side, head, t = row // 32, row // 16 % 2, row // 4 % 4, row % 4
    new = np.zeros((P, 6, TS))
    pick = np.zeros((P, 6, P))
    for j in range(6):
        b = 4 * j + u if j < 2 else 2 * (j - 2) + u // 2
        tok = np.arange(TS)[None, :]
        new[:, j] = -1.0 * ~((tok // 4 == b[:, None]) & (tok % 4 <= t[:, None]))
        pick[b * 4 + t, j, row] = 1.0
    parts["new"] = new.reshape(P, -1)
    parts["pick"] = pick.reshape(P, -1)
    r = row % 32
    iside, itile = r // 8, r // 4 % 2
    parts["ihead"] = (r < 16)[:, None] * (np.arange(4)[None, :] == (2 * itile + iside)[:, None])
    parts["imix"] = ((r < 16)[:, None] & (u[:, None] == u[None, :]) & (t[:, None] == t[None, :]))
    parts["chead"] = np.arange(16)[None, :] == ((2 * (u % 2) + side) * 4 + head)[:, None]
    cend = np.arange(32)[None, None, :] * CMP_S + CMP_W - 1
    tt = (np.arange(NB)[None, :] * P + row[:, None])[:, :, None]
    parts["cmp"] = (-1.0 * (cend > tt)).reshape(P, -1)
    at, n = {}, 0
    for name, a in parts.items():
        at[name] = (n, n + a.shape[1])
        n += a.shape[1]
    return np.concatenate([a.astype(np.float32) for a in parts.values()], 1), at


CONST, AT = constants()


class Core:
    pass


def setup_memory(nc, ctx, dram):
    c = Core()
    c.nc, c.dram = nc, dram
    c.n_stage = 0
    sb = lambda n, s, d=F32: ctx.enter_context(nc.sbuf_tensor(n, s, d))
    c.sems = []
    c.const = sb("tables", [P, CONST.shape[1]])
    c.causal_bf = sb("causal_bf", [P, P], BF16)
    c.cmp_bf = sb("cmp_bf", [P, NB * 32], BF16)
    c.new_bf = sb("new_bf", [P, 6 * TS], BF16)
    c.ident_big = sb("ident_big", [P, P], BF16)
    c.xT = sb("xT", [P, KT, T])
    c.x_sum = sb("x_sum", [P, T])
    c.x_hi = sb("x_hi", [P, KT, T], F32R)
    c.x_lo = sb("x_lo", [P, KT, T], F32R)
    c.ln_gb = sb("ln_gb", [P, 4, 2, KT])
    c.w_raw = sb("w_raw", [P, 2, KCH, P])
    c.w_hi = sb("w_hi", [P, 2, KCH, P], F32R)
    c.w_lo = sb("w_lo", [P, 2, KCH, P], F32R)
    c.ps = ctx.enter_context(nc.psum_tensor("ps", [P, 8, 512], F32))
    c.k = lambda name: c.const[:, AT[name][0]:AT[name][1]]
    return c


def stage(c, name):
    c.n_stage += 1
    tag = f"{name}{c.n_stage}"

    def sem(signal):
        c.sems.append(c.nc.alloc_semaphore(name=f"{tag}_{signal}"))
        return c.sems[-1]
    return c.nc.Block(tag), sem


def reuse_semaphores(c):
    c.nc.clear_and_free_semaphores(c.sems)
    c.sems = []
    c.nc.all_engine_barrier()


def halves(ap):
    return ap.rearrange("p (h n) -> p h n", h=2)



def load_unit(c, sp, slot, pieces, raw_in):
    for place, src in pieces:
        sp.dma_start(place(c.w_raw[:, slot]), src).then_inc(raw_in, 16)


class Ahead:

    def __init__(self, c, sem, units):
        self.c, self.units = c, units
        self.raw_in = [sem("ahead_raw0"), sem("ahead_raw1")]
        self.hi_made = sem("ahead_hi")

    def load(self, sp):
        for slot, (pieces, _) in enumerate(self.units):
            load_unit(self.c, sp, slot, pieces, self.raw_in[slot])

    def split_hi(self, act, slot):
        pieces, kt = self.units[slot]
        act.wait_ge(self.raw_in[slot], 16 * len(pieces))
        split_hi(self.c, act, slot, kt).then_inc(self.hi_made, 1)

    def split_lo(self, dve, slot):
        dve.wait_ge(self.hi_made, slot + 1)
        split_lo(self.c, dve, slot, self.units[slot][1])


def pe_first_unit(c, pe, start):
    for k in range(KT):
        start.wait_tile(pe, k)
        for h in range(2):
            cols = slice(h * HALF, (h + 1) * HALF)
            out = c.ps[:, h, 0:HALF]
            pe.matmul(out, c.w_hi[:, 0, k, :], c.x_hi[:, k, cols], start=k == 0, stop=False)
            pe.matmul(out, c.w_hi[:, 0, k, :], c.x_lo[:, k, cols], start=False, stop=False)
            last = pe.matmul(out, c.w_lo[:, 0, k, :], c.x_hi[:, k, cols], start=False, stop=k == KT - 1)
    return last


def pe_unit(c, pe, slot, kt, k0, x_hi, x_lo, bank, start, stop):
    for h in range(2):
        cols = slice(h * HALF, (h + 1) * HALF)
        out = c.ps[:, bank + h, 0:HALF]
        for k in range(kt):
            first, end = start and k == 0, stop and k == kt - 1
            pe.matmul(out, c.w_hi[:, slot, k, :], x_hi[:, k0 + k, cols], start=first, stop=False)
            pe.matmul(out, c.w_hi[:, slot, k, :], x_lo[:, k0 + k, cols], start=False, stop=False)
            last = pe.matmul(out, c.w_lo[:, slot, k, :], x_hi[:, k0 + k, cols], start=False, stop=end)
    return last


def split_hi(c, act, slot, kt, scale=1.0):
    return act.activation(c.w_hi[:, slot, 0:kt, :], c.w_raw[:, slot, 0:kt, :], ACT.Copy, scale=scale)


def split_lo(c, dve, slot, kt, scale=1.0):
    if scale != 1.0:
        return dve.scalar_tensor_tensor(c.w_lo[:, slot, 0:kt, :], c.w_raw[:, slot, 0:kt, :], scale,
                                        c.w_hi[:, slot, 0:kt, :].bitcast(F32), ALU.mult, ALU.subtract)
    return dve.tensor_tensor(c.w_lo[:, slot, 0:kt, :], c.w_raw[:, slot, 0:kt, :],
                             c.w_hi[:, slot, 0:kt, :].bitcast(F32), ALU.subtract)


def w_rows(w, cols, k0=0, kt=KT):
    return w[k0 * P:(k0 + kt) * P, cols].rearrange("(k p) n -> p k n", p=P)


def slab_pieces(w, slab):
    return [(lambda r, d0=d0, n=n: r[:, 0:KT, d0:d0 + n], w_rows(w, slice(col, col + n))) for d0, col, n in slab]


def up_pieces(w, cols):
    return [(lambda r: r[:, 0:KT, :], w_rows(w, cols))]


def down_pieces(w, s, cols):
    return [(lambda r: r[:, :, :], w_rows(w, cols, s * KCH, KCH))]



class Load:

    def __init__(self, c, sem, tmp):
        self.c = c
        self.x_nat = tmp.enter_context(c.nc.sbuf_tensor("x_nat", [P, NB + 1, D], F32))
        self.ln_nat = tmp.enter_context(c.nc.sbuf_tensor("ln_nat", [64, P], F32))
        self.ident_in, self.const_in, self.ln_in, self.turned, self.evac, self.hi, self.ln_t, self.ln_e = (sem(s) for s in
            ("ident_in", "const_in", "ln_in", "turned", "evac", "x_hi_set", "ln_turned", "ln_evac"))
        self.lo = [sem("x_lo_set_dve"), sem("x_lo_set_pool")]
        self.x_in = [sem(f"x_in{i}") for i in range(KT // 2)]

    def sync(self, sp):
        c = self.c
        sp.dma_start(c.const[:, 0:P], c.dram["const"][:, 0:P]).then_inc(self.ident_in, 16)
        for i in range(KT // 2):
            cols = slice(2 * i * P, 2 * (i + 1) * P)
            sp.dma_start(self.x_nat[:, 0:NB, cols], c.dram["x_prompt"][0][:, cols].rearrange("(b p) d -> p b d", p=P)).then_inc(self.x_in[i], 16)
            sp.dma_start(self.x_nat[0:TS, NB, cols], c.dram["x_sample"].rearrange("b t d -> (b t) d")[:, cols]).then_inc(self.x_in[i], 16)

    def sync_late(self, sp):
        c = self.c
        sp.dma_start(c.const[:, P:], c.dram["const"][:, P:]).then_inc(self.const_in, 16)
        for i, name in enumerate(("ln1_g", "ln1_b", "ln2_g", "ln2_b")):
            sp.dma_start(self.ln_nat[16 * i:16 * i + 16, :], c.dram[name].rearrange("l (k p) -> (l k) p", p=P)).then_inc(self.ln_in, 16)

    def pe(self, pe):
        c = self.c
        pe.wait_ge(self.ident_in, 16)
        for k in range(KT):
            pe.wait_ge(self.x_in[k // 2], 32)
            if k >= 3:
                pe.wait_ge(self.evac, k - 2)
            b0 = 2 + 2 * (k % 3)
            for b in range(NB):
                pe.transpose(c.ps[:, b0, b * P:(b + 1) * P], self.x_nat[:, b, k * P:(k + 1) * P], c.k("ident"))
            pe.transpose(c.ps[:, b0 + 1, 0:TS], self.x_nat[0:TS, NB, k * P:(k + 1) * P],
                         c.k("ident")[0:TS, 0:TS]).then_inc(self.turned, 1)

    def pe_late(self, pe, bank):
        pe.wait_ge(self.ln_in, 64)
        pe.transpose(self.c.ps[:, bank, 0:64], self.ln_nat[:, :], self.c.k("ident")[0:64, 0:64]).then_inc(self.ln_t, 1)
        pe.wait_ge(self.ln_e, 1)

    def dve(self, dve, split):
        c = self.c
        for k in range(KT):
            dve.wait_ge(self.turned, k + 1)
            b0 = 2 + 2 * (k % 3)
            dve.tensor_copy(c.xT[:, k, 0:SEQ], c.ps[:, b0, :])
            dve.tensor_copy(c.xT[:, k, SEQ:T], c.ps[:, b0 + 1, 0:TS]).then_inc(self.evac, 1)
            if k % 2 == 1:
                self.low(dve, k - 1)
            if k in (4, 6):
                split((k - 4) // 2)
        dve.wait_ge(self.const_in, 16)

    def dve_late(self, dve, bank):
        c = self.c
        dve.wait_ge(self.ln_t, 1)
        dve.tensor_copy(c.ln_gb[:, :, :, :].rearrange("p (w l) g k -> p w g l k", w=2),
                        c.ps[:, bank, 0:64].rearrange("p (w g l k) -> p w g l k", w=2, g=2, l=2)).then_inc(self.ln_e, 1)

    def low(self, eng, k):
        c = self.c
        eng.wait_ge(self.hi, k + 1)
        eng.tensor_tensor(c.x_lo[:, k, :], c.xT[:, k, :], c.x_hi[:, k, :].bitcast(F32), ALU.subtract).then_inc(self.lo[k % 2], 1)

    def act(self, act, split):
        for k in range(KT):
            act.wait_ge(self.evac, k + 1)
            act.activation(self.c.x_hi[:, k, :], self.c.xT[:, k, :], ACT.Copy).then_inc(self.hi, 1)
            if k in (3, 5):
                split((k - 3) // 2)

    def pool(self, pool):
        c = self.c
        for k in range(1, KT, 2):
            self.low(pool, k)
        pool.wait_ge(self.const_in, 16)
        pool.tensor_copy(c.causal_bf[:, :], c.k("causal"))
        pool.tensor_copy(c.cmp_bf[:, :], c.k("cmp"))
        pool.tensor_copy(c.new_bf[:, :], c.k("new"))
        pool.tensor_scalar(c.ident_big[:, :], c.k("ident"), BIG, None, ALU.mult)

    def wait_tile(self, pe, k):
        pe.wait_ge(self.lo[k % 2], k // 2 + 1)


class Norm:

    def __init__(self, c, sem, tmp, which):
        self.c, self.which = c, which
        sb = lambda n, s: tmp.enter_context(c.nc.sbuf_tensor(f"norm{which}_{n}", s, F32))
        self.sq, self.std, self.rstd, self.eps = sb("sq", [P, 2, T]), sb("std", [P, T]), sb("rstd", [P, T]), sb("eps", [P, 1])
        self.ready = sb("ready", [P, 1])
        self.mean_done, self.centred, self.squared, self.var_done, self.rooted, self.inverted, self.scaled, self.eps_set = (
            sem(s) for s in ("mean_done", "centred", "squared", "var_done", "rooted", "inverted", "scaled", "eps_set"))
        self.hi, self.lo = sem("x_hi_set"), [sem("x_lo_set_dve"), sem("x_lo_set_pool")]
        self.done = sem("x_done")

    def sync(self, sp):
        pass

    sync_late = sync

    def pe_late(self, eng, bank):
        pass

    dve_late = pe_late

    def pe(self, pe):
        c = self.c
        for h in range(2):
            last = pe.matmul(c.ps[:, 4 + h, 0:HALF], c.k("mean"), c.x_sum[:, h * HALF:(h + 1) * HALF], start=True, stop=True)
        last.then_inc(self.mean_done, 1)
        for k in range(KT):
            pe.wait_ge(self.squared, k + 1)
            for h in range(2):
                last = pe.matmul(c.ps[:, 6 + h, 0:HALF], c.k("mean"), self.sq[:, k % 2, h * HALF:(h + 1) * HALF],
                                 start=(k == 0), stop=(k == KT - 1))
            last.then_inc(self.var_done, 1)

    def dve(self, dve, split=None):
        c = self.c
        dve.memset(self.eps[:, :], EPS).then_inc(self.eps_set, 1)
        dve.wait_ge(self.mean_done, 1)
        for k in range(KT):
            dve.tensor_tensor(halves(c.xT[:, k, :]), halves(c.xT[:, k, :]), c.ps[:, 4:6, 0:HALF], ALU.subtract).then_inc(self.centred, 1)
        if split:
            split(0)
            split(1)
        dve.wait_ge(self.rooted, 1)
        dve.reciprocal(self.rstd[:, :], self.std[:, :]).then_inc(self.inverted, 1)
        dve.wait_ge(self.inverted, 1)
        dve.wait_ge(self.squared, KT)
        for k in range(KT):
            dve.scalar_tensor_tensor(c.xT[:, k, :], c.xT[:, k, :], c.ln_gb[:, self.which, 0, k:k + 1], self.rstd[:, :],
                                     ALU.mult, ALU.mult).then_inc(self.scaled, 1)
            if split and k >= 2 and k % 2 == 0:
                self.low(dve, k - 2)
        if split:
            self.low(dve, KT - 2)

    def low(self, dve, k):
        c = self.c
        dve.wait_ge(self.hi, k + 1)
        dve.scalar_tensor_tensor(c.x_lo[:, k, :], c.xT[:, k, :], c.ln_gb[:, self.which, 1, k:k + 1],
                                 c.x_hi[:, k, :].bitcast(F32), ALU.add, ALU.subtract).then_inc(self.lo[0], 1)

    def wait_tile(self, pe, k):
        pe.wait_ge(self.lo[k % 2], k // 2 + 1)

    def pool(self, pool):
        c = self.c
        for k in range(1, KT, 2):
            pool.wait_ge(self.done, k // 2 + 1)
            pool.tensor_tensor(c.x_lo[:, k, :], c.xT[:, k, :], c.x_hi[:, k, :].bitcast(F32), ALU.subtract).then_inc(self.lo[1], 1)

    def act(self, act, split=None):
        c = self.c
        act.wait_ge(self.eps_set, 1)
        act.activation(self.ready[:, :], self.eps[:, :], ACT.Sqrt)
        for k in range(KT):
            act.wait_ge(self.centred, k + 1)
            if k >= 2:
                act.wait_ge(self.var_done, k - 1)
            act.activation(self.sq[:, k % 2, :], c.xT[:, k, :], ACT.Square).then_inc(self.squared, 1)
            if split and k in (4, 6):
                split((k - 4) // 2)
        act.wait_ge(self.var_done, KT)
        act.activation(halves(self.std[:, :]), c.ps[:, 6:8, 0:HALF], ACT.Sqrt, bias=self.eps[:, :]).then_inc(self.rooted, 1)
        shift = lambda out, k: act.activation(out, c.xT[:, k, :], ACT.Identity, bias=c.ln_gb[:, self.which, 1, k:k + 1])
        if split:
            for k in range(KT + 1):
                if k < KT:
                    act.wait_ge(self.scaled, k + 1)
                    shift(c.x_hi[:, k, :], k).then_inc(self.hi, 1)
                if k >= 2 and k % 2 == 0:
                    act.wait_ge(self.hi, k)
                    shift(c.xT[:, k - 1, :], k - 1).then_inc(self.done, 1)
            for k in range(0, KT, 2):
                self.wait_tile(act, k)
                shift(c.xT[:, k, :], k).then_inc(self.done, 1)
        else:
            for k in range(KT):
                act.wait_ge(self.scaled, k + 1)
                shift(c.xT[:, k, :], k).then_inc(self.done, 1)


def stage_in_proj(c, name, begin, w, n_q, rope_slabs, plain_slabs, projT):
    nc = c.nc
    block, sem = stage(c, name)
    slabs = rope_slabs + plain_slabs
    n_rope = len(rope_slabs)
    raw_loaded = [sem("raw0"), sem("raw1")]
    hi_made, lo_made, unit_used = sem("hi_made"), sem("lo_made"), sem("unit_used")
    swapped, cosed, sined, summed = sem("swapped"), sem("cosed"), sem("sined"), sem("summed")
    with ExitStack() as tmp:
        swap = tmp.enter_context(nc.sbuf_tensor(f"{name}_swap", [P, 2, T], F32))
        n_dma = [0, 0]
        loads = []
        for n, slab in enumerate(slabs):
            n_dma[n % 2] += len(slab)
            loads.append(16 * n_dma[n % 2])
        start = begin(sem, tmp)
        with block as blk:
            @blk.sync
            def _(sp):
                start.sync(sp)
                for n, slab in enumerate(slabs):
                    if n == 2:
                        start.sync_late(sp)
                    if n >= 2:
                        sp.wait_ge(hi_made, n - 1)
                        sp.wait_ge(lo_made, n - 1)
                    load_unit(c, sp, n % 2, slab_pieces(w, slab), raw_loaded[n % 2])

            @blk.gpsimd
            def _(pool):
                start.pool(pool)

            def psum_of(n):
                return c.ps[:, 2 * (n % 4):2 * (n % 4) + 2, 0:HALF]

            @blk.scalar
            def _(act):
                def hi(n):
                    act.wait_ge(raw_loaded[n % 2], loads[n])
                    if n >= 2:
                        act.wait_ge(unit_used, n - 1)
                    split_hi(c, act, n % 2, KT, SCALE if n < n_q else 1.0).then_inc(hi_made, 1)

                start.act(act, hi)
                for n in range(len(slabs)):
                    if 2 <= n + 1 < len(slabs):
                        hi(n + 1)
                    act.wait_ge(unit_used, n + 1)
                    if n < n_rope:
                        if n >= 2:
                            act.wait_ge(summed, n - 1)
                        for qd in range(4):
                            o = 32 * (qd ^ 1)
                            last = act.activation(halves(swap[32 * qd:32 * qd + 32, n % 2, :]),
                                                  psum_of(n)[o:o + 32], ACT.Copy)
                        last.then_inc(swapped, 1)
                    else:
                        act.activation(halves(projT[:, n, :]), psum_of(n), ACT.Copy).then_inc(swapped, 1)

            @blk.vector
            def _(dve):
                def lo(n):
                    dve.wait_ge(hi_made, n + 1)
                    split_lo(c, dve, n % 2, KT, SCALE if n < n_q else 1.0).then_inc(lo_made, 1)

                start.dve(dve, lo)
                start.dve_late(dve, 6)
                for n in range(len(slabs)):
                    if 2 <= n + 1 < len(slabs):
                        lo(n + 1)
                    if n < n_rope:
                        dve.wait_ge(swapped, n + 1)
                        dve.tensor_tensor(halves(projT[:, n, :]), psum_of(n), halves(c.k("cos")), ALU.mult).then_inc(cosed, 1)
                        dve.tensor_tensor(swap[:, n % 2, :], swap[:, n % 2, :], c.k("sin"), ALU.mult).then_inc(sined, 1)
                        dve.wait_ge(cosed, n + 1)
                        dve.wait_ge(sined, n + 1)
                        dve.tensor_tensor(projT[:, n, :], projT[:, n, :], swap[:, n % 2, :], ALU.add).then_inc(summed, 1)

            @blk.tensor
            def _(pe):
                start.pe(pe)
                pe.wait_ge(lo_made, 1)
                pe_first_unit(c, pe, start).then_inc(unit_used, 1)
                start.pe_late(pe, 6)
                for n in range(1, len(slabs)):
                    pe.wait_ge(lo_made, n + 1)
                    if n >= 4:
                        pe.wait_ge(swapped, n - 3)
                        pe.wait_ge(cosed, min(n - 3, n_rope))
                    pe_unit(c, pe, n % 2, KT, 0, c.x_hi, c.x_lo, 2 * (n % 4), True, True).then_inc(unit_used, 1)


def stage_out_proj(c, name, w, row_of):
    block, sem = stage(c, name)
    raw_loaded = [sem("raw0"), sem("raw1")]
    hi_made, lo_made, unit_used, added = sem("hi_made"), sem("lo_made"), sem("unit_used"), sem("added")
    x_summed = sem("x_summed")
    with block as blk:
        @blk.sync
        def _(sp):
            for n in range(2, KT):
                sp.wait_ge(hi_made, n - 1)
                sp.wait_ge(lo_made, n - 1)
                load_unit(c, sp, n % 2, row_of(w, slice(n * P, (n + 1) * P)), raw_loaded[n % 2])
        n_piece = len(row_of(w, slice(0, P)))

        @blk.scalar
        def _(act):
            act.sem_inc(hi_made, 2)
            for n in range(2, KT):
                act.wait_ge(raw_loaded[n % 2], 16 * n_piece * (n // 2))
                act.wait_ge(unit_used, n - 1)
                split_hi(c, act, n % 2, KT).then_inc(hi_made, 1)

        @blk.vector
        def _(dve):
            def lo(n):
                dve.wait_ge(hi_made, n + 1)
                split_lo(c, dve, n % 2, KT).then_inc(lo_made, 1)

            dve.sem_inc(lo_made, 2)
            for n in range(KT):
                if 2 <= n + 1 < KT:
                    lo(n + 1)
                dve.wait_ge(unit_used, n + 1)
                dve.scalar_tensor_tensor(halves(c.xT[:, n, :]), halves(c.xT[:, n, :]), ALPHA,
                                         c.ps[:, 2 * (n % 4):2 * (n % 4) + 2, 0:HALF], ALU.mult, ALU.add).then_inc(added, 1)

        @blk.gpsimd
        def _(pool):
            for n in range(KT):
                pool.wait_ge(added, n + 1)
                if n == 0:
                    pool.tensor_copy(c.x_sum[:, :], c.xT[:, 0, :]).then_inc(x_summed, 1)
                else:
                    pool.wait_ge(x_summed, n)
                    pool.tensor_tensor(c.x_sum[:, :], c.x_sum[:, :], c.xT[:, n, :], ALU.add).then_inc(x_summed, 1)

        @blk.tensor
        def _(pe):
            for n in range(KT):
                pe.wait_ge(lo_made, n + 1)
                if n >= 4:
                    pe.wait_ge(added, n - 3)
                pe_unit(c, pe, n % 2, KT, 0, c.x_hi, c.x_lo, 2 * (n % 4), True, True).then_inc(unit_used, 1)


def stage_ffn_up(c, layer, begin, h_hi, h_lo):
    nc = c.nc
    wg, wu = c.dram["ffn_w_gate"][layer], c.dram["ffn_w_up"][layer]
    block, sem = stage(c, "up")
    g_raw, u_raw = sem("gate_raw_in"), sem("up_raw_in")
    g_hi, u_hi, g_lo, u_lo = sem("gate_hi"), sem("up_hi"), sem("gate_lo"), sem("up_lo")
    g_used, u_used = sem("gate_used"), sem("up_used")
    ahead = Ahead(c, sem, [(down_pieces(c.dram["ffn_w_down"][layer], s, slice(0, P)), KCH) for s in range(2)])
    silu, prod, h_top, h_rest = sem("silu"), sem("prod"), sem("h_top"), sem("h_rest")
    with ExitStack() as tmp:
        act_g = tmp.enter_context(nc.sbuf_tensor(f"silu{layer}", [P, T], F32))
        h_f = tmp.enter_context(nc.sbuf_tensor(f"h_f{layer}", [P, T], F32))
        start = begin(sem, tmp)
        with block as blk:
            @blk.sync
            def _(sp):
                start.sync(sp)
                load_unit(c, sp, 0, up_pieces(wg, slice(0, P)), g_raw)
                load_unit(c, sp, 1, up_pieces(wu, slice(0, P)), u_raw)
                with sp.Fori(1, FT) as f:
                    cols = bass.ds(f * P, P)
                    sp.wait_ge(g_lo, f)
                    load_unit(c, sp, 0, up_pieces(wg, cols), g_raw)
                    sp.wait_ge(u_lo, f)
                    load_unit(c, sp, 1, up_pieces(wu, cols), u_raw)
                sp.wait_ge(g_lo, FT)
                sp.wait_ge(u_lo, FT)
                ahead.load(sp)

            @blk.scalar
            def _(act):
                def gate_hi(f, first=False):
                    act.wait_ge(g_raw, 16 * f + 16)
                    if not first:
                        act.wait_ge(g_used, f)
                    split_hi(c, act, 0, KT).then_inc(g_hi, 1)

                def up_hi(f, first=False):
                    act.wait_ge(u_raw, 16 * f + 16)
                    if not first:
                        act.wait_ge(u_used, f)
                    split_hi(c, act, 1, KT).then_inc(u_hi, 1)

                def gate_act(f, first=False):
                    act.wait_ge(g_used, f + 1)
                    if not first:
                        act.wait_ge(prod, f)
                    act.activation(halves(act_g[:, :]), c.ps[:, 0:2, 0:HALF], ACT.Silu).then_inc(silu, 1)

                def top(f):
                    act.wait_ge(prod, f + 1)
                    act.activation(h_hi[:, bass.ds(f, 1), :], h_f[:, :].rearrange("p (a n) -> p a n", a=1),
                                   ACT.Copy).then_inc(h_top, 1)

                start.act(act, lambda n: (gate_hi, up_hi)[n](0, True))
                gate_hi(1)
                gate_act(0, True)
                up_hi(1)
                top(0)
                with act.Fori(1, FT - 1) as f:
                    gate_hi(f + 1)
                    gate_act(f)
                    up_hi(f + 1)
                    top(f)
                gate_act(FT - 1)
                ahead.split_hi(act, 0)
                top(FT - 1)
                ahead.split_hi(act, 1)

            @blk.vector
            def _(dve):
                def gate_lo(f):
                    dve.wait_ge(g_hi, f + 1)
                    split_lo(c, dve, 0, KT).then_inc(g_lo, 1)

                def up_lo(f):
                    dve.wait_ge(u_hi, f + 1)
                    split_lo(c, dve, 1, KT).then_inc(u_lo, 1)

                def mul(f, first=False):
                    if not first:
                        dve.wait_ge(h_rest, f)
                    dve.wait_ge(silu, f + 1)
                    dve.wait_ge(u_used, f + 1)
                    dve.tensor_tensor(halves(h_f[:, :]), halves(act_g[:, :]), c.ps[:, 2:4, 0:HALF], ALU.mult).then_inc(prod, 1)

                def low(f):
                    dve.wait_ge(h_top, f + 1)
                    at = bass.ds(f, 1)
                    dve.tensor_tensor(h_lo[:, at, :], h_f[:, :].rearrange("p (a n) -> p a n", a=1),
                                      h_hi[:, at, :].bitcast(F32), ALU.subtract).then_inc(h_rest, 1)

                start.dve(dve, lambda n: (gate_lo, up_lo)[n](0))

                def tile(f, first=False):
                    gate_lo(f + 1)
                    mul(f, first)
                    up_lo(f + 1)
                    low(f)

                tile(0, True)
                with dve.Fori(1, FT - 1) as f:
                    tile(f)
                ahead.split_lo(dve, 0)
                mul(FT - 1)
                low(FT - 1)
                ahead.split_lo(dve, 1)

            @blk.gpsimd
            def _(pool):
                start.pool(pool)

            @blk.tensor
            def _(pe):
                def tile(f, first=False):
                    pe.wait_ge(g_lo, f + 1)
                    if first:
                        pe_first_unit(c, pe, start).then_inc(g_used, 1)
                    else:
                        pe.wait_ge(silu, f)
                        pe_unit(c, pe, 0, KT, 0, c.x_hi, c.x_lo, 0, True, True).then_inc(g_used, 1)
                    pe.wait_ge(u_lo, f + 1)
                    if not first:
                        pe.wait_ge(prod, f)
                    pe_unit(c, pe, 1, KT, 0, c.x_hi, c.x_lo, 2, True, True).then_inc(u_used, 1)

                start.pe(pe)
                tile(0, True)
                with pe.Fori(1, FT) as f:
                    tile(f)


def stage_ffn_down(c, layer, h_hi, h_lo):
    wd = c.dram["ffn_w_down"][layer]
    block, sem = stage(c, "down")
    raw = [sem("raw_a_in"), sem("raw_b_in")]
    hi = [sem("hi_a"), sem("hi_b")]
    lo = [sem("lo_a"), sem("lo_b")]
    used = [sem("used_a"), sem("used_b")]
    added, x_summed = sem("added"), sem("x_summed")
    with block as blk:
        @blk.gpsimd
        def _(pool):
            pool.wait_ge(added, 1)
            pool.tensor_copy(c.x_sum[:, :], c.xT[:, 0, :]).then_inc(x_summed, 1)
            with pool.Fori(1, KT) as n:
                pool.wait_ge(added, n + 1)
                pool.wait_ge(x_summed, n)
                line = c.x_sum[:, :].rearrange("p (a n) -> p a n", a=1)
                pool.tensor_tensor(line, line, c.xT[:, bass.ds(n, 1), :], ALU.add).then_inc(x_summed, 1)

        @blk.sync
        def _(sp):
            with sp.Fori(1, KT) as n:
                for s in range(2):
                    sp.wait_ge(lo[s], n)
                    load_unit(c, sp, s, down_pieces(wd, s, bass.ds(n * P, P)), raw[s])

        @blk.scalar
        def _(act):
            act.sem_inc(hi[0], 1)
            act.sem_inc(hi[1], 1)
            with act.Fori(1, KT) as n:
                for s in range(2):
                    act.wait_ge(raw[s], 16 * n)
                    act.wait_ge(used[s], n)
                    split_hi(c, act, s, KCH).then_inc(hi[s], 1)

        @blk.vector
        def _(dve):
            def split(n, s):
                dve.wait_ge(hi[s], n + 1)
                split_lo(c, dve, s, KCH).then_inc(lo[s], 1)

            def add(n, bank):
                dve.wait_ge(used[1], n + 1)
                at = bass.ds(n, 1)
                x = c.xT[:, at, :].rearrange("p a (h n) -> p (a h) n", h=2)
                dve.scalar_tensor_tensor(x, x, ALPHA, c.ps[:, bank:bank + 2, 0:HALF], ALU.mult, ALU.add).then_inc(added, 1)

            dve.sem_inc(lo[0], 1)
            dve.sem_inc(lo[1], 1)

            def pair(n):
                for j in range(2):
                    split(n + j + 1, 0)
                    split(n + j + 1, 1)
                    add(n + j, 2 * j)

            with dve.Fori(0, KT - 2, 2) as n:
                pair(n)
            split(KT - 1, 0)
            split(KT - 1, 1)
            add(KT - 2, 0)
            add(KT - 1, 2)

        @blk.tensor
        def _(pe):
            def tile(n, bank, first=False):
                pe.wait_ge(lo[0], n + 1)
                if not first:
                    pe.wait_ge(added, n - 1)
                pe_unit(c, pe, 0, KCH, 0, h_hi, h_lo, bank, True, False).then_inc(used[0], 1)
                pe.wait_ge(lo[1], n + 1)
                pe_unit(c, pe, 1, KCH, KCH, h_hi, h_lo, bank, False, True).then_inc(used[1], 1)
            tile(0, 0, True)
            tile(1, 2, True)
            with pe.Fori(2, KT, 2) as n:
                tile(n, 0)
                tile(n + 1, 2)


def stage_store(c, begin):
    nc = c.nc
    block, sem = stage(c, "store")
    turned, evac, evac_s, out = sem("turned"), sem("evac"), sem("evac_s"), sem("out")
    with ExitStack() as tmp:
        y = tmp.enter_context(nc.sbuf_tensor("y_nat", [P, NB + 1, D], F32))
        start = begin(sem, tmp)
        with block as blk:
            @blk.tensor
            def _(pe):
                start.pe(pe)
                for k in range(KT):
                    pe.wait_ge(start.done, k + 1)
                    if k >= 2:
                        pe.wait_ge(evac, k - 1)
                        pe.wait_ge(evac_s, k - 1)
                    b0 = 2 * (k % 2)
                    for b in range(NB):
                        pe.transpose(c.ps[:, b0, b * P:(b + 1) * P], c.xT[:, k, b * P:(b + 1) * P], c.k("ident"))
                    pe.transpose(c.ps[0:TS, b0 + 1, 0:P], c.xT[:, k, SEQ:T], c.k("ident")).then_inc(turned, 1)

            @blk.vector
            def _(dve):
                start.dve(dve)
                for k in range(KT):
                    dve.wait_ge(turned, k + 1)
                    dve.tensor_copy(y[:, 0:NB, k * P:(k + 1) * P], c.ps[:, 2 * (k % 2), :].rearrange("p (b n) -> p b n", b=NB)).then_inc(evac, 1)

            @blk.scalar
            def _(act):
                start.act(act)
                for k in range(KT):
                    act.wait_ge(turned, k + 1)
                    act.activation(y[0:TS, NB, k * P:(k + 1) * P], c.ps[0:TS, 2 * (k % 2) + 1, 0:P], ACT.Copy).then_inc(evac_s, 1)

            @blk.sync
            def _(sp):
                for i in range(KT // 2):
                    cols = slice(2 * i * P, 2 * (i + 1) * P)
                    sp.wait_ge(evac, 2 * i + 2)
                    sp.dma_start(c.dram["y_prompt"][0][:, cols].rearrange("(b p) d -> p b d", p=P), y[:, 0:NB, cols]).then_inc(out, 16)
                    sp.wait_ge(evac_s, 2 * i + 2)
                    sp.dma_start(c.dram["y_sample"].rearrange("b t d -> (b t) d")[:, cols], y[0:TS, NB, cols]).then_inc(out, 16)
                sp.wait_ge(out, 16 * KT)



def stage_rows(c, name, projT, items, fetch=None):
    nc = c.nc
    block, sem = stage(c, name)
    turned, evac_p, evac_s = sem("turned"), sem("evac_p"), sem("evac_s")
    n_ring = min(4, len(items))
    out = [sem(f"out{i}") for i in range(n_ring)]
    with ExitStack() as tmp:
        ring = tmp.enter_context(nc.sbuf_tensor(f"{name}_rows", [P, n_ring, NB + 1, P], F32))
        dst = [ring[:, n % n_ring] if keep is None else keep for n, (_, keep, _) in enumerate(items)]
        sent, before = [0] * n_ring, []
        for n, (_, _, stores) in enumerate(items):
            before.append(sent[n % n_ring])
            sent[n % n_ring] += 32 * len(stores)
        with block as blk:
            @blk.tensor
            def _(pe):
                for n, (slab, _, _) in enumerate(items):
                    if n >= 3:
                        pe.wait_ge(evac_p, n - 2)
                        pe.wait_ge(evac_s, n - 2)
                    bank = 2 * (n % 3)
                    for b in range(NB):
                        pe.transpose(c.ps[:, bank, b * P:(b + 1) * P], projT[:, slab, b * P:(b + 1) * P], c.k("ident"))
                    pe.transpose(c.ps[0:TS, bank + 1, 0:P], projT[:, slab, SEQ:T], c.k("ident")).then_inc(turned, 1)

            @blk.vector
            def _(dve):
                for n in range(len(items)):
                    dve.wait_ge(turned, n + 1)
                    if n >= n_ring and before[n]:
                        dve.wait_ge(out[n % n_ring], before[n])
                    dve.tensor_copy(dst[n][:, 0:NB, :], c.ps[:, 2 * (n % 3), :].rearrange("p (b n) -> p b n", b=NB)).then_inc(evac_p, 1)

            @blk.scalar
            def _(act):
                for n in range(len(items)):
                    act.wait_ge(turned, n + 1)
                    if n >= n_ring and before[n]:
                        act.wait_ge(out[n % n_ring], before[n])
                    act.activation(dst[n][0:TS, NB, :], c.ps[0:TS, 2 * (n % 3) + 1, 0:P], ACT.Copy).then_inc(evac_s, 1)

            if fetch:
                @blk.gpsimd
                def _(pool):
                    fetch(pool, sem)

            @blk.sync
            def _(sp):
                for n, (_, _, stores) in enumerate(items):
                    if stores:
                        sp.wait_ge(evac_p, n + 1)
                        sp.wait_ge(evac_s, n + 1)
                    for col, prompt, sample in stores:
                        w = prompt.shape[-1]
                        sp.dma_start(prompt.rearrange("(b p) n -> p b n", p=P), dst[n][:, 0:NB, col:col + w]).then_inc(out[n % n_ring], 16)
                        sp.dma_start(sample, dst[n][0:TS, NB, col:col + w]).then_inc(out[n % n_ring], 16)
                for s in range(n_ring):
                    if sent[s]:
                        sp.wait_ge(out[s], sent[s])



class Tile:

    def __init__(self, scores, biases, n_keys, values, mover):
        self.scores, self.biases, self.n_keys, self.values, self.mover = scores, biases, n_keys, values, mover
        self.chunks = [(c0, min(P, n_keys - c0)) for c0 in range(0, n_keys, P)]


class Group:

    def __init__(self, tiles, n_seg, n_br, gate, leaves):
        self.tiles, self.n_seg, self.n_br, self.gate, self.leaves = tiles, n_seg, n_br, gate, leaves


TURN = 3
VALUE = 5
S_RING, P_RING, PT_RING = 3, 4, 3


def stage_attend(c, name, groups, ahead_units=None, fetch=None):
    nc = c.nc
    block, sem = stage(c, name)
    scored, peaked, scaled, exped, turned, valued = (sem(s) for s in
        ("scored", "peaked", "scaled", "exped", "turned", "valued"))
    moved = {"act": sem("moved_act"), "dve": sem("moved_dve")}
    guarded, inverted, weighed, mixing, mixed, back, top, rest = (sem(s) for s in
        ("guarded", "inverted", "weighed", "mixing", "mixed", "back", "top", "rest"))
    ahead = Ahead(c, sem, ahead_units) if ahead_units else None
    tiles = [t for g in groups for t in g.tiles]
    group_of = [g for g, x in enumerate(groups) for _ in x.tiles]
    last_of = [max(j for j, x in enumerate(group_of) if x == g) for g in range(len(groups))]
    n_t, per = len(tiles), len(groups[0].tiles)
    n_steps = n_t + VALUE + 5
    S = lambda j: c.ps[:, j % S_RING, :]
    TB = lambda j: c.ps[:, 3 + j % 2, :]
    OB = lambda g: c.ps[:, 5 + g % 2, :]
    BACK = c.ps[:, 7, 0:P]

    def wait_moved(eng, j):
        who = tiles[j].mover
        eng.wait_ge(moved[who], sum(t.mover == who for t in tiles[:j + 1]))

    def groups_at(j, lag):
        return [g for g in range(len(groups)) if last_of[g] == j - lag]

    with ExitStack() as tmp:
        sb = lambda n, s: tmp.enter_context(nc.sbuf_tensor(f"{name}_{n}", s, F32))
        prob = sb("prob", [P, P_RING, max(t.n_keys for t in tiles)])
        probT = sb("probT", [P, PT_RING, max(len(t.chunks) for t in tiles), P])
        peak, shift, total, total1, inv, weight = (sb(n, [P, n_t]) for n in
            ("peak", "shift", "total", "total1", "inv", "weight"))
        rows = sb("rows", [P, 2, P])
        with block as blk:
            @blk.sync
            def _(sp):
                if ahead:
                    ahead.load(sp)
                if fetch:
                    fetch(sp, sem)

            @blk.tensor
            def _(pe):
                def scores(j):
                    t = tiles[j]
                    if j >= S_RING:
                        pe.wait_ge(exped, j - S_RING + 1)
                    mm = t.scores + [(0, P, c0, n, c.ident_big[:, :], rhs) for c0, n, rhs in t.biases]
                    opened = set()
                    for i, (p0, p1, c0, n, lhsT, rhs) in enumerate(mm):
                        last = pe.matmul(S(j)[p0:p1, c0:c0 + n], lhsT, rhs, start=p0 not in opened,
                                         stop=i == len(mm) - 1, skip_group_check=True)
                        opened |= set(range(p0, p1, 32))
                    last.then_inc(scored, 1)

                def turn(j):
                    pe.wait_ge(exped, j + 1)
                    if j >= 2:
                        wait_moved(pe, j - 2)
                    for i, (c0, n) in enumerate(tiles[j].chunks):
                        last = pe.transpose(TB(j)[0:n, i * P:(i + 1) * P], prob[:, j % P_RING, c0:c0 + n], c.k("ident"))
                    last.then_inc(turned, 1)

                def values(j):
                    t, g = tiles[j], group_of[j]
                    wait_moved(pe, j)
                    if g >= 2 and group_of[j - 1] != g:
                        pe.wait_ge(mixed, g - 1)
                    for p0, p1, c0, n, who, chunk, rhs, start, stop in t.values:
                        keys = t.chunks[chunk][1]
                        last = pe.matmul(OB(g)[p0:p1, c0:c0 + n], probT[0:keys, j % PT_RING, chunk, who], rhs,
                                         start=start, stop=stop, skip_group_check=True)
                    last.then_inc(valued, 1)

                for j in range(n_steps):
                    if j < n_t:
                        scores(j)
                    if 0 <= j - TURN < n_t:
                        turn(j - TURN)
                    if 0 <= j - VALUE < n_t:
                        values(j - VALUE)
                    for g in groups_at(j, VALUE + 2):
                        pe.wait_ge(mixed, g + 1)
                        if g:
                            pe.wait_ge(rest, g)
                        pe.transpose(BACK, rows[:, g % 2, :], c.k("ident")).then_inc(back, 1)

            def full_and_part(t):
                full = sum(n == P for _, n in t.chunks)
                return full, (t.chunks[full][1] if full < len(t.chunks) else 0)

            def move(eng, copy, j):
                t = tiles[j]
                eng.wait_ge(turned, j + 1)
                if j >= PT_RING:
                    eng.wait_ge(valued, j - PT_RING + 1)
                full, n = full_and_part(t)
                if full:
                    last = copy(probT[:, j % PT_RING, 0:full, :], TB(j)[:, 0:full * P].rearrange("p (k n) -> p k n", n=P))
                if n:
                    last = copy(probT[0:n, j % PT_RING, full, :], TB(j)[0:n, full * P:(full + 1) * P])
                last.then_inc(moved[t.mover], 1)

            @blk.vector
            def _(dve):
                if ahead:
                    ahead.split_lo(dve, 0)
                    ahead.split_lo(dve, 1)
                n_mix = 0
                for j in range(n_steps):
                    if j < n_t:
                        dve.wait_ge(scored, j + 1)
                        dve.tensor_reduce(peak[:, j:j + 1], S(j)[:, 0:tiles[j].n_keys], AX_X, ALU.max, negate=True).then_inc(peaked, 1)
                        dve.wait_ge(peaked, j + 1)
                        dve.tensor_scalar(shift[:, j:j + 1], peak[:, j:j + 1], BIG / 10, None, ALU.min).then_inc(scaled, 1)
                    if 0 <= j - TURN < n_t and tiles[j - TURN].mover == "dve":
                        move(dve, dve.tensor_copy, j - TURN)
                    for g in groups_at(j, 2):
                        dve.wait_ge(exped, last_of[g] + 1)
                        at = slice(g * per, (g + 1) * per)
                        dve.tensor_scalar(total1[:, at], total[:, at], 0.5, None, ALU.max).then_inc(guarded, 1)
                        dve.wait_ge(guarded, g + 1)
                        dve.reciprocal(inv[:, at], total1[:, at]).then_inc(inverted, 1)
                        if groups[g].gate is not None:
                            dve.wait_ge(inverted, g + 1)
                            view = lambda x: x[:, at].rearrange("p (s a) -> p s a", s=groups[g].n_seg)
                            dve.tensor_tensor(view(weight), view(inv), groups[g].gate, ALU.mult).then_inc(weighed, 1)
                    for g in groups_at(j, VALUE + 1):
                        x = groups[g]
                        w = inv if x.gate is None else weight
                        dve.wait_ge(inverted if x.gate is None else weighed, g + 1)
                        dve.wait_ge(valued, last_of[g] + 1)
                        if g >= 2:
                            dve.wait_ge(back, g - 1)
                        width = P // x.n_seg
                        for a in range(x.n_br):
                            if a:
                                dve.wait_ge(mixing, n_mix)
                            for s in range(x.n_seg):
                                o = OB(g)[:, (s * x.n_br + a) * width:(s * x.n_br + a + 1) * width]
                                r = rows[:, g % 2, s * width:(s + 1) * width]
                                f = w[:, g * per + s * x.n_br + a:g * per + s * x.n_br + a + 1]
                                if a == 0:
                                    last = dve.tensor_scalar(r, o, f, None, ALU.mult)
                                else:
                                    last = dve.scalar_tensor_tensor(r, o, f, r, ALU.mult, ALU.add)
                                if a < x.n_br - 1:
                                    last.then_inc(mixing, 1)
                                    n_mix += 1
                        last.then_inc(mixed, 1)
                    for g in groups_at(j, VALUE + 4):
                        dve.wait_ge(top, g + 1)
                        for place, part in groups[g].leaves:
                            last = dve.tensor_tensor(place(c.x_lo), part(BACK), place(c.x_hi).bitcast(F32), ALU.subtract)
                        last.then_inc(rest, 1)

            @blk.scalar
            def _(act):
                copy = lambda out, in_: act.activation(out, in_, ACT.Copy)
                if ahead:
                    ahead.split_hi(act, 0)
                    ahead.split_hi(act, 1)
                for j in range(n_steps):
                    if j < n_t:
                        act.wait_ge(scaled, j + 1)
                        if j >= P_RING:
                            act.wait_ge(turned, j - P_RING + 1)
                        n = tiles[j].n_keys
                        act.activation(prob[:, j % P_RING, 0:n], S(j)[:, 0:n], ACT.Exp, bias=shift[:, j:j + 1],
                                       accum_out=total[:, j:j + 1]).then_inc(exped, 1)
                    if 0 <= j - TURN < n_t and tiles[j - TURN].mover == "act":
                        move(act, copy, j - TURN)
                    for g in groups_at(j, VALUE + 3):
                        act.wait_ge(back, g + 1)
                        for place, part in groups[g].leaves:
                            last = copy(place(c.x_hi), part(BACK))
                        last.then_inc(top, 1)


class Stack:

    def __init__(self):
        self.hi, self.lo = [], []

    def queries(self, side, src, dst):
        own, other = rows_of(side), rows_of(1 - side)
        self.hi.append((dst[own], src))
        self.lo.append((dst[other], src, dst[own], len(self.hi)))

    def keys(self, side, src, hi, lo):
        own, other = rows_of(side), rows_of(1 - side)
        self.hi += [(hi[own], src), (hi[other], src)]
        self.lo += [(part, src, hi[own], len(self.hi)) for part in (lo[own], lo[other])]

    def fill_hi(self, copy, made, a, b):
        for dst, src in self.hi[a:b]:
            copy(dst, src).then_inc(made, 1)

    def fill_lo(self, eng, made, a, b, done=None):
        for dst, src, hi, n in self.lo[a:b]:
            eng.wait_ge(made, n)
            ins = eng.tensor_tensor(dst, src, hi.bitcast(F32), ALU.subtract)
            if done:
                ins.then_inc(done, 1)


def rows_of(side):
    return slice(side * HD, side * HD + HD)


def idle_slots(c):
    lines = [w[:, :, :, :].rearrange("p s k n -> p (s k n)") for w in (c.w_hi, c.w_lo)]
    return [line[:, e * SEQ:(e + 1) * SEQ] for line in lines for e in range(2 * KCH * P // SEQ)]


class Rows:

    def __init__(self, n, side, q, keys, bias, values, gate, group, mover, first, last):
        self.n, self.side, self.q, self.keys, self.bias, self.values = n, side, q, keys, bias, values
        self.gate, self.group, self.mover, self.first, self.last = gate, group, mover, first, last
        self.wide = n
        self.short = None
        self.n_chunk = n // P


class Short:

    def __init__(self, heads, bias, gate):
        self.heads, self.bias, self.gate, self.mover = heads, bias, gate, "act"
        self.wide, self.n_chunk = 8 * 32, 2


TURN_P = 4
VALUE_P = 6


def stage_attend_prompt(c, name, tiles, leaf, n_groups, late=None, fetch=None, weave=None):
    nc = c.nc
    block, sem = stage(c, name)
    scored, peaked, exped, inverted, normed, turned, valued = (sem(s) for s in
        ("scored", "peaked", "exped", "inverted", "normed", "turned", "valued"))
    moved = {"act": sem("moved_act"), "dve": sem("moved_dve")}
    top, rest, link, stacked, late_set = sem("top"), sem("rest"), sem("link"), sem("stacked"), sem("late_set")
    n_t, n_prob, n_probT = len(tiles), 6, 3
    shorts = [j for j, t in enumerate(tiles) if isinstance(t, Short)]
    group_end = [max(j for j, t in enumerate(tiles) if j not in shorts and t.group == g) for g in range(n_groups)]
    S = lambda j: c.ps[:, j % 4, :]
    TB = lambda j: c.ps[:, 4 + j % 2, :]
    OB = lambda g: c.ps[:, 6 + g % 2, 0:P]
    LAG = 2

    def wait_moved(eng, j):
        who = tiles[j].mover
        eng.wait_ge(moved[who], sum(t.mover == who for t in tiles[:j + 1]))

    def through(j):
        return sum(i not in shorts for i in range(j + 1))

    with ExitStack() as tmp:
        sb = lambda n, s: tmp.enter_context(nc.sbuf_tensor(f"{name}_{n}", s, F32))
        prob = sb("prob", [P, n_prob, SEQ])
        probT = sb("probT", [P, n_probT, NB, P])
        peak, total, inv = (sb(n, [P, 8]) for n in ("peak", "total", "inv"))
        if shorts:
            shortT = sb("shortT", [P, 2, 2, P])
            peak8, total8, inv8 = (sb(n, [P, 2, 8]) for n in ("peak8", "total8", "inv8"))
        by_head = lambda x: x.rearrange("p (h n) -> p h n", n=32)
        spread = lambda x: x.rearrange("p (h a) -> p h a", a=1).broadcast_to([P, 8, 32])
        with block as blk:
            if fetch:
                @blk.sync
                def _(sp):
                    fetch(sp, sem, lambda: sp.wait_ge(late_set, len(late.lo)))

            @blk.tensor
            def _(pe):
                def scores(j):
                    t = tiles[j]
                    if j >= 4:
                        pe.wait_ge(peaked if j - 4 in shorts else exped, j - 3)
                    if late and j == n_t // 2:
                        pe.wait_ge(late_set, len(late.lo))
                    if j in shorts:
                        for h, (q, hi, lo) in enumerate(t.heads):
                            o = S(j)[:, 32 * h:32 * h + 32]
                            pe.matmul(o, q, hi, start=h == 0, stop=False, skip_group_check=True)
                            pe.matmul(o, q, lo, start=False, stop=False, skip_group_check=True)
                        last = pe.matmul(by_head(S(j)[:, 0:256]), c.ident_big[:, :], t.bias, start=False, stop=True,
                                         skip_group_check=True)
                    else:
                        n = max(t.n, 2 * P)
                        pe.matmul(S(j)[:, 0:n], t.q, t.keys[0][:, 0:n], start=True, stop=False, skip_group_check=True)
                        pe.matmul(S(j)[:, 0:n], t.q, t.keys[1][:, 0:n], start=False, stop=False, skip_group_check=True)
                        c0, w, rhs = t.bias
                        last = pe.matmul(S(j)[:, c0:c0 + w], c.ident_big[:, :], rhs, start=False, stop=True,
                                         skip_group_check=True)
                    last.then_inc(scored, 1)

                def turn(j):
                    pe.wait_ge(normed, j + 1)
                    if j >= 2:
                        wait_moved(pe, j - 2)
                    for i in range(tiles[j].n_chunk):
                        last = pe.transpose(TB(j)[:, i * P:(i + 1) * P], prob[:, j % n_prob, i * P:(i + 1) * P], c.k("ident"))
                    last.then_inc(turned, 1)

                def values(j):
                    wait_moved(pe, j)
                    if j in shorts:
                        return
                    t = tiles[j]
                    if t.group >= 2 and j and (j - 1 in shorts or tiles[j - 1].group != t.group):
                        pe.wait_ge(rest, t.group - 1)
                        pe.wait_ge(top, t.group - 1)
                    out = OB(t.group)[rows_of(t.side)]
                    products = [(lhsT, probT[:, j % n_probT, k, :]) for k, lhsT in t.values]
                    if t.short:
                        n, chunk, part, lhsT = t.short
                        products = [(lhsT, shortT[part, n % 2, chunk, :])] + products
                    for i, (lhsT, rhs) in enumerate(products):
                        last = pe.matmul(out, lhsT, rhs, start=t.first and i == 0,
                                         stop=t.last and i == len(products) - 1, skip_group_check=True)
                    last.then_inc(valued, 1)

                for j in range(n_t + VALUE_P):
                    if j < n_t:
                        scores(j)
                    if 0 <= j - TURN_P < n_t:
                        turn(j - TURN_P)
                    if j >= VALUE_P:
                        values(j - VALUE_P)

            def move(eng, copy, j):
                t = tiles[j]
                eng.wait_ge(turned, j + 1)
                if j in shorts:
                    n = shorts.index(j)
                    if n >= 2:
                        eng.wait_ge(valued, through(shorts[n - 1] - 1))
                    dst = shortT[:, n % 2]
                else:
                    if j >= n_probT and through(j - n_probT):
                        eng.wait_ge(valued, through(j - n_probT))
                    dst = probT[:, j % n_probT, 0:t.n_chunk, :]
                copy(dst, TB(j)[:, 0:t.n_chunk * P].rearrange("p (k n) -> p k n", n=P)).then_inc(moved[t.mover], 1)

            @blk.vector
            def _(dve):
                linked = Linked(dve, link)
                more = weave(dve, sem) if weave else iter(())

                def peaks(j):
                    t = tiles[j]
                    dve.wait_ge(scored, j + 1)
                    if j in shorts:
                        n = shorts.index(j)
                        linked(dve.tensor_reduce(peak8[:, n % 2, :], by_head(S(j)[:, 0:256]), AX_X, ALU.max, negate=True))
                        linked(dve.tensor_scalar(peak8[:, n % 2, :], peak8[:, n % 2, :], BIG / 10, None, ALU.min))
                        if j >= n_prob:
                            dve.wait_ge(turned, j - n_prob + 1)
                        dve.tensor_tensor(by_head(prob[:, j % n_prob, 0:256]), by_head(S(j)[:, 0:256]),
                                          spread(peak8[:, n % 2, :]), ALU.add).then_inc(peaked, 1)
                    else:
                        dve.tensor_reduce(peak[:, j % 8:j % 8 + 1], S(j)[:, 0:t.n], AX_X, ALU.max, negate=True).then_inc(peaked, 1)

                def invert(j):
                    dve.wait_ge(exped, j + 1)
                    if j in shorts:
                        n = shorts.index(j)
                        linked(dve.reduce_sum(total8[:, n % 2, :], by_head(prob[:, j % n_prob, 0:256]), AX_X))
                        linked(dve.tensor_scalar(total8[:, n % 2, :], total8[:, n % 2, :], 0.5, None, ALU.max))
                        linked(dve.reciprocal(inv8[:, n % 2, :], total8[:, n % 2, :]))
                        dve.tensor_tensor(inv8[:, n % 2, :].rearrange("p (s h) -> p s h", s=2),
                                          inv8[:, n % 2, :].rearrange("p (s h) -> p s h", s=2), tiles[j].gate, ALU.mult).then_inc(inverted, 1)
                    else:
                        dve.reciprocal(inv[:, j % 8:j % 8 + 1], total[:, j % 8:j % 8 + 1]).then_inc(inverted, 1)

                done = 0
                for j in range(n_t + VALUE_P + 2):
                    if j < n_t:
                        peaks(j)
                    if 0 <= j - TURN_P < n_t and tiles[j - TURN_P].mover == "dve":
                        move(dve, dve.tensor_copy, j - TURN_P)
                    next(more, None)
                    if late and j % 2 and LAG <= j // 2 < LAG + len(late.lo):
                        n = j // 2 - LAG
                        late.fill_lo(dve, stacked, n, n + 1, late_set)
                    if 0 <= j - 1 < n_t:
                        invert(j - 1)
                    while done < n_groups and group_end[done] <= j - VALUE_P - 1:
                        dve.wait_ge(top, done + 1)
                        place = leaf(done)
                        dve.tensor_tensor(place(c.x_lo), OB(done), place(c.x_hi).bitcast(F32), ALU.subtract).then_inc(rest, 1)
                        done += 1
                for _ in more:
                    pass

            @blk.gpsimd
            def _(pool):
                for j, t in enumerate(tiles):
                    pool.wait_ge(inverted, j + 1)
                    w = prob[:, j % n_prob, 0:t.wide]
                    if j in shorts:
                        n = shorts.index(j)
                        pool.tensor_tensor(by_head(w), by_head(w), spread(inv8[:, n % 2, :]), ALU.mult).then_inc(normed, 1)
                    else:
                        pool.tensor_scalar(w, w, inv[:, j % 8:j % 8 + 1], 1.0 if t.gate is None else t.gate, ALU.mult, ALU.mult).then_inc(normed, 1)

            @blk.scalar
            def _(act):
                copy = lambda out, in_: act.activation(out, in_, ACT.Copy)
                done = 0
                for j in range(n_t + VALUE_P + 2):
                    if j < n_t:
                        act.wait_ge(peaked, j + 1)
                        if j in shorts:
                            w = prob[:, j % n_prob, 0:256]
                            act.activation(w, w, ACT.Exp).then_inc(exped, 1)
                        else:
                            if j >= n_prob:
                                act.wait_ge(turned, j - n_prob + 1)
                            n = tiles[j].n
                            act.activation(prob[:, j % n_prob, 0:n], S(j)[:, 0:n], ACT.Exp, bias=peak[:, j % 8:j % 8 + 1],
                                           accum_out=total[:, j % 8:j % 8 + 1]).then_inc(exped, 1)
                    if 0 <= j - TURN_P < n_t and tiles[j - TURN_P].mover == "act":
                        move(act, copy, j - TURN_P)
                    if late and j % 2 and j // 2 < len(late.hi):
                        late.fill_hi(copy, stacked, j // 2, j // 2 + 1)
                    while done < n_groups and group_end[done] <= j - VALUE_P:
                        act.wait_ge(valued, through(group_end[done]))
                        copy(leaf(done)(c.x_hi), OB(done)).then_inc(top, 1)
                        done += 1


class Linked:

    def __init__(self, eng, link):
        self.eng, self.link, self.count = eng, link, 0

    def __call__(self, ins):
        self.count += 1
        ins.then_inc(self.link, 1)
        self.eng.wait_ge(self.link, self.count)


def prompt_tiles(sections, branches, short=None):
    tiles, n_groups, n_short, leaves = [], 0, 0, []
    for a in range(sections):
        for qb in range(NB):
            if short:
                tiles.append(short[0](a, qb))
            for i in range(4):
                pair = 4 * a + i
                for b, (q, keys, value, bias, gate, mover) in enumerate(branches):
                    for side in range(2):
                        t = Rows((qb + 1) * P, side, q(pair, side, qb), keys(a, side), bias(qb),
                                 [(k, value(a, side, k)) for k in range(qb + 1)], gate(pair, side, qb), n_groups,
                                 mover(side), b == 0, b == len(branches) - 1)
                        if short and b == 0:
                            t.short = (n_short, side, slice(32 * i, 32 * i + 32), short[1](a, side, i))
                        tiles.append(t)
                leaves.append(lambda x, pair=pair, qb=qb: x[:, pair, qb * P:(qb + 1) * P])
                n_groups += 1
            n_short += 1
    return tiles, lambda g: leaves[g], n_groups



def take_best(dve, linked, scores, bests, n_take):
    n, sem, start = len(scores), linked.link, linked.count
    done = 0

    def step(ins):
        nonlocal done
        ins.then_inc(sem, 1)
        done += 1

    def after_own():
        if done >= n:
            dve.wait_ge(sem, start + done - n + 1)

    for r in range(-(-n_take // 8)):
        left = n_take - 8 * r
        for x, best in zip(scores, bests):
            after_own()
            step(dve.max(best, x))
            yield
        if left < 8:
            for best in bests:
                after_own()
                step(dve.memset(best[:, left:8], TAKEN))
        for x, best in zip(scores, bests):
            after_own()
            step(dve.match_replace(x, best, x, TAKEN))
            yield
    linked.count = start + done
    dve.wait_ge(sem, linked.count)


def stage_prepare(c, projT, iw, sel, keep_rows, stacks, kikT, v_old):
    nc, d = c.nc, c.dram
    block, sem = stage(c, "prepare")
    scored, relud, summed, link = sem("scored"), sem("relud"), sem("summed"), sem("link")
    table_in, v_in, page_turned, page_moved = sem("table_in"), sem("v_in"), sem("page_turned"), sem("page_moved")
    conv_in, conv_turned, conv_moved, tail_set, tail_turned, tail_moved, conv_out = (sem(s) for s in
        ("conv_in", "conv_turned", "conv_moved", "tail_set", "tail_turned", "tail_moved", "conv_out"))
    u_set, tapped = sem("u_set"), sem("tapped")
    conv_link, prod, top, rest, stacked = sem("conv_link"), sem("prod"), sem("top"), sem("rest"), sem("stacked")
    W = D // 2 // P
    n_ring = 4
    n_pool_lo = len(stacks.lo) * 2 // 3
    land = [sem(f"land{i}") for i in range(n_ring)]
    jobs = [(qb, h) for qb in range(1, NB) for h in range(4)]
    pages = [(b, g) for b in range(DEC_B) for g in range(NPAGE)]
    with ExitStack() as tmp:
        sb = lambda n, s, dt=F32: tmp.enter_context(nc.sbuf_tensor(n, s, dt))
        relu = sb("ix_relu", [P, 2, SEQ])
        first = [sum((q + 1) * P for q in range(1, qb)) for qb in range(1, NB + 1)]
        score = sb("ix_score", [P, first[-1]])
        best = sb("ix_best", [P, NB - 1, 8])
        table = sb("pg_table", [1, DEC_B * NPAGE], I32)
        ring = sb("pg_ring", [P, n_ring, 2 * P])
        LINE, SAMPLE = SEQ + DEC_B * (2 + DEC_T), SEQ + 2
        both = sb("cv_both", [76, P])
        bothT = sb("cv_bothT", [P, 76])
        u = sb("cv_u", [P, 2, LINE + 2])
        acc = sb("cv_acc", [P, 2, LINE + 2])
        term = sb("cv_term", [P, LINE])
        terms = [term[:, :], projT[:, 8:10, :].rearrange("p k n -> p (k n)")[:, 0:LINE]]
        tail = sb("cv_tail", [P, W, 18])
        tail_rows = sb("cv_tail_rows", [72, P])
        with block as blk:
            @blk.sync
            def _(sp):
                sp.dma_start(table[:, :], d["page_table"].rearrange("(a b) g -> a (b g)", a=1)).then_inc(table_in, 16)
                sp.dma_start(both[0:64, :], d["state_b_conv"][0].rearrange("b j (k p) -> (b j k) p", p=P)).then_inc(conv_in, 16)
                sp.dma_start(both[64:76, :], d["ab_conv_w"][0].rearrange("j (k p) -> (j k) p", p=P)).then_inc(conv_in, 16)
                sp.wait_ge(table_in, 16)
                n_pool = d["cache_a_k"].shape[1]
                for n, (b, g) in enumerate(pages):
                    page = sp.value_load(table[0:1, b * NPAGE + g:b * NPAGE + g + 1], min_val=0, max_val=n_pool - 1)
                    if n >= n_ring:
                        sp.wait_ge(page_turned, n - n_ring + 1)
                    sp.dma_start(ring[:, n % n_ring, 0:P], d["cache_a_k"][0][bass.ds(page, 1)]
                                 .rearrange("a p g e -> p (a g e)")).then_inc(land[n % n_ring], 16)
                    for s in range(2):
                        sp.dma_start(ring[:, n % n_ring, P + s * HD:P + (s + 1) * HD], d["cache_a_ik"][0][bass.ds(page, 1)]
                                     .rearrange("a p e -> p (a e)")).then_inc(land[n % n_ring], 16)
                    sp.dma_start(v_old[:, b, g, :], d["cache_a_v"][0][bass.ds(page, 1)]
                                 .rearrange("a p g e -> p (a g e)")).then_inc(v_in, 16)
                sp.wait_ge(tail_moved, 1)
                for k in range(W):
                    sp.dma_start(d["b_conv_s"][0].rearrange("b j d -> (b j) d")[:, k * P:(k + 1) * P],
                                 tail_rows[18 * k:18 * k + 16, :]).then_inc(conv_out, 16)
                    sp.dma_start(d["b_conv_p"][0, 0][:, k * P:(k + 1) * P], tail_rows[18 * k + 16:18 * k + 18, :]).then_inc(conv_out, 16)
                sp.wait_ge(v_in, 16 * len(pages))
                sp.wait_ge(conv_out, 16 * 2 * W)

            @blk.tensor
            def _(pe):
                for qb in range(1, NB):
                    for h in range(4):
                        j = 4 * (qb - 1) + h
                        if j >= 4:
                            pe.wait_ge(relud, j - 3)
                        rows = rows_of(h % 2)
                        n = (qb + 1) * P
                        pe.matmul(c.ps[:, j % 4, 0:n], projT[rows, 4 + h // 2, qb * P:(qb + 1) * P],
                                  projT[rows, 7, 0:n], start=True, stop=True).then_inc(scored, 1)
                pe.wait_ge(conv_in, 32)
                pe.transpose(c.ps[:, 7, 0:76], both[:, :], c.k("ident")[0:76, 0:76]).then_inc(conv_turned, 1)
                for n in range(len(pages)):
                    if n >= 3:
                        pe.wait_ge(page_moved, n - 2)
                    pe.wait_ge(land[n % n_ring], 48 * (n // n_ring + 1))
                    for h in range(2):
                        last = pe.transpose(c.ps[:, 4 + n % 3, h * P:(h + 1) * P], ring[:, n % n_ring, h * P:(h + 1) * P], c.k("ident"))
                    last.then_inc(page_turned, 1)
                pe.wait_ge(tail_set, W)
                pe.transpose(c.ps[0:72, 7, P:2 * P], tail[:, :, :].rearrange("p k n -> p (k n)"), c.k("ident")).then_inc(tail_turned, 1)

            def sample(line):
                return line[:, SAMPLE:].rearrange("p (b t) -> p b t", b=DEC_B)[:, :, 0:DEC_T]

            @blk.scalar
            def _(act):
                copy = lambda out, in_: act.activation(out, in_, ACT.Copy)
                for qb in range(1, NB):
                    for h in range(4):
                        j = 4 * (qb - 1) + h
                        n = (qb + 1) * P
                        act.wait_ge(scored, j + 1)
                        if j >= 2:
                            act.wait_ge(summed, j - 1)
                        act.activation(relu[:, j % 2, 0:n], c.ps[:, j % 4, 0:n], ACT.Relu, scale=SCALE).then_inc(relud, 1)
                act.wait_ge(conv_turned, 1)
                copy(bothT[:, :], c.ps[:, 7, 0:76]).then_inc(conv_moved, 1)
                act.wait_ge(conv_moved, 1)
                stacks.fill_hi(copy, stacked, 0, len(stacks.hi))
                for k in range(W):
                    act.wait_ge(u_set, k + 1)
                    if k >= 1:
                        act.wait_ge(prod, k)
                    if k >= 2:
                        act.wait_ge(rest, k - 1)
                    for j, out in enumerate([acc[:, k % 2, 0:LINE]] + terms):
                        last = act.activation(out, u[:, k % 2, j:j + LINE], ACT.Copy, scale=bothT[:, 64 + j * W + k:65 + j * W + k])
                    last.then_inc(tapped, 1)
                    for n in range(k * len(pages) // W, (k + 1) * len(pages) // W):
                        b, g = pages[n]
                        act.wait_ge(page_turned, n + 1)
                        copy(kikT[:, :, b, g * PAGE:(g + 1) * PAGE], c.ps[:, 4 + n % 3, 0:2 * P].rearrange("p (h n) -> p h n", n=P)).then_inc(page_moved, 1)
                    act.wait_ge(prod, k + 1)
                    copy(c.x_hi[:, 4 + k, 0:SEQ], acc[:, k % 2, 0:SEQ])
                    copy(c.x_hi[:, 4 + k, SEQ:T].rearrange("p (b t) -> p b t", b=DEC_B), sample(acc[:, k % 2])).then_inc(top, 1)
                act.wait_ge(tail_turned, 1)
                copy(tail_rows[:, :], c.ps[0:72, 7, P:2 * P]).then_inc(tail_moved, 1)

            @blk.vector
            def _(dve):
                linked = Linked(dve, link)
                linked(dve.tensor_scalar(iw[:, 0:NB, :], keep_rows[:, 0:NB, :], 0.5, None, ALU.mult))
                linked(dve.tensor_scalar(iw[0:TS, NB, :], keep_rows[0:TS, NB, :], 0.5, None, ALU.mult))
                scores = [score[:, first[i]:first[i + 1]] for i in range(NB - 1)]
                for j, (qb, h) in enumerate(jobs):
                    n = (qb + 1) * P
                    x = scores[qb - 1]
                    dve.wait_ge(relud, j + 1)
                    if h == 0:
                        dve.tensor_scalar(x, relu[:, j % 2, 0:n], iw[:, qb, 0:1], None, ALU.mult).then_inc(summed, 1)
                    else:
                        dve.wait_ge(summed, j)
                        dve.scalar_tensor_tensor(x, relu[:, j % 2, 0:n], iw[:, qb, h:h + 1], x, ALU.mult, ALU.add).then_inc(summed, 1)
                dve.wait_ge(summed, len(jobs))
                for qb in range(1, NB):
                    own = scores[qb - 1][:, qb * P:(qb + 1) * P]
                    linked(dve.scalar_tensor_tensor(own, c.k("causal"), BIG, own, ALU.mult, ALU.add))
                for _ in take_best(dve, linked, scores, [best[:, i, :] for i in range(NB - 1)], TOPK_P):
                    pass
                for i, x in enumerate(scores):
                    dve.tensor_scalar(sel[:, i + 1, 0:(i + 2) * P], x, TAKEN, 1.0, ALU.is_equal, ALU.subtract)
                stacks.fill_lo(dve, stacked, n_pool_lo, len(stacks.lo))

            @blk.gpsimd
            def _(pool):
                linked = Linked(pool, conv_link)
                linked(pool.memset(u[:, :, 0:2], 0.0))
                seq = lambda slab: projT[:, slab, SEQ:T].rearrange("p (b t) -> p b t", b=DEC_B)
                pool.wait_ge(conv_moved, 1)

                def gated_input(k):
                    if k >= 2:
                        pool.wait_ge(tapped, k - 1)
                    line = u[:, k % 2]
                    by_seq = line[:, SAMPLE:].rearrange("p (b t) -> p b t", b=DEC_B)
                    pool.tensor_copy(by_seq[:, :, 0:2], bothT[:, 0:64].rearrange("p (b j k) -> p k b j", b=DEC_B, j=2)[:, k])
                    pool.tensor_tensor(by_seq[:, :, 2:], seq(14 + k), seq(18 + k), ALU.mult)
                    pool.tensor_tensor(line[:, 2:SAMPLE], projT[:, 14 + k, 0:SEQ], projT[:, 18 + k, 0:SEQ], ALU.mult).then_inc(u_set, 1)
                    pool.wait_ge(u_set, k + 1)
                    pool.tensor_copy(tail[:, k, 0:16].rearrange("p (b j) -> p b j", j=2), by_seq[:, :, DEC_T:])
                    pool.tensor_copy(tail[:, k, 16:18], line[:, SEQ:SAMPLE]).then_inc(tail_set, 1)

                def low(k):
                    pool.wait_ge(top, k + 1)
                    pool.tensor_tensor(c.x_lo[:, 4 + k, 0:SEQ], acc[:, k % 2, 0:SEQ], c.x_hi[:, 4 + k, 0:SEQ].bitcast(F32), ALU.subtract)
                    pool.tensor_tensor(c.x_lo[:, 4 + k, SEQ:T].rearrange("p (b t) -> p b t", b=DEC_B), sample(acc[:, k % 2]),
                                       c.x_hi[:, 4 + k, SEQ:T].bitcast(F32).rearrange("p (b t) -> p b t", b=DEC_B), ALU.subtract).then_inc(rest, 1)

                gated_input(0)
                for k in range(W):
                    if k + 1 < W:
                        gated_input(k + 1)
                    line = acc[:, k % 2, :]
                    pool.wait_ge(tapped, k + 1)
                    for part in terms:
                        linked(pool.tensor_tensor(line[:, 0:LINE], line[:, 0:LINE], part, ALU.add))
                    pool.tensor_tensor(line[:, 0:SEQ], line[:, 0:SEQ], projT[:, 10 + k, 0:SEQ], ALU.mult)
                    pool.tensor_tensor(sample(line), sample(line), seq(10 + k), ALU.mult).then_inc(prod, 1)
                    if k >= 1:
                        low(k - 1)
                low(W - 1)
                pool.wait_ge(rest, W)
                stacks.fill_lo(pool, stacked, 0, n_pool_lo)


def stage_index_sample(c, projT, iw_rows, ikT, score, q_blk):
    nc = c.nc
    block, sem = stage(c, "index_s")
    q_set, scored, relud, mixed, picked, link = (sem(s) for s in ("q_set", "scored", "relud", "mixed", "picked", "link"))
    mix_set = sem("mix_set")
    with ExitStack() as tmp:
        sb = lambda n, s, d=F32: tmp.enter_context(nc.sbuf_tensor(n, s, d))
        iq = sb("is_iq", [P, DEC_B, 32])
        relu = sb("is_relu", [P, 2, NEW])
        mix = sb("is_mix", [P, 2, P])
        col = sb("is_col", [P, 2])
        hit = sb("is_hit", [P, 2, 4])
        with block as blk:
            @blk.vector
            def _(dve):
                linked = Linked(dve, link)

                linked(dve.memset(iq[:, :, :], 0.0))
                linked(dve.memset(q_blk[:, :, :, :, :], 0.0))
                iq_v = iq[:, :, 0:16].rearrange("p b (s i t) -> p b s i t", s=2, i=2)
                for side in range(2):
                    rows = slice(side * HD, side * HD + HD)
                    for i in range(2):
                        dve.tensor_copy(iq_v[rows, :, side, i, :], projT[rows, 4 + i, SEQ:T].rearrange("p (b t) -> p b t", t=DEC_T)).then_inc(q_set, 1)
                    for h in range(4):
                        dve.tensor_copy(q_blk[rows, :, side, h, :], projT[rows, h, SEQ:T].rearrange("p (b t) -> p b t", t=DEC_T))
                dve.wait_ge(picked, 1)
                for j in range(2):
                    linked(dve.tensor_tensor(hit[:, j, :], c.ps[:, 7, 4 * j:4 * j + 4], c.k("ihead"), ALU.mult))
                    linked(dve.reduce_sum(col[:, j:j + 1], hit[:, j, :], AX_X))
                    dve.tensor_scalar(mix[:, j, :], c.k("imix"), col[:, j:j + 1], None, ALU.mult).then_inc(mix_set, 1)
                for j in range(2):
                    dve.wait_ge(mixed, j + 1)
                    linked(dve.tensor_copy(score[:, j, :], c.ps[:, 2 + j, 0:NEW]))
                    own = score[:, j, PAST:NEW]
                    linked(dve.scalar_tensor_tensor(own, c.k("new")[:, j * TS:(j + 1) * TS], BIG, own, ALU.mult, ALU.add))
            @blk.tensor
            def _(pe):
                for j in range(2):
                    last = pe.matmul(c.ps[:, 7, 4 * j:4 * j + 4], c.k("pick")[0:TS, j * P:(j + 1) * P], iw_rows,
                                     start=(j == 0), stop=(j == 1), skip_group_check=True)
                last.then_inc(picked, 1)
                pe.wait_ge(q_set, 4)
                for j in range(2):
                    for u in range(4):
                        b = 4 * j + u
                        pe.matmul(c.ps[32 * u:32 * u + 32, j, 0:PAST], iq[:, b, :], ikT[:, 0, b, :], start=True, stop=False, skip_group_check=True)
                        last = pe.matmul(c.ps[32 * u:32 * u + 32, j, PAST:NEW], iq[:, b, :], projT[:, 7, SEQ:T], start=False, stop=True, skip_group_check=True)
                    last.then_inc(scored, 1)
                for j in range(2):
                    pe.wait_ge(mix_set, j + 1)
                    pe.wait_ge(relud, j + 1)
                    pe.matmul(c.ps[:, 2 + j, 0:NEW], mix[:, j, :], relu[:, j, :], start=True, stop=True).then_inc(mixed, 1)

            @blk.scalar
            def _(act):
                for j in range(2):
                    act.wait_ge(scored, j + 1)
                    act.activation(relu[:, j, :], c.ps[:, j, 0:NEW], ACT.Relu, scale=SCALE).then_inc(relud, 1)


def sample_groups(n, units, branches, gate, leaves):
    out = []
    for j in range(n):
        tiles = []
        mine = units[4 * j:4 * j + 4]
        for a, (q, cached, n_old, new, bias, value) in enumerate(branches):
            scores = []
            for u, unit in enumerate(mine):
                scores.append((32 * u, 32 * u + 32, 0, n_old, q(unit), cached(unit)))
                if new:
                    scores.append((32 * u, 32 * u + 32, n_old, TS, q(unit), new(unit)))
            n_keys = n_old + (TS if new else 0)
            n_chunk = -(-n_keys // P)
            values = []
            for u, unit in enumerate(mine):
                for k in range(n_chunk):
                    values.append((32 * u, 32 * u + 32, a * P, P, slice(32 * u, 32 * u + 32), k,
                                   value(unit, k, min(P, n_keys - k * P)), a == 0 and k == 0,
                                   a == len(branches) - 1 and k == n_chunk - 1))
            tiles.append(Tile(scores, [bias(j)] if bias else [], n_keys, values, ("act", "dve")[a % 2]))
        out.append(Group(tiles, 1, len(branches), gate(j) if gate else None, leaves(j)))
    return out



RING_C = 12


def stage_compress(c, projT, k_cmpT, v_cmp_p, v_cmp_s, stacks, table, ring):
    nc = c.nc
    block, sem = stage(c, "compress")
    d, tags = c.dram, ("k", "v")
    zeroed, small_in, pe_t, pe_m, placed, bias_m, gelu, outp, outm, win_out, v_clear = (sem(s) for s in
        ("zeroed", "small_in", "pe_t", "pe_m", "placed", "bias_m", "gelu", "outp", "outm", "win_out", "v_clear"))
    w1_in, hid, turned, stacked = sem("w1_in"), sem("hid"), sem("turned"), sem("stacked")
    n_ring = RING_C
    land = [sem(f"land{i}") for i in range(n_ring)]
    evac = [sem("evac_dve"), sem("evac_act")]
    N = (2 * SEQ + 2 * DEC_B * PAST) // CMP_S
    OLD = 2 * SEQ
    steps = [(tag, b, g) for tag in range(2) for b in range(DEC_B) for g in range(NPAGE)]
    per = len(steps) // 2
    w1d = [x[:, 0:CMP_W // 2 * P].rearrange("p (j e) -> p j e", e=P) for x in
           (c.w_raw[:, :, :, :].rearrange("p s k n -> p (s k n)"), projT[:, 16:20, :].rearrange("p k n -> p (k n)"))]
    with ExitStack() as tmp:
        sb = lambda n, s, dt=F32: tmp.enter_context(nc.sbuf_tensor(n, s, dt))
        line = sb("cp_line", [P, N * CMP_S + CMP_W])
        w2d = sb("cp_w2", [P, 2, P])
        rows = sb("cp_pe_rows", [CMP_W, 2, P])
        bias = sb("cp_bias", [P, 2])
        hidT = sb("cp_hidT", [P, N])
        old = line[:, OLD:OLD + 2 * DEC_B * PAST].rearrange("p (a b n) -> p a b n", a=2, b=DEC_B)
        with block as blk:
            @blk.gpsimd
            def _(pool):
                for x in w1d:
                    pool.memset(x, 0.0).then_inc(zeroed, 1)
                pool.memset(w2d[:, :, :], 0.0).then_inc(zeroed, 1)

            @blk.sync
            def _(sp):
                numbers = {}

                def load_page(n):
                    tag, b, g = steps[n]
                    cache = d["cache_c_cmp_" + tags[tag]]
                    if (b, g) not in numbers:
                        numbers[b, g] = page_number(sp, table, b * NPAGE + g, cache)
                    page = numbers[b, g]
                    if n >= n_ring:
                        sp.wait_ge(turned, n - n_ring + 1)
                    sp.dma_start(ring[:, n % n_ring, :], cache[0][bass.ds(page, 1)].rearrange("a p g e -> p (a g e)")).then_inc(land[n % n_ring], 16)

                for n in range(n_ring, per + n_ring):
                    load_page(n)
                for tag in tags:
                    sp.dma_start(d[f"c_win_{tag}_s"][0][:, 0:PAST - DEC_T], d[f"state_c_win_{tag}"][0][:, DEC_T:PAST]).then_inc(win_out, 16)
                for n in range(per + n_ring, 2 * per):
                    load_page(n)
                sp.wait_ge(win_out, 32)

            def second(pe, tag):
                pe.wait_ge(gelu, tag + 1)
                if tag == 0:
                    pe.matmul(c.ps[:, 2, 0:N], w2d[:, 0, :], hidT[:, :], start=True, stop=True).then_inc(outp, 1)
                    return
                pe.wait_ge(outm, 1)
                for i in range(2):
                    pe.matmul(c.ps[0:NCMP_P, 2, i * P:(i + 1) * P], hidT[:, 32 * i:32 * i + NCMP_P], w2d[:, 1, :],
                              start=(i == 0), stop=(i == 1), skip_group_check=True)
                for i in range(2 * DEC_B):
                    c0 = OLD // CMP_S + i * (PAST // CMP_S)
                    last = pe.matmul(c.ps[0:NCMP_S, 3 + i // 4, (i % 4) * P:(i % 4 + 1) * P], hidT[:, c0:c0 + NCMP_S], w2d[:, 1, :],
                                     start=(i % 4 == 0), stop=(i % 4 == 3), skip_group_check=True)
                last.then_inc(outp, 1)

            @blk.tensor
            def _(pe):
                for tag in range(2):
                    for n in range(tag * per, (tag + 1) * per):
                        if n >= 4:
                            pe.wait_ge(evac[n % 2], (n - 4) // 2 + 1)
                        if n >= n_ring:
                            pe.wait_ge(land[n % n_ring], 16 * (n // n_ring))
                        for h in range(2):
                            last = pe.transpose(c.ps[:, 3 + n % 4, h * P:(h + 1) * P], ring[:, n % n_ring, h * P:(h + 1) * P], c.k("ident"))
                        last.then_inc(turned, 1)
                    if tag == 0:
                        pe.wait_ge(small_in, 16 * 8)
                    else:
                        second(pe, 0)
                    pe.transpose(c.ps[:, 1, tag * CMP_W:(tag + 1) * CMP_W], rows[:, tag, :], c.k("ident")[0:CMP_W, 0:CMP_W]).then_inc(pe_t, 1)
                    pe.wait_ge(pe_m, tag + 1)
                    pe.wait_ge(placed, 2 * (tag + 1))
                    for e in evac:
                        pe.wait_ge(e, (tag + 1) * per // 2)
                    pe.wait_ge(w1_in, 64 * (tag + 1))
                    for j in range(CMP_W):
                        last = pe.matmul(c.ps[:, 0, 0:N + 1], w1d[j // (CMP_W // 2)][:, j % (CMP_W // 2), :],
                                         line[:, j:j + N * CMP_S + 1:CMP_S], start=j == 0, stop=j == CMP_W - 1)
                    last.then_inc(hid, 1)
                second(pe, 1)

            def move(eng, copy, n):
                tag, b, g = steps[n]
                eng.wait_ge(turned, n + 1)
                copy(old[:, :, b, g * PAGE:(g + 1) * PAGE], c.ps[:, 3 + n % 4, 0:2 * P].rearrange("p (h n) -> p h n", n=P)).then_inc(evac[n % 2], 1)

            def place(eng, copy, tag, i):
                copy(line[:, i * SEQ:(i + 1) * SEQ], projT[:, (8, 14)[tag] + i, 0:SEQ]).then_inc(placed, 1)

            n_hi, n_lo = len(stacks.hi), len(stacks.lo)

            @blk.vector
            def _(dve):
                for tag in range(2):
                    if tag:
                        stacks.fill_lo(dve, stacked, 0, n_lo // 2)
                        dve.wait_ge(hid, 1)
                        dve.wait_ge(gelu, 1)
                    place(dve, dve.tensor_copy, tag, 0)
                    for n in range(tag * per, (tag + 1) * per, 2):
                        move(dve, dve.tensor_copy, n)
                    if tag:
                        dve.wait_ge(outp, 1)
                        dve.tensor_copy(k_cmpT[:, :], c.ps[:, 2, 0:N]).then_inc(outm, 1)
                    dve.wait_ge(pe_t, tag + 1)
                    dve.tensor_copy(line[:, N * CMP_S:N * CMP_S + CMP_W], c.ps[:, 1, tag * CMP_W:(tag + 1) * CMP_W]).then_inc(pe_m, 1)
                dve.memset(v_cmp_p[:, :], 0.0).then_inc(v_clear, 1)
                stacks.fill_lo(dve, stacked, n_lo // 2, n_lo)
                dve.wait_ge(v_clear, 1)
                dve.wait_ge(outp, 2)
                for i in range(4):
                    dve.tensor_copy(v_cmp_p[32 * i:32 * i + NCMP_P, :], c.ps[0:NCMP_P, 2, 0:2 * P])

            @blk.scalar
            def _(act):
                copy = lambda out, in_: act.activation(out, in_, ACT.Copy)

                def load_w1(tag):
                    w1 = d["c_cmp_w1_" + tags[tag]][0].rearrange("j d e -> d j e")
                    for s in range(2):
                        own = rows_of(s)
                        for half, x in enumerate(w1d):
                            at = slice(half * CMP_W // 2, (half + 1) * CMP_W // 2)
                            act.dma_start(x[own, :, own], w1[:, at, :]).then_inc(w1_in, 16)

                for tag in range(2):
                    if tag:
                        act.wait_ge(hid, 1)
                    else:
                        act.wait_ge(zeroed, 3)
                    load_w1(tag)
                    if not tag:
                        for i in range(2):
                            for s in range(2):
                                own = rows_of(s)
                                act.dma_start(w2d[own, i, own], d["c_cmp_w2_" + tags[i]][0]).then_inc(small_in, 16)
                                act.dma_start(rows[:, i, own], d["c_cmp_pe_" + tags[i]][0]).then_inc(small_in, 16)
                    place(act, copy, tag, 1)
                    for n in range(tag * per + 1, (tag + 1) * per, 2):
                        move(act, copy, n)
                    stacks.fill_hi(copy, stacked, tag * n_hi // 2, (tag + 1) * n_hi // 2)
                    act.wait_ge(hid, tag + 1)
                    copy(bias[:, tag:tag + 1], c.ps[:, 0, N:N + 1]).then_inc(bias_m, 1)
                    act.wait_ge(bias_m, tag + 1)
                    if tag:
                        act.wait_ge(outp, 1)
                    act.activation(hidT[:, :], c.ps[:, 0, 0:N], ACT.Gelu_apprx_tanh, bias=bias[:, tag:tag + 1]).then_inc(gelu, 1)
                act.wait_ge(outp, 2)
                copy(v_cmp_s[0:NCMP_S, :].rearrange("p (a n) -> p a n", a=4), c.ps[0:NCMP_S, 3:7, :])


def stage_gates(c, projT, gate_sig, gate_s, q_blk, k_cmpT, kc2):
    nc = c.nc
    block, sem = stage(c, "gates")
    sig, picked, link = sem("sig"), sem("picked"), sem("link")
    with ExitStack() as tmp:
        hit = tmp.enter_context(nc.sbuf_tensor("gt_hit", [P, 3, 16], F32))
        cleared, stacked = sem("cleared"), sem("stacked")
        with block as blk:
            @blk.gpsimd
            def _(pool):
                pool.memset(kc2[:, :, :, :].bitcast(F32), 0.0).then_inc(cleared, 1)
                pool.wait_ge(cleared, 1)
                stacks = Stack()
                for a in range(2):
                    for side in range(2):
                        stacks.keys(side, k_cmpT[rows_of(side), 32 * a:32 * a + NCMP_P],
                                    kc2[:, 0, 2 * a + side, 0:NCMP_P], kc2[:, 1, 2 * a + side, 0:NCMP_P])
                stacks.fill_hi(pool.tensor_copy, stacked, 0, len(stacks.hi))
                stacks.fill_lo(pool, stacked, 0, len(stacks.lo))

            @blk.scalar
            def _(act):
                act.activation(gate_sig[:, 0:NB, :], gate_sig[:, 0:NB, :], ACT.Sigmoid)
                act.activation(gate_sig[0:TS, NB, :], gate_sig[0:TS, NB, :], ACT.Sigmoid).then_inc(sig, 1)

            @blk.tensor
            def _(pe):
                pe.wait_ge(sig, 1)
                for j in range(4):
                    last = pe.matmul(c.ps[:, 0, 48 * j:48 * j + 48], c.k("pick")[0:TS, (2 + j) * P:(3 + j) * P],
                                     gate_sig[0:TS, NB, :], start=(j == 0), stop=(j == 3), skip_group_check=True)
                last.then_inc(picked, 1)

            @blk.vector
            def _(dve):
                linked = Linked(dve, link)

                linked(dve.memset(q_blk[:, :, :, :, :, :], 0.0))
                for side in range(2):
                    rows = slice(side * HD, side * HD + HD)
                    for pair in range(2):
                        for h in range(4):
                            dve.tensor_copy(q_blk[rows, :, pair, side, h, :],
                                            projT[rows, 4 * pair + h, SEQ:T].rearrange("p (b t) -> p b t", t=DEC_T))
                dve.wait_ge(picked, 1)
                for j in range(4):
                    g = c.ps[:, 0, 48 * j:48 * j + 48].rearrange("p (h a) -> p a h", a=3)
                    for a in range(3):
                        linked(dve.tensor_tensor(hit[:, a, :], g[:, a, :], c.k("chead"), ALU.mult))
                    linked(dve.reduce_sum(gate_s[:, j, :], hit[:, :, :], AX_X))



def program(nc, dram):
    with ExitStack() as ctx:
        c = setup_memory(nc, ctx, dram)
        d = dram
        pair = lambda a, b: [(0, a, HD), (HD, b, HD)]
        a_rope = [pair(A_Q + i * HD, A_Q + (4 + i) * HD) for i in range(4)]
        a_rope += [[(0, A_IQ, P)], [(0, A_IQ + P, P)], [(0, A_K, P)], pair(A_IK, A_IK)]
        a_plain = [[(0, A_V, P)], [(0, A_IW, P)]] + [[(0, A_GB + i * P, P)] for i in range(12)]
        c_rope = [pair(C_Q + p * 512 + h * HD, C_Q + p * 512 + 256 + h * HD) for p in range(2) for h in range(4)]
        c_rope += [[(0, col + i * P, P)] for col in (C_KC, C_KS, C_KW) for i in range(2)]
        c_plain = [[(0, col + i * P, P)] for col in (C_VC, C_VS, C_VW) for i in range(2)]
        c_plain += [[(0, C_G + 48 - P, P)]]

        with ExitStack() as mem:
            sb = lambda n, s, dt=F32: mem.enter_context(nc.sbuf_tensor(n, s, dt))
            projT = sb("a_projT", [P, 22, T])
            stage_in_proj(c, "a_in", lambda sem, tmp: Load(c, sem, tmp), d["ab_w_in"][0], 4, a_rope, a_plain, projT)
            v_rows = sb("a_v_rows", [P, NB + 1, P])
            iw_full = sb("a_iw_rows", [P, NB + 1, P])
            iw = sb("a_iw", [P, NB + 1, 4])
            p_rows = lambda name: d[name][0, 0].rearrange("t g e -> t (g e)")
            s_rows = lambda name: d[name][0].rearrange("b t g e -> (b t) (g e)")
            stage_rows(c, "a_rows", projT, [
                (6, None, [(0, p_rows("a_k_p"), s_rows("a_k_s"))]),
                (7, None, [(0, d["a_ik_p"][0, 0], d["a_ik_s"][0].rearrange("b t e -> (b t) e"))]),
                (8, v_rows, [(0, p_rows("a_v_p"), s_rows("a_v_s"))]),
                (9, iw_full, [])])
            sel = sb("a_sel", [P, NB, SEQ], BF16)
            reuse_semaphores(c)
            a_more = sb("a_more_stacks", [P, 2, SEQ], F32R)
            slots = idle_slots(c) + [a_more[:, e, :] for e in range(2)]
            a_q2, a_k2 = slots[0:8], slots[8:12]
            stacks = Stack()
            for side in range(2):
                for i in range(4):
                    stacks.queries(side, projT[rows_of(side), i, 0:SEQ], a_q2[2 * i + side])
                stacks.keys(side, projT[rows_of(side), 6, 0:SEQ], a_k2[2 * side], a_k2[2 * side + 1])
            kikT = sb("a_kikT", [P, 2, DEC_B, PAST])
            v_old = sb("a_v_old", [P, DEC_B, NPAGE, P])
            stage_prepare(c, projT, iw, sel, iw_full[:, :, 0:4], stacks, kikT, v_old)
            sel_s = sb("a_sel_s", [P, 2, NEW], BF16)
            q_blk = sb("a_q_blk", [P, DEC_B, 2, 4, DEC_T])
            score_s = sb("a_score_s", [P, 2, NEW])
            best_s = sb("a_best_s", [P, 2, 8])
            stage_index_sample(c, projT, iw[0:TS, NB, :], kikT[:, 1:2], score_s, q_blk)

            def take_sample_keys(dve, sem):
                linked = Linked(dve, sem("sample_link"))
                yield from take_best(dve, linked, [score_s[:, j, :] for j in range(2)], [best_s[:, j, :] for j in range(2)], TOPK_S)
                for j in range(2):
                    dve.tensor_scalar(sel_s[:, j, :], score_s[:, j, :], TAKEN, 1.0, ALU.is_equal, ALU.subtract)
                    yield

            stage_attend_prompt(c, "a_att", *prompt_tiles(1, [(
                lambda i, s, qb: a_q2[2 * i + s][:, qb * P:(qb + 1) * P],
                lambda a, s: a_k2[2 * s:2 * s + 2],
                lambda a, s, k: v_rows[:, k, rows_of(s)],
                lambda qb: (0, (qb + 1) * P, sel[:, qb, 0:(qb + 1) * P]) if qb else (0, P, c.causal_bf[:, :]),
                lambda i, s, qb: None, lambda side: "act")]), weave=take_sample_keys)

            q_of = lambda b: q_blk[:, b].rearrange("p s h t -> p (s h t)")

            def a_leaves(j):
                def side(s):
                    place = lambda x: x[rows_of(s), 0:4, SEQ + 16 * j:SEQ + 16 * j + 16].rearrange("p h (u t) -> p u h t", t=DEC_T)
                    cols = lambda o: o[rows_of(s), 0:P].rearrange("p (u s h t) -> p u s h t", u=4, s=2, h=4)[:, :, s]
                    return [(lambda x, u=u: place(x)[:, u], lambda o, u=u: cols(o)[:, u]) for u in range(4)]
                return side(0) + side(1)

            def a_out_rows(w, cols):
                return [(lambda r: r[0:HD, 0:4, :], w[0:256, cols].rearrange("(k p) n -> p k n", p=HD)),
                        (lambda r: r[HD:P, 0:4, :], w[256:512, cols].rearrange("(k p) n -> p k n", p=HD)),
                        (lambda r: r[:, 4:8, :], w[512:1024, cols].rearrange("(k p) n -> p k n", p=P))]

            stage_attend(c, "a_att_s", sample_groups(2, list(range(DEC_B)), [(
                q_of, lambda b: kikT[:, 0, b, :], PAST, lambda b: projT[:, 6, SEQ:T],
                lambda j: (0, NEW, sel_s[:, j, :]),
                lambda b, k, n: v_old[:, b, k, :] if k < NPAGE else v_rows[0:TS, NB, :])],
                None, a_leaves), [(a_out_rows(d["ab_w_out"][0], slice(n * P, (n + 1) * P)), KT) for n in range(2)])

            stage_out_proj(c, "a_out", d["ab_w_out"][0], a_out_rows)
        reuse_semaphores(c)
        channel_mixer(c, 0)
        reuse_semaphores(c)

        with ExitStack() as mem:
            sb = lambda n, s, dt=F32: mem.enter_context(nc.sbuf_tensor(n, s, dt))
            projT = sb("c_projT", [P, 21, T])
            stage_in_proj(c, "c_in", lambda sem, tmp: Norm(c, sem, tmp, 2), d["c_w_in"][0], 8, c_rope, c_plain, projT)
            vs_rows = [sb(f"vs_rows{i}", [P, NB + 1, P]) for i in range(2)]
            vw_rows = [sb(f"vw_rows{i}", [P, NB + 1, P]) for i in range(2)]
            k_cmpT = sb("k_cmpT", [P, (2 * SEQ + 2 * DEC_B * PAST) // CMP_S])
            v_cmp_p = sb("v_cmp_p", [P, 2 * P])
            kc2 = sb("kc2", [P, 2, 4, 32], F32R)
            g_rows = sb("g_rows", [P, NB + 1, P])
            gate_s = sb("gate_s", [P, 4, 3])
            p_rows = lambda name, i: d[name][0, 0].rearrange("t g e -> t (g e)")[:, i * P:(i + 1) * P]
            s_rows = lambda name, i: d[name][0].rearrange("b t g e -> (b t) (g e)")[:, i * P:(i + 1) * P]
            w_new = lambda name, i: d[name][0][:, PAST - DEC_T:PAST].rearrange("b t g e -> b t (g e)")[:, :, i * P:(i + 1) * P]
            table = sb("c_table", [1, DEC_B * NPAGE], I32)
            till_compress = ExitStack()
            ring = till_compress.enter_context(nc.sbuf_tensor("c_page_ring", [P, RING_C, 2 * P], F32))

            def fetch_pages(pool, sem):
                table_in, landed = sem("table_in"), sem("pages_in")
                pool.dma_start(table[:, :], d["page_table"].rearrange("(a b) g -> a (b g)", a=1)).then_inc(table_in, 16)
                pool.wait_ge(table_in, 16)
                for n in range(RING_C):
                    page = page_number(pool, table, n, d["cache_c_cmp_k"])
                    pool.dma_start(ring[:, n, :], d["cache_c_cmp_k"][0][bass.ds(page, 1)]
                                  .rearrange("a p g e -> p (a g e)")).then_inc(landed, 16)
                pool.wait_ge(landed, 16 * RING_C)

            stage_rows(c, "c_rows", projT,
                       [(8 + i, None, [(0, p_rows("c_cmp_k_p", i), s_rows("c_cmp_k_s", i))]) for i in range(2)]
                       + [(10 + i, None, [(0, p_rows("c_slc_k_p", i), s_rows("c_slc_k_s", i))]) for i in range(2)]
                       + [(12 + i, None, [(0, p_rows("c_win_k_p", i), w_new("c_win_k_s", i))]) for i in range(2)]
                       + [(14 + i, None, [(0, p_rows("c_cmp_v_p", i), s_rows("c_cmp_v_s", i))]) for i in range(2)]
                       + [(16 + i, vs_rows[i], [(0, p_rows("c_slc_v_p", i), s_rows("c_slc_v_s", i))]) for i in range(2)]
                       + [(18 + i, vw_rows[i], [(0, p_rows("c_win_v_p", i), w_new("c_win_v_s", i))]) for i in range(2)]
                       + [(20, g_rows, [])], fetch_pages)
            slots = idle_slots(c)

            def section_stacks(a, q2, k2):
                stacks = Stack()
                for side in range(2):
                    for i in range(4):
                        stacks.queries(side, projT[rows_of(side), 4 * a + i, 0:SEQ], q2[2 * i + side])
                    for b, slab in enumerate((10, 12)):
                        at = 4 * b + 2 * side
                        stacks.keys(side, projT[rows_of(side), slab + a, 0:SEQ], k2[at], k2[at + 1])
                return stacks

            q2_first, k2_first = [x[:, 4 + i, 0:SEQ] for i in range(4) for x in (c.x_hi, c.x_lo)], slots[0:8]
            stacks = section_stacks(0, q2_first, k2_first)
            v_cmp_s = projT[:, 14:18, :].rearrange("p k n -> p (k n)")[:, 0:2 * DEC_B * P]
            stage_compress(c, projT, k_cmpT, v_cmp_p, v_cmp_s, stacks, table, ring)
            till_compress.close()
            reuse_semaphores(c)
            gate_sig = g_rows[:, :, P - 48:P]
            q_blk = projT[:, 8, 0:SEQ].rearrange("p (b i s h t) -> p b i s h t", b=DEC_B, i=2, s=2, h=4)
            stage_gates(c, projT, gate_sig, gate_s, q_blk, k_cmpT, kc2)

            def c_out_rows(w, cols):
                v = w[:, cols].rearrange("(a s h p) n -> a s p h n", a=2, s=2, h=4)
                return [((lambda r, a=a, s=s: r[rows_of(s), 4 * a:4 * a + 4, :]), v[a, s]) for a in range(2) for s in range(2)]

            def gate(i, qb):
                g = gate_sig[:, qb, i // 4 * 24:i // 4 * 24 + 24].rearrange("p (s h a) -> p s h a", s=2, h=4)
                return g[:, :, i % 4, :]

            causal = lambda qb: (qb * P, P, c.causal_bf[:, :])
            flat = lambda x: x.rearrange("p k n -> p (k n)")[:, 0:4 * NPAGE * 2 * P].rearrange("p (b g n) -> p b g n", b=4, g=NPAGE)
            vs_old = [flat(projT[:, 4 * half:4 * half + 4, :]) for half in range(2)]
            vw_old = [flat(c.w_raw[:, :, :, :].rearrange("p s k n -> p (s k) n")), None]

            key_slots = [projT[:, slab, o:o + 2 * P] for slab in (9, 18, 19, 20) for o in (0, 2 * P)]

            def fetch_window(sp, half, name, dst, landed):
                for u in range(4):
                    sp.dma_start(dst[:, u], d[name][0, 4 * half + u].rearrange("(g p) h e -> p g (h e)", g=NPAGE)).then_inc(landed, 16)

            def fetch_values(sp, sem, slabs_read):
                landed = sem("values_in")
                fetch_window(sp, 0, "state_c_win_v", vw_old[0], landed)
                for half in range(2):
                    if half:
                        slabs_read()
                    for u in range(4):
                        for g in range(NPAGE):
                            page = page_number(sp, table, (4 * half + u) * NPAGE + g, d["cache_c_slc_v"])
                            sp.dma_start(vs_old[half][:, u, g, :], d["cache_c_slc_v"][0][bass.ds(page, 1)]
                                         .rearrange("a p g e -> p (a g e)")).then_inc(landed, 16)
                for step, dst in zip(key_steps(0), key_slots):
                    fetch_keys(c, sp, table, step, dst).then_inc(landed, 16)
                sp.wait_ge(landed, 16 * (4 + 2 * 4 * NPAGE + len(key_slots)))

            till_samples = ExitStack()
            more = till_samples.enter_context(nc.sbuf_tensor("more_stacks", [P, 14, SEQ], F32R))
            slots += [more[:, e, :] for e in range(14)]
            c_q2, c_k2 = q2_first + slots[8:16], k2_first + slots[16:24]
            c_q = lambda i, s, qb: c_q2[2 * i + s][:, qb * P:(qb + 1) * P]
            c_gate = lambda branch: (lambda i, s, qb: gate(i, qb)[:, s, branch:branch + 1])
            kc = lambda part, a, s: kc2[:, part, 2 * a + s, :]
            short = lambda a, qb: Short(
                [(c_q(4 * a + h, s, qb), kc(0, a, s), kc(1, a, s)) for s in range(2) for h in range(4)],
                c.cmp_bf[:, qb * 32:qb * 32 + 32].rearrange("p (a n) -> p a n", a=1).broadcast_to([P, 8, 32]),
                gate_sig[:, qb, a * 24:a * 24 + 24].rearrange("p (s h b) -> p s h b", s=2, h=4)[:, :, :, 0])
            stage_attend_prompt(c, "c_att", *prompt_tiles(2, [
                (c_q, lambda a, s: c_k2[8 * a + 2 * s:8 * a + 2 * s + 2],
                 lambda a, s, k: vs_rows[a][:, k, rows_of(s)], causal, c_gate(1), lambda side: "act"),
                (c_q, lambda a, s: c_k2[8 * a + 4 + 2 * s:8 * a + 6 + 2 * s],
                 lambda a, s, k: vw_rows[a][:, k, rows_of(s)], causal, c_gate(2), lambda side: ("act", "dve")[side])],
                (short, lambda a, s, i: v_cmp_p[32 * i:32 * i + 32, a * P + s * HD:a * P + (s + 1) * HD])),
                late=section_stacks(1, c_q2[8:16], c_k2[8:16]), fetch=fetch_values)

            till_samples.close()
            vw_old[1] = sb("vw_old", [P, 4, NPAGE, 2 * P])
            more_slots = sb("key_slots", [P, 8, 2 * P])

            def fetch_second(sp, sem):
                landed = sem("second_in")
                slots = key_slots + [more_slots[:, i, :] for i in range(8)]
                for step, dst in zip(key_steps(1), slots):
                    fetch_keys(c, sp, table, step, dst).then_inc(landed, 16)
                fetch_window(sp, 1, "state_c_win_v", vw_old[1], landed)
                sp.wait_ge(landed, 16 * (len(slots) + 4))

            for half in range(2):
                seqs = list(range(4 * half, 4 * half + 4))
                with ExitStack() as tmp:
                    sbt = lambda n, s: tmp.enter_context(nc.sbuf_tensor(f"{n}{half}", s, F32))
                    ksT = sbt("ksT", [P, 2, 4, PAST])
                    kwT = sbt("kwT", [P, 2, 4, PAST])
                    stage_keys(c, f"c_keys{half}", table, half,
                               key_slots + ([more_slots[:, i, :] for i in range(8)] if half else []), ksT, kwT)
                    units = [(b, p) for b in seqs for p in range(2)]
                    q_of = lambda u: q_blk[:, u[0], u[1]].rearrange("p s h t -> p (s h t)")
                    new_bias = lambda j: (PAST, TS, c.new_bf[:, (2 + 2 * half + j) * TS:(3 + 2 * half + j) * TS])
                    g_of = lambda j: gate_s[:, 2 * half + j:2 * half + j + 1, :]

                    def c_leaves(j):
                        out = []
                        for s in range(2):
                            for u in range(4):
                                b, p = units[4 * j + u]
                                out.append((lambda x, s=s, b=b, p=p: x[rows_of(s), 4 * p:4 * p + 4, SEQ + 4 * b:SEQ + 4 * b + 4],
                                            lambda o, s=s, u=u: o[rows_of(s), 32 * u + 16 * s:32 * u + 16 * s + 16]
                                            .rearrange("p (h t) -> p h t", t=DEC_T)))
                        return out

                    old_v = lambda old, new: (lambda u, k, n: old[:, seqs.index(u[0]), k, u[1] * P:(u[1] + 1) * P]
                                              if k < NPAGE else new[u[1]][0:TS, NB, :])
                    cmp_at = lambda u: 2 * SEQ // CMP_S + (u[1] * DEC_B + u[0]) * PAST // CMP_S
                    stage_attend(c, f"c_att_s{half}", sample_groups(2, units, [
                        (q_of, lambda u: k_cmpT[:, cmp_at(u):cmp_at(u) + NCMP_S], NCMP_S, None, None,
                         lambda u, k, n: v_cmp_s[0:NCMP_S, (u[1] * DEC_B + u[0]) * P:(u[1] * DEC_B + u[0] + 1) * P]),
                        (q_of, lambda u: ksT[:, u[1], seqs.index(u[0]), :], PAST, lambda u: projT[:, 10 + u[1], SEQ:T],
                         new_bias, old_v(vs_old[half], vs_rows)),
                        (q_of, lambda u: kwT[:, u[1], seqs.index(u[0]), :], PAST, lambda u: projT[:, 12 + u[1], SEQ:T],
                         new_bias, old_v(vw_old[half], vw_rows))], g_of, c_leaves),
                        [(c_out_rows(d["c_w_out"][0], slice(n * P, (n + 1) * P)), KT) for n in range(2)] if half else None,
                        None if half else fetch_second)

            stage_out_proj(c, "c_out", d["c_w_out"][0], c_out_rows)
        reuse_semaphores(c)
        channel_mixer(c, 1)
        reuse_semaphores(c)
        stage_store(c, lambda sem, tmp: Norm(c, sem, tmp, 3))


def page_number(sp, table, at, cache):
    return sp.value_load(table[0:1, at:at + 1], min_val=0, max_val=cache.shape[1] - 1)


def key_steps(half):
    return [(b, g, paged) for b in range(4 * half, 4 * half + 4) for g in range(NPAGE) for paged in (True, False)]


def fetch_keys(c, sp, table, step, dst):
    d = c.dram
    b, g, paged = step
    if paged:
        page = page_number(sp, table, b * NPAGE + g, d["cache_c_slc_k"])
        return sp.dma_start(dst, d["cache_c_slc_k"][0][bass.ds(page, 1)].rearrange("a p g e -> p (a g e)"))
    return sp.dma_start(dst, d["state_c_win_k"][0, b, g * PAGE:(g + 1) * PAGE].rearrange("p g e -> p (g e)"))


def stage_keys(c, name, table, half, slots, ksT, kwT):
    nc = c.nc
    block, sem = stage(c, name)
    n_ring = len(slots)
    land = [sem(f"land{i}") for i in range(n_ring)]
    turned = sem("turned")
    evac = [sem("evac_dve"), sem("evac_act")]
    steps = key_steps(half)
    with block as blk:
        @blk.sync
        def _(sp):
            for n in range(n_ring, len(steps)):
                sp.wait_ge(turned, n - n_ring + 1)
                fetch_keys(c, sp, table, steps[n], slots[n % n_ring]).then_inc(land[n % n_ring], 16)

        @blk.tensor
        def _(pe):
            for n in range(len(steps)):
                if n >= n_ring:
                    pe.wait_ge(land[n % n_ring], 16 * (n // n_ring))
                if n >= 8:
                    pe.wait_ge(evac[n % 2], (n - 8) // 2 + 1)
                for h in range(2):
                    last = pe.transpose(c.ps[:, n % 8, h * P:(h + 1) * P], slots[n % n_ring][:, h * P:(h + 1) * P], c.k("ident"))
                last.then_inc(turned, 1)

        def move(eng, copy, n):
            b, g, paged = steps[n]
            dst = ksT if paged else kwT
            eng.wait_ge(turned, n + 1)
            copy(dst[:, :, b % 4, g * PAGE:(g + 1) * PAGE],
                 c.ps[:, n % 8, 0:2 * P].rearrange("p (h n) -> p h n", n=P)).then_inc(evac[n % 2], 1)

        @blk.vector
        def _(dve):
            for n in range(0, len(steps), 2):
                move(dve, dve.tensor_copy, n)

        @blk.scalar
        def _(act):
            for n in range(1, len(steps), 2):
                move(act, lambda out, in_: act.activation(out, in_, ACT.Copy), n)


def channel_mixer(c, layer):
    with ExitStack() as mem:
        h_hi = mem.enter_context(c.nc.sbuf_tensor(f"h_hi{layer}", [P, FT, T], F32R))
        h_lo = mem.enter_context(c.nc.sbuf_tensor(f"h_lo{layer}", [P, FT, T], F32R))
        stage_ffn_up(c, layer, lambda sem, tmp: Norm(c, sem, tmp, layer), h_hi, h_lo)
        stage_ffn_down(c, layer, h_hi, h_lo)


INPUTS = ["x_prompt", "x_sample", "cache_a_k", "cache_a_v", "cache_a_ik", "state_b_conv", "cache_c_cmp_k",
          "cache_c_cmp_v", "cache_c_slc_k", "cache_c_slc_v", "state_c_win_k", "state_c_win_v", "page_table",
          "ab_w_in", "ab_conv_w", "ab_w_out", "c_w_in", "c_cmp_pe_k", "c_cmp_w1_k", "c_cmp_w2_k", "c_cmp_pe_v",
          "c_cmp_w1_v", "c_cmp_w2_v", "c_w_out", "ffn_w_gate", "ffn_w_up", "ffn_w_down", "ln1_g", "ln1_b",
          "ln2_g", "ln2_b"]
_A = (1, 1, SEQ, 2, HD)
_C = (1, 1, SEQ, 4, HD)
_AS = (1, DEC_B, DEC_T, 2, HD)
_CS = (1, DEC_B, DEC_T, 4, HD)
OUTPUTS = {"y_prompt": (1, SEQ, D), "y_sample": (DEC_B, DEC_T, D),
           "a_k_p": _A, "a_v_p": _A, "a_ik_p": (1, 1, SEQ, HD), "b_conv_p": (1, 1, 2, D // 2),
           "c_cmp_k_p": _C, "c_cmp_v_p": _C, "c_slc_k_p": _C, "c_slc_v_p": _C, "c_win_k_p": _C, "c_win_v_p": _C,
           "a_k_s": _AS, "a_v_s": _AS, "a_ik_s": (1, DEC_B, DEC_T, HD), "b_conv_s": (1, DEC_B, 2, D // 2),
           "c_cmp_k_s": _CS, "c_cmp_v_s": _CS, "c_slc_k_s": _CS, "c_slc_v_s": _CS,
           "c_win_k_s": (1, DEC_B, PAST, 4, HD), "c_win_v_s": (1, DEC_B, PAST, 4, HD)}


def kernel(**inputs):
    import concourse.bacc as bacc
    from concourse.bass_utils import run_bass_kernel_spmd as run

    nc = bacc.Bacc("TRN2", target_bir_lowering=False, num_devices=1)
    arrays, dram = {}, {}
    for name in INPUTS:
        a = np.ascontiguousarray(inputs[name])
        arrays[f"in_{name}"] = a
        dram[name] = nc.dram_tensor(f"in_{name}", a.shape, mybir.dt.from_np(a.dtype), kind="ExternalInput").ap()
    arrays["in_const"] = CONST
    dram["const"] = nc.dram_tensor("in_const", CONST.shape, F32, kind="ExternalInput").ap()
    for name, shape in OUTPUTS.items():
        dram[name] = nc.dram_tensor(f"out_{name}", shape, F32, kind="ExternalOutput").ap()
    program(nc, dram)
    r = run(nc, [arrays], core_ids=[0])
    return tuple(r.results[0][f"out_{name}"] for name in OUTPUTS)
```
